# Optimizing a Trainium2 kernel written in Bass

```python
import numpy as np
import jax
import jax.numpy as jnp
from jax import lax

D_MODEL = 1024
BATCH = 1
SEQ = 1024
DEPTH = 1
DEC_BATCH = 8
DEC_SEQ = 4
PAST_LEN = 256
PAGE_SIZE = 128

N_HEADS_A = D_MODEL // 256
HEAD_DIM_A = 128
WIDTH_A = N_HEADS_A * HEAD_DIM_A
CONV_W = 4
DELTA_CHUNK = 64
WINDOWS = (128, 512, 2048)
DILATIONS = (1, 4, 16)
N_GROUPS = 3
HEADS_PER_GROUP = D_MODEL // 256
HEAD_DIM_B = 64
N_HEADS_B = N_GROUPS * HEADS_PER_GROUP
WIDTH_B = N_HEADS_B * HEAD_DIM_B
WIDTH_B_OUT = HEADS_PER_GROUP * HEAD_DIM_B
Q_BLOCK = 128
D_FF = 4 * D_MODEL
IN_SPLITS = (3 * WIDTH_A, WIDTH_A, N_HEADS_A, N_HEADS_A, WIDTH_B, WIDTH_B, WIDTH_B, D_MODEL, D_MODEL)
N_IN = 3 * WIDTH_A + WIDTH_A + 2 * N_HEADS_A + 3 * WIDTH_B + 2 * D_MODEL
EPS = 1e-6

kernel_name = 'dilated_delta_hybrid_step'

def rms_norm(x, g):
    x32 = x.astype(jnp.float32)
    y = x32 * lax.rsqrt(jnp.mean(x32 * x32, axis=-1, keepdims=True) + EPS)
    return (y * g.astype(jnp.float32)).astype(x.dtype)

def l2_normalize(x):
    return x * lax.rsqrt(jnp.sum(x * x, axis=-1, keepdims=True) + EPS)

def alibi_slopes():
    h = jnp.arange(1, N_HEADS_B + 1, dtype=jnp.float32)
    return jnp.exp2(-8.0 * h / N_HEADS_B).reshape(N_GROUPS, HEADS_PER_GROUP)

def gated_delta_rule(q, k, v, log_a, beta, s0):
    B, T, H, DK = q.shape
    DV = v.shape[-1]
    C = DELTA_CHUNK if T % DELTA_CHUNK == 0 else T
    N = T // C
    f32 = jnp.float32

    def blocks(a):
        a = a.astype(f32).reshape((B, N, C, H) + a.shape[3:])
        return jnp.moveaxis(a, (1, 3), (0, 2))

    q, k, v, g, bt = blocks(q), blocks(k), blocks(v), blocks(log_a), blocks(beta)
    G = jnp.cumsum(g, axis=-1)
    causal = jnp.tril(jnp.ones((C, C), dtype=bool))
    strict = jnp.tril(jnp.ones((C, C), dtype=bool), -1)
    decay = jnp.exp(jnp.where(causal, G[..., :, None] - G[..., None, :], -jnp.inf))
    kb = k * bt[..., None]
    a_mat = jnp.where(strict, jnp.einsum('nbhid,nbhjd->nbhij', kb, k) * decay, 0.0)
    eye = jnp.eye(C, dtype=f32)
    rhs = jnp.concatenate([kb * jnp.exp(G)[..., None], v * bt[..., None]], axis=-1)
    wu = lax.linalg.triangular_solve(eye + a_mat, rhs, left_side=True, lower=True)
    w, u = wu[..., :DK], wu[..., DK:]
    qk = jnp.einsum('nbhid,nbhjd->nbhij', q, k) * decay
    qg = q * jnp.exp(G)[..., None]
    kd = k * jnp.exp(G[..., -1:] - G)[..., None]
    g_last = jnp.exp(G[..., -1])

    def step(S, xs):
        w_c, u_c, qk_c, qg_c, kd_c, gl_c = xs
        v_new = u_c - jnp.einsum('bhck,bhkv->bhcv', w_c, S)
        o_c = jnp.einsum('bhck,bhkv->bhcv', qg_c, S) + jnp.einsum('bhij,bhjv->bhiv', qk_c, v_new)
        S = S * gl_c[..., None, None] + jnp.einsum('bhck,bhcv->bhkv', kd_c, v_new)
        return S, o_c

    S, o = lax.scan(step, s0.astype(f32), (w, u, qk, qg, kd, g_last))
    o = jnp.moveaxis(o, (0, 2), (1, 3)).reshape(B, T, H, DV)
    return o, S

def dilated_group_attention(q, kv_src, p0, window, dilation, slopes):
    B, T, H, D = q.shape
    qb = Q_BLOCK if T % Q_BLOCK == 0 else T
    n_off = window // dilation + 1
    offs = jnp.arange(n_off) * dilation
    rows = jnp.arange(qb)
    local_idx = window + rows[:, None] - offs[None, :]
    bias = -slopes[:, None] * offs[None, :].astype(jnp.float32)
    scale = D ** -0.5

    def one_block(blk):
        start = blk * qb
        q_blk = lax.dynamic_slice_in_dim(q, start, qb, axis=1).astype(jnp.float32)
        win = lax.dynamic_slice_in_dim(kv_src, start, qb + window, axis=1)
        kv = jnp.take(win, local_idx, axis=1).astype(jnp.float32)
        s = jnp.einsum('bqhd,bqkhd->bhqk', q_blk, kv[:, :, :, 0]) * scale + bias[None, :, None, :]
        valid = (p0 + start + rows[:, None] - offs[None, :]) >= 0
        s = jnp.where(valid, s, -jnp.inf)
        lse = jax.nn.logsumexp(s, axis=-1)
        p = jnp.exp(s - lse[..., None])
        o = jnp.einsum('bhqk,bqkhd->bqhd', p, kv[:, :, :, 1])
        return o, jnp.swapaxes(lse, 1, 2)

    o, lse = lax.map(one_block, jnp.arange(T // qb))
    o = jnp.moveaxis(o, 0, 1).reshape(B, T, H, D)
    lse = jnp.moveaxis(lse, 0, 1).reshape(B, T, H)
    return o, lse

def hybrid_layer(x, p0, win_past, conv_buf, s0, norm1, w_in, conv_w, a_log, dt_bias, gnorm_a,
                 w_br_a, w_br_b, w_out, norm2, w_up, w_down):
    B, T, _ = x.shape
    f32 = jnp.float32
    h = rms_norm(x, norm1)
    proj = jnp.einsum('btd,de->bte', h, w_in)
    split_at = [int(i) for i in np.cumsum(IN_SPLITS)[:-1]]
    qkv_a, z, a_raw, b_raw, q_b, k_b, v_b, gate_a, gate_b = jnp.split(proj, split_at, axis=-1)

    src = jnp.concatenate([conv_buf.astype(x.dtype), qkv_a], axis=1)
    conv = sum(src[:, j:j + T] * conv_w[j] for j in range(CONV_W))
    new_conv = src[:, T:]
    qa, ka, va = jnp.split(jax.nn.silu(conv), 3, axis=-1)
    head_shape = (B, T, N_HEADS_A, HEAD_DIM_A)
    qa = l2_normalize(qa.reshape(head_shape).astype(f32)) * HEAD_DIM_A ** -0.5
    ka = l2_normalize(ka.reshape(head_shape).astype(f32))
    va = va.reshape(head_shape)
    log_a = -jnp.exp(a_log.astype(f32)) * jax.nn.softplus(a_raw.astype(f32) + dt_bias.astype(f32))
    beta = jax.nn.sigmoid(b_raw.astype(f32))
    o_a, s_new = gated_delta_rule(qa, ka, va, log_a, beta, s0)
    o_a = rms_norm(o_a, gnorm_a) * jax.nn.silu(z.reshape(head_shape).astype(f32))
    o_a = o_a.reshape(B, T, WIDTH_A).astype(x.dtype)

    slopes = alibi_slopes()
    grp_shape = (B, T, N_GROUPS, HEADS_PER_GROUP, HEAD_DIM_B)
    qs, ks, vs = q_b.reshape(grp_shape), k_b.reshape(grp_shape), v_b.reshape(grp_shape)
    outs, lses, new_win = [], [], []
    for g in range(N_GROUPS):
        window = WINDOWS[g]
        past = win_past[g].astype(x.dtype)
        new = jnp.stack([ks[:, :, g], vs[:, :, g]], axis=2)
        pad = jnp.zeros((B, window - past.shape[1]) + new.shape[2:], x.dtype)
        kv_src = jnp.concatenate([pad, past, new], axis=1)
        o_g, lse_g = dilated_group_attention(qs[:, :, g], kv_src, p0, window, DILATIONS[g], slopes[g])
        outs.append(o_g)
        lses.append(lse_g)
        keep = min(window, p0 + T)
        new_win.append(kv_src[:, -keep:])
    wts = jax.nn.softmax(jnp.stack(lses), axis=0)
    o_b = jnp.sum(wts[..., None] * jnp.stack(outs), axis=0)
    o_b = o_b.reshape(B, T, WIDTH_B_OUT).astype(x.dtype)

    merged = jax.nn.sigmoid(gate_a) * (o_a @ w_br_a) + jax.nn.sigmoid(gate_b) * (o_b @ w_br_b)
    x = x + merged @ w_out
    h2 = rms_norm(x, norm2)
    x = x + jnp.square(jax.nn.relu(h2 @ w_up)) @ w_down
    return x, new_win, s_new.astype(x.dtype), new_conv

def run_trunk(x, p0, win_caches, delta_cache, conv_cache, layer_params, final_norm):
    win_out = [[] for _ in range(N_GROUPS)]
    delta_out, conv_out = [], []
    for l in range(DEPTH):
        past = [c[l] for c in win_caches]
        x, wins, s_new, c_new = hybrid_layer(x, p0, past, conv_cache[l], delta_cache[l],
                                             *[p[l] for p in layer_params])
        for g in range(N_GROUPS):
            win_out[g].append(wins[g])
        delta_out.append(s_new)
        conv_out.append(c_new)
    return (rms_norm(x, final_norm), [jnp.stack(w) for w in win_out],
            jnp.stack(delta_out), jnp.stack(conv_out))

def setup_inputs(seed: int = 0) -> dict:
    key = jax.random.key(seed)
    ks = jax.random.split(key, 20)
    f32 = jnp.float32

    def nrm(k, shape, s=1.0):
        return jax.random.normal(k, shape, f32) * s

    wl = [min(w, PAST_LEN) for w in WINDOWS]
    dt = jnp.exp(jax.random.uniform(ks[11], (DEPTH, N_HEADS_A), f32,
                                    float(np.log(1e-3)), float(np.log(1e-1))))
    return {
        'x_prompt': nrm(ks[0], (BATCH, SEQ, D_MODEL)),
        'x_sample': nrm(ks[1], (DEC_BATCH, DEC_SEQ, D_MODEL)),
        'cache_win0': nrm(ks[2], (DEPTH, DEC_BATCH, wl[0], 2, HEADS_PER_GROUP, HEAD_DIM_B)),
        'cache_win1': nrm(ks[3], (DEPTH, DEC_BATCH, wl[1], 2, HEADS_PER_GROUP, HEAD_DIM_B)),
        'cache_win2': nrm(ks[4], (DEPTH, DEC_BATCH, wl[2], 2, HEADS_PER_GROUP, HEAD_DIM_B)),
        'state_delta': nrm(ks[5], (DEPTH, DEC_BATCH, N_HEADS_A, HEAD_DIM_A, HEAD_DIM_A), 0.3),
        'state_conv': nrm(ks[6], (DEPTH, DEC_BATCH, CONV_W - 1, 3 * WIDTH_A)),
        'norm1': 1.0 + nrm(ks[7], (DEPTH, D_MODEL), 0.02),
        'w_in': nrm(ks[8], (DEPTH, D_MODEL, N_IN), D_MODEL ** -0.5),
        'conv_w': nrm(ks[9], (DEPTH, CONV_W, 3 * WIDTH_A), CONV_W ** -0.5),
        'a_log': jnp.log(jax.random.uniform(ks[10], (DEPTH, N_HEADS_A), f32, 1.0, 16.0)),
        'dt_bias': dt + jnp.log(-jnp.expm1(-dt)),
        'gnorm_a': 1.0 + nrm(ks[12], (DEPTH, HEAD_DIM_A), 0.02),
        'w_br_a': nrm(ks[13], (DEPTH, WIDTH_A, D_MODEL), WIDTH_A ** -0.5),
        'w_br_b': nrm(ks[14], (DEPTH, WIDTH_B_OUT, D_MODEL), WIDTH_B_OUT ** -0.5),
        'w_out': nrm(ks[15], (DEPTH, D_MODEL, D_MODEL), D_MODEL ** -0.5),
        'norm2': 1.0 + nrm(ks[16], (DEPTH, D_MODEL), 0.02),
        'w_up': nrm(ks[17], (DEPTH, D_MODEL, D_FF), D_MODEL ** -0.5),
        'w_down': nrm(ks[18], (DEPTH, D_FF, D_MODEL), D_FF ** -0.5),
        'final_norm': 1.0 + nrm(ks[19], (D_MODEL,), 0.02),
    }

def reference(x_prompt, x_sample, cache_win0, cache_win1, cache_win2, state_delta, state_conv,
              norm1, w_in, conv_w, a_log, dt_bias, gnorm_a, w_br_a, w_br_b, w_out, norm2,
              w_up, w_down, final_norm):
    layer_params = (norm1, w_in, conv_w, a_log, dt_bias, gnorm_a, w_br_a, w_br_b, w_out,
                    norm2, w_up, w_down)
    dt = x_prompt.dtype
    bp = x_prompt.shape[0]
    zero_win = jnp.zeros((DEPTH, bp, 0, 2, HEADS_PER_GROUP, HEAD_DIM_B), dt)
    zero_delta = jnp.zeros((DEPTH, bp, N_HEADS_A, HEAD_DIM_A, HEAD_DIM_A), dt)
    zero_conv = jnp.zeros((DEPTH, bp, CONV_W - 1, 3 * WIDTH_A), dt)
    y_prompt, wins_p, delta_p, conv_p = run_trunk(
        x_prompt, 0, (zero_win, zero_win, zero_win), zero_delta, zero_conv, layer_params, final_norm)
    y_sample, wins_s, delta_s, conv_s = run_trunk(
        x_sample, PAST_LEN, (cache_win0, cache_win1, cache_win2), state_delta, state_conv,
        layer_params, final_norm)
    return (y_prompt, y_sample, wins_p[0], wins_p[1], wins_p[2], delta_p, conv_p,
            wins_s[0], wins_s[1], wins_s[2], delta_s, conv_s)


_drawn_inputs = setup_inputs


def setup_inputs(seed=0):
    import zlib

    import numpy as np

    out = dict(_drawn_inputs(seed))
    spreads = {}
    factors = {'gnorm_a': 8.0, 'norm2': 3.264, 'final_norm': 2.848}
    for name, (base, spread) in spreads.items():
        noise = np.random.default_rng([zlib.crc32(name.encode()), seed]).standard_normal(out[name].shape)
        drawn = base * np.exp(spread * noise) if base else spread * noise
        out[name] = jnp.asarray(drawn.astype(out[name].dtype))
    for name, factor in factors.items():
        out[name] = (out[name] * factor).astype(out[name].dtype)
    return out
```

```python
from contextlib import ExitStack

import numpy as np

import concourse.bass as bass
from concourse import mybir

F32, F32R = mybir.dt.float32, mybir.dt.float32r
ALU, ACT, AX = mybir.AluOpType, mybir.ActivationFunctionType, mybir.AxisListType

P = 128
D, DFF = 1024, 4096
TP, NSEQ, TSEQ = 1024, 8, 4
TS = NSEQ * TSEQ
T = TP + TS
NG, TN = 3, (TP + NSEQ * TSEQ) // 3
KD = D // P
NH, HD = 4, 128
WA = NH * HD
NCH = TP // P
NT9 = NCH + 1
PAST = 256
WIN, DIL = (128, 512, 2048), (1, 4, 16)
NHB, HB = 4, 64
WB = 3 * NHB * HB
C_AB = 4 * WA
C_QKV = C_AB + 2 * NH
C_GA = C_QKV + 3 * WB
C_GB = C_GA + D
EPS = 1e-6
BLK = 16
NBLK = P // BLK
BIG = 1e30


def slopes():
    return np.exp2(-8.0 * np.arange(1, 3 * NHB + 1, dtype=np.float32) / (3 * NHB)).reshape(3, NHB)


def constants():
    c = {"ident": np.eye(P, dtype=np.float32)}
    j, i = np.arange(P)[:, None], np.arange(P)[None, :]
    levels = [((i // (2 * s) == j // (2 * s)) & (i // s > j // s)) for s in (16, 32, 64)]
    c["masks"] = np.stack([i >= j, i > j] + levels, 1).astype(np.float32)
    js, is_ = np.arange(TS)[:, None], np.arange(TS)[None, :]
    same = js // TSEQ == is_ // TSEQ
    c["masks_s"] = np.stack([same & (is_ >= js), same & (is_ > js)], 1).astype(np.float32)
    own = (np.arange(NSEQ)[:, None] == np.arange(TS)[None, :] // TSEQ).astype(np.float32)
    c["own_row"] = np.broadcast_to(own, (P, NSEQ, TS)).copy()
    c["own_col"] = own.T.copy()
    c["q_scale"] = -HB ** -0.5 * (np.arange(P)[:, None] // HB == np.arange(2)[None, :]).astype(np.float32)
    own9 = np.concatenate([own, np.ones((1, TS), np.float32)])
    c["own_q"] = np.broadcast_to(own9[None, :, None, :], (P, NSEQ + 1, 2, TS)).copy()
    reset = np.ones(T, np.float32)
    reset[0:TP:P] = 0
    reset[TP::TSEQ] = 0
    c["reset"] = np.broadcast_to(reset, (8, T)).copy()
    c["unit"] = np.broadcast_to(np.eye(BLK, dtype=np.float32).reshape(1, BLK * BLK), (NCH * NBLK, BLK * BLK)).copy()
    q, k = np.arange(P)[:, None], np.arange(2 * P)[None, :] - P
    sl = slopes()
    bias = np.zeros((3, 2, P, 2, 2 * P), np.float32)
    for g in range(3):
        off = q - k
        ok = (off >= 0) & (off <= WIN[g] // DIL[g])
        dist = off * DIL[g]
        if g == 2:
            ok = (off >= 0) & (off % 2 == 0) & (k >= 0)
            dist = off * 8
        for h in range(NHB):
            bias[g, h // 2, :, h % 2] = np.where(ok, sl[g, h] * dist, BIG)
    c["bias_p"] = bias
    bs = np.zeros((3, 2, 2, TS, PAST + TS), np.float32)
    tok = np.arange(TS)[:, None]
    for g in range(3):
        ncache = min(WIN[g], PAST)
        pos = PAST - ncache + np.arange(ncache)[None, :]
        dist = PAST + tok % TSEQ - pos
        ok = (dist % DIL[g] == 0) & (dist <= WIN[g])
        dn = tok % TSEQ - np.arange(TS)[None, :] % TSEQ
        okn = (tok // TSEQ == np.arange(TS)[None, :] // TSEQ) & (dn >= 0) & (dn % DIL[g] == 0)
        for h in range(NHB):
            bs[g, h // 2, h % 2, :, 0:ncache] = np.where(ok, sl[g, h] * dist, BIG)
            bs[g, h // 2, h % 2, :, ncache:ncache + TS] = np.where(okn, sl[g, h] * dn, BIG)
    c["bias_s"] = bs.reshape(3, 2, 2 * TS, PAST + TS)
    return c


class Chain:

    def __init__(self, sem, lengths, name):
        self.sem, self.lengths, self.name, self.base, self.n = sem, lengths, name, 0, 0

    def link(self, eng, ins):
        self.n += 1
        ins.then_inc(self.sem, 1)
        eng.wait_ge(self.sem, self.base + self.n)

    def rounds(self, eng, name, times, body):
        key = f"{self.name} {name}"
        base, n = self.base, self.n
        with eng.Fori(0, times) as i:
            self.base, self.n = base + n + i * self.lengths.get(key, 0), 0
            body(i)
            per = self.n
        self.lengths[key] = per
        self.base, self.n = base, n + times * per


INPUTS = ["x_prompt", "x_sample", "cache_win0", "cache_win1", "cache_win2", "state_delta", "state_conv",
          "norm1", "w_in", "conv_w", "a_log", "dt_bias", "gnorm_a", "w_br_a", "w_br_b", "w_out", "norm2",
          "w_up", "w_down", "final_norm"]
OUTS = [("y_prompt", (1, TP, D)), ("y_sample", (NSEQ, TSEQ, D)),
        ("win0_p", (1, 1, 128, 2, NHB, HB)), ("win1_p", (1, 1, 512, 2, NHB, HB)), ("win2_p", (1, 1, TP, 2, NHB, HB)),
        ("delta_p", (1, 1, NH, HD, HD)), ("conv_p", (1, 1, 3, 3 * WA)),
        ("win0_s", (1, NSEQ, 128, 2, NHB, HB)), ("win1_s", (1, NSEQ, PAST + TSEQ, 2, NHB, HB)),
        ("win2_s", (1, NSEQ, PAST + TSEQ, 2, NHB, HB)),
        ("delta_s", (1, NSEQ, NH, HD, HD)), ("conv_s", (1, NSEQ, 3, 3 * WA))]

N_AB, N_HEAD, N_ATT, N_GA, N_BR, N_OUT, N_MLP = 0, 1, 33, 49, 51, 59, 67


def build(nc, a, lengths):
    ctx = ExitStack()
    with ctx:
        def sb(name, shape, dt=F32, scope=None):
            return (scope or ctx).enter_context(nc.sbuf_tensor(name, shape, dt))

        S = {}

        def sem(name):
            if name not in S:
                S[name] = ctx.enter_context(nc.semaphore(name))
            return S[name]

        def dram(name, shape):
            return nc.dram_tensor(name, shape, F32).ap()

        rows_d = dram("rows_scratch", [16, T])
        diag_d = dram("diag_scratch", [NCH, NBLK, BLK, BLK])
        tinv_d = dram("tinv_scratch", [NCH, NBLK, BLK, BLK])
        oa_d = dram("oa_scratch", [NH, P, T])
        ga_d, gb_d = dram("ga_scratch", [KD, P, T]), dram("gb_scratch", [KD, P, T])
        qkv_d = dram("qkv_scratch", [6, 3, P, T])
        att_d = dram("att_scratch", [3, T, NHB, HB + 2])

        hH, hL = sb("hH", [P, KD, T], F32R), sb("hL", [P, KD, T], F32R)
        Wraw = sb("Wraw", [P, 2, KD, P])
        WH, WL = sb("WH", [P, 2, KD, P], F32R), sb("WL", [P, 2, KD, P], F32R)
        ident, ones = sb("ident_sb", [P, P]), sb("ones", [P, 1])
        vec, vec_rows = sb("vec", [P, 25]), sb("vec_rows", [25, P])
        fill = sb("fill", [P, 2, TN])
        ssx, rx = sb("ssx", [P, 16]), sb("rx", [P, 16])
        NORM1, NORM2, FNORM, GNORM = 0, 8, 16, 24

        dense = [ctx.enter_context(nc.psum_tensor(f"dense{t}", [P, 512], F32)) for t in range(NG)]
        work = [ctx.enter_context(nc.psum_tensor(f"work{t}", [P, 512], F32)) for t in range(5)]

        w_in = a["w_in"][0].rearrange("(k p) n -> p k n", p=P)
        tiles9 = [(TN * g + P * k, P if k < 2 else TN - 2 * P) for g in range(NG) for k in range(3)]
        chV, chA, chG = (Chain(sem(n), lengths, n) for n in ("own_vector", "own_scalar", "own_pool"))
        V, A, G, PE = nc.vector, nc.scalar, nc.gpsimd, nc.tensor

        def load_w(sp, n0, n, parts):
            s = n0 % 2
            sp.wait_ge(sem("w_split"), n + 1)
            for dst, src in parts(Wraw[:, s]):
                sp.dma_start(dst, src).then_inc(sem(f"w_loaded{s}"), 16)

        def load_cols(sp, n0, n, w, col):
            load_w(sp, n0, n, lambda raw: [(raw, w[:, :, bass.ds(col, P)])])

        def split_hi(act, n0, n, loads, k=KD):
            s = n0 % 2
            act.wait_ge(sem(f"w_loaded{s}"), 16 * loads)
            act.wait_ge(sem("d_done"), 3 * n)
            A.activation(WH[:, s, 0:k], Wraw[:, s, 0:k], ACT.Copy).then_inc(sem("w_hi"), 1)

        def split_lo(pool, n0, n, k=KD):
            s = n0 % 2
            pool.wait_ge(sem("w_hi"), n + 1)
            G.tensor_tensor(WL[:, s, 0:k], Wraw[:, s, 0:k], WH[:, s, 0:k].bitcast(F32),
                            ALU.subtract).then_inc(sem("w_split"), 1)

        def product(n0, t, out, xH, xL, k0=0, nk=KD):
            s = n0 % 2
            cols = slice(TN * t, TN * t + TN)
            for k in range(nk):
                for i, (w, x) in enumerate(((WH, xH), (WH, xL), (WL, xH))):
                    ins = PE.matmul(out[:, 0:TN], w[:, s, k0 + k, :], x[:, k, cols],
                                    start=(k == 0 and i == 0), stop=(k == nk - 1 and i == 2))
            return ins

        def job(pe, n0, n, t, xH=None, xL=None):
            if t == 0:
                pe.wait_ge(sem("w_split"), n + 3)
            pe.wait_ge(sem(f"d_free{t}"), n)
            product(n0, t, dense[t], hH if xH is None else xH, hL if xL is None else xL).then_inc(sem("d_done"), 1)

        def apart(eng):
            eng.sem_inc(sem("apart"), 1)

        def part(pe, n0, n, p):
            t, k, s = p // KD, p % KD, n0 % 2
            if p == 0:
                pe.wait_ge(sem("w_split"), n + 3)
            if k == 0:
                pe.wait_ge(sem(f"d_free{t}"), n)
            for i, (w, x) in enumerate(((WH, hH), (WH, hL), (WL, hH))):
                ins = PE.matmul(dense[t][:, 0:TN], w[:, s, k, :], x[:, k, TN * t:TN * t + TN],
                                start=(k == 0 and i == 0), stop=(k == KD - 1 and i == 2))
            if k == KD - 1:
                ins.then_inc(sem("d_done"), 1)

        def fill_out(act, n0, n, t, half, before, func, dst):
            done(act, n, t)
            act.wait_ge(sem(f"stored{half}"), 16 * before + 1)
            A.activation(fill[:, half], dense[t][:, 0:TN], func).then_inc(sem(f"d_free{t}"), 1)
            act.wait_ge(sem(f"d_free{t}"), n + 1)
            act.dma_start(dst[:, TN * t:TN * t + TN], fill[:, half]).then_inc(sem(f"stored{half}"), 16)

        def fill_pair(act, n0, n, it, c, before):
            x, t = c // NG, c % NG
            dst = (qkv_d[bass.ds(it, 1), x] if x < 3 else ga_d[bass.ds(it, 1)]).rearrange("o p t -> (o p) t")
            fill_out(act, n0 + x, n + x, t, c % 2, before + c // 2, ACT.Copy if x < 3 else ACT.Sigmoid, dst)

        def pair_cols(it, x):
            return C_QKV + x * WB + it * P if x < 3 else C_GA + it * P

        def done(eng, n, t):
            eng.wait_ge(sem("d_done"), 3 * n + t + 4)

        sc_h = ExitStack()
        xt, xs = sb("xt", [P, 2, D], F32, sc_h), sb("xs", [P, 2, D], F32, sc_h)
        junk = sb("junk", [P, D], F32, sc_h)
        sc_h.close()

        def x_rows(sp, m, dst, s):
            c, n = tiles9[m]
            if c + n <= TP:
                sp.dma_start(dst[0:n], a["x_prompt"][0, c:c + n, :]).then_inc(s, 16)
                return 1
            sp.dma_start(dst[0:TP - c], a["x_prompt"][0, c:TP, :]).then_inc(s, 16)
            sp.dma_start(dst[TP - c:n], a["x_sample"].rearrange("b t d -> (b t) d")).then_inc(s, 16)
            return 2

        def start_sync(sp):
            for r, name in ((NORM1, "norm1"), (NORM2, "norm2")):
                sp.dma_start(vec_rows[r:r + KD, :], a[name][0].rearrange("(k p) -> k p", p=P)).then_inc(sem("consts"), 16)
            sp.dma_start(vec_rows[FNORM:FNORM + KD, :], a["final_norm"].rearrange("(k p) -> k p", p=P)).then_inc(sem("consts"), 16)
            sp.dma_start(vec_rows[GNORM:GNORM + 1, :], a["gnorm_a"]).then_inc(sem("consts"), 16)
            sp.dma_start(ident[:], a["ident"]).then_inc(sem("consts"), 16)
            for m in range(9):
                if m >= 2:
                    sp.wait_ge(sem("x_scaled"), m - 1)
                x_rows(sp, m, xt[:, m % 2], sem(f"x_in{m % 2}"))
                if m == 1:
                    load_cols(sp, N_AB, N_AB, w_in, C_AB)

        FROM_ONE = ("at_made", "att_s_stored", "att_stored", "back", "gate_stored", "kv_stored", "kvs_stored", "min_s", "mins",
                    "o_turned", "oa_part", "oa_stored", "pv_s", "q_own", "s0_done", "s0_new", "s0_stored", "s_smp", "sq_added",
                    "state_stored", "stored0", "stored1", "tails_stored", "tails_turned", "tinv_out", "v_done", "y_done")

        def start_pool(pool):
            for name in FROM_ONE:
                pool.sem_inc(sem(name), 1)
            pool.sem_inc(sem("w_split"), 2)
            G.memset(ones[:], 1.0).then_inc(sem("zeroed"), 1)
            split_lo(pool, N_AB, N_AB)

        def start_scalar(act):
            def square(m):
                n = tiles9[m][1]
                act.wait_ge(sem(f"x_in{m % 2}"), 16 * (m // 2 + 1 + (m == 8)))
                A.activation(junk[0:n, :], xt[0:n, m % 2], ACT.Square, accum_out=ssx[0:n, m:m + 1]).then_inc(sem("squares"), 1)
                act.wait_ge(sem("squares"), m + 1)
            act.wait_ge(sem("vec_T"), 1)
            A.activation(vec[:], work[4][:, 0:25], ACT.Copy).then_inc(sem("vec_set"), 1)
            act.wait_ge(sem("vec_set"), 1)
            square(0)
            for m in range(9):
                c, n = tiles9[m]
                act.wait_ge(sem("mean"), m + 1)
                A.activation(rx[0:n, m:m + 1], rx[0:n, m:m + 1], ACT.Sqrt).then_inc(sem("root"), 1)
                if m < 8:
                    square(m + 1)
                for half in range(2):
                    act.wait_ge(sem("turned"), 2 * m + half + 1)
                    for k in range(4):
                        kk = 4 * half + k
                        ins = A.activation(hH[:, kk, c:c + n], work[2 * (m % 2) + half][:, k * P:k * P + n], ACT.Copy,
                                           scale=vec[:, NORM1 + kk:NORM1 + kk + 1])
                    ins.then_inc(sem("h_hi"), 1)
                if m == 0:
                    split_hi(act, N_AB, N_AB, 1)

        def start_vector(dve):
            def mean(m):
                n = tiles9[m][1]
                dve.wait_ge(sem("squares"), m + 1)
                V.tensor_scalar(rx[0:n, m:m + 1], ssx[0:n, m:m + 1], 1.0 / D, EPS, ALU.mult, ALU.add).then_inc(sem("mean"), 1)
            mean(0)
            for m in range(9):
                c, n = tiles9[m]
                dve.wait_ge(sem("root"), m + 1)
                chV.link(dve, V.reciprocal(rx[0:n, m:m + 1], rx[0:n, m:m + 1]))
                if m >= 2:
                    dve.wait_ge(sem("turned"), 2 * (m - 1))
                V.tensor_scalar(xs[0:n, m % 2], xt[0:n, m % 2], rx[0:n, m:m + 1], None, ALU.mult).then_inc(sem("x_scaled"), 1)
                if m < 8:
                    mean(m + 1)
                for half in range(2):
                    dve.wait_ge(sem("h_hi"), 2 * m + half + 1)
                    for k in range(4):
                        kk = 4 * half + k
                        ins = V.scalar_tensor_tensor(out=hL[:, kk, c:c + n], in0=work[2 * (m % 2) + half][:, k * P:k * P + n],
                                                     scalar=vec[:, NORM1 + kk:NORM1 + kk + 1],
                                                     in1=hH[:, kk, c:c + n].bitcast(F32), op0=ALU.mult, op1=ALU.subtract)
                    ins.then_inc(sem("h_lo"), 1)

        def start_tensor(pe):
            pe.wait_ge(sem("consts"), 16 * 5)
            PE.transpose(work[4][:, 0:25], vec_rows[:, :], ident[0:25, 0:25]).then_inc(sem("vec_T"), 1)
            pe.sem_inc(sem("d_done"), 3)
            for m in range(9):
                c, n = tiles9[m]
                pe.wait_ge(sem("x_scaled"), m + 1)
                for half in range(2):
                    if m >= 2:
                        pe.wait_ge(sem("h_lo"), 2 * (m - 2) + half + 1)
                    for k in range(4):
                        kk = 4 * half + k
                        ins = PE.transpose(work[2 * (m % 2) + half][:, k * P:k * P + n], xs[0:n, m % 2, kk * P:kk * P + P],
                                           ident[0:n, 0:n])
                    ins.then_inc(sem("turned"), 1)

        sc_ab = ExitStack()
        row_t = sb("row_t", [72, T], F32, sc_ab)
        ab_x, ab_e = sb("ab_x", [8, T], F32, sc_ab), sb("ab_e", [8, T], F32, sc_ab)
        reset = sb("reset_sb", [8, T], F32, sc_ab)
        ab_v = sb("ab_v", [8, 4], F32, sc_ab)
        sc_ab.close()
        sc_d = ExitStack()
        pre = sb("pre", [P, 2, 3 + TP + NSEQ * 7], F32, sc_d)
        conv = sb("conv", [P, TP + NSEQ * 7], F32, sc_d)
        qkv = sb("qkv", [P, 3, T], F32, sc_d)
        sq = sb("sq", [P, 2, NT9 * P], F32, sc_d)
        em = sb("em", [P, NT9, P], F32, sc_d)
        cum_b, beta_b = sb("cum_b", [P, T], F32, sc_d), sb("beta_b", [P, T], F32, sc_d)
        turned = sb("turned", [P, NT9, 3, P], F32, sc_d)
        kbg, kd, vb = (sb(n, [P, NT9, P], F32, sc_d) for n in ("kbg", "kd", "vb"))
        tok3 = sb("tok3", [P, 2, 3, P], F32, sc_d)
        at = sb("at", [P, NT9, P], F32, sc_d)
        bd = sb("bd", [P, NCH, P], F32, sc_d)
        qk_t = sb("qk_t", [P, NT9, P], F32, sc_d)
        silz = sb("silz", [P, T], F32, sc_d)
        t_sys, systems = sb("t_sys", [NCH * NBLK, BLK * BLK], F32, sc_d), sb("systems", [P, 2, BLK * BLK], F32, sc_d)
        state = sb("state", [P, 2, P], F32, sc_d)
        s0 = sb("s0", [P, NSEQ, P], F32, sc_d)
        vnew = sb("vnew", [P, 2, P], F32, sc_d)
        tails, sc_in, sc_t = sb("tails", [P, 3, 27], F32, sc_d), tok3[0:28, 0], sb("sc_t", [P, 3, 28], F32, sc_d)
        tails_t = sb("tails_t", [27, 3, P], F32, sc_d)
        col = sb("col", [P, NT9, 72], F32, sc_d)
        ecum, elast = sb("ecum", [P, NT9, 8], F32, sc_d), sb("elast", [P, NT9, 8], F32, sc_d)
        ck, cq, cbg, ckd, cqg, cb, ccum = (sb(n, [P, NT9], F32, sc_d) for n in ("ck", "cq", "cbg", "ckd", "cqg", "cb", "ccum"))
        ssn = sb("ssn", [P, 2 * NT9], F32, sc_d)
        glast = sb("glast", [P, 2 * NCH], F32, sc_d)
        osum = sb("osum", [P, NT9], F32, sc_d)
        masks = sb("masks_sb", [P, 5, P], F32, sc_d)
        masks_s = sb("masks_s_sb", [TS, 2, TS], F32, sc_d)
        own_row, own_col = sb("own_row_sb", [P, NSEQ, TS], F32, sc_d), sb("own_col_sb", [TS, NSEQ], F32, sc_d)
        small8 = sb("small8", [TS, 4, TS], F32, sc_d)
        sc_d.close()
        e_all = sq[:, 0].rearrange("p (t i) -> p t i", i=P)
        emb = sq[:, 1].rearrange("p (t i) -> p t i", i=P)
        t_all = sq[:, 0, 0:TP].rearrange("p (t i) -> p t i", i=P)
        tt_all = emb
        at_lvl = [qkv[:, s, 0:TP].rearrange("p (t i) -> p t i", i=P) for s in range(3)]
        y_all = pre[:, 1, 0:TP].rearrange("p (t i) -> p t i", i=P)
        kdm = pre[0:TS, 0, 0:TP].rearrange("p (b i) -> p b i", i=P)
        nw = conv[:, 0:T]
        a_sys, p_sys = systems[0:NCH * NBLK, 0], systems[0:NCH * NBLK, 1]
        wm, qm = (systems[:, x].rearrange("p (b t) -> p b t", t=TS) for x in range(2))
        o_raw = em
        oa_out = cum_b
        SEQ = lambda ap: ap.rearrange("p (b t) -> p b t", t=TSEQ)
        W7 = TSEQ + 3
        tokens = [(P * t, P) for t in range(NCH)] + [(TP, TS)]

        def ab_sync(sp):
            sp.wait_ge(sem("zeroed"), 2)
            sp.dma_start(ab_v[0:4, 0:1], a["a_log"].rearrange("o h -> h o")).then_inc(sem("consts"), 16)
            sp.dma_start(ab_v[0:4, 1:2], a["dt_bias"].rearrange("o h -> h o")).then_inc(sem("consts"), 16)
            sp.dma_start(reset[:], a["reset"]).then_inc(sem("consts"), 16)
            for dst, name in ((masks, "masks"), (masks_s, "masks_s"), (own_row, "own_row"), (own_col, "own_col"), (t_sys, "unit")):
                sp.dma_start(dst[:], a[name]).then_inc(sem("consts"), 16)

        def ab_pool(pool):
            pool.wait_ge(sem("h_lo"), 18)
            G.memset(ab_v[:], 0.0).then_inc(sem("zeroed"), 1)
            pool.wait_ge(sem("consts"), 208)
            G.memset(row_t[:], 0.0).then_inc(sem("zeroed"), 1)
            split_lo(pool, N_HEAD, N_HEAD)
            split_lo(pool, N_HEAD + 1, N_HEAD + 1)
            pool.wait_ge(sem("cols_read"), 1)
            G.memset(sq[:, :, T:NT9 * P], 0.0).then_inc(sem("zeroed"), 1)
            G.memset(bd[:], 0.0).then_inc(sem("zeroed"), 1)
            G.memset(osum[:], 0.0).then_inc(sem("zeroed"), 1)

        def ab_scalar(act):
            act.wait_ge(sem("zeroed"), 3)
            for t in range(NG):
                done(act, N_AB, t)
                A.activation(row_t[32:40, TN * t:TN * t + TN], dense[t][0:8, 0:TN], ACT.Sigmoid).then_inc(sem("ab_act"), 1)
            split_hi(act, N_HEAD, N_HEAD, N_HEAD // 2 + 1)
            split_hi(act, N_HEAD + 1, N_HEAD + 1, (N_HEAD + 1) // 2 + 1)
            act.wait_ge(sem("consts"), 208)
            A.activation(ab_v[:, 2:3], ab_v[:, 0:1], ACT.Exp).then_inc(sem("ab_act"), 1)
            act.wait_ge(sem("ab_x"), 1)
            chA.link(act, A.activation(ab_e[:], ab_x[:], ACT.Abs))
            chA.link(act, A.activation(ab_e[:], ab_e[:], ACT.Exp, scale=-1.0))
            A.activation(ab_e[:], ab_e[:], ACT.Ln, bias=1.0).then_inc(sem("ab_act"), 1)
            act.wait_ge(sem("rows_ready"), 1)
            act.dma_start(rows_d[0:8, :], row_t[0:8, :]).then_inc(sem("rows_out"), 16)
            act.dma_start(rows_d[8:16, :], row_t[32:40, :]).then_inc(sem("rows_out"), 16)
            act.wait_ge(sem("cols_read"), 1)
            A.activation(ecum[:], col[:, :, 0:8], ACT.Exp)
            A.activation(elast[:], col[:, :, 64:72], ACT.Exp)
            act.wait_ge(sem("rows_out"), 32)
            act.wait_ge(sem("zeroed"), 6)

        def ab_vector(dve):
            dve.wait_ge(sem("consts"), 208)
            for t in range(NG):
                dve.wait_ge(sem("ab_act"), t + 1)
                ins = V.tensor_scalar(ab_x[:, TN * t:TN * t + TN], dense[t][0:8, 0:TN], ab_v[:, 1:2], None, ALU.add)
                ins.then_inc(sem(f"d_free{t}"), 1)
            for t in range(NG):
                dve.wait_ge(sem(f"d_free{t}"), 1)
            dve.wait_ge(sem("ab_act"), 4)
            V.tensor_scalar(ab_v[:, 3:4], ab_v[:, 2:3], -1.0, None, ALU.mult).then_inc(sem("ab_x"), 1)
            dve.wait_ge(sem("ab_act"), 5)
            chV.link(dve, V.scalar_tensor_tensor(out=ab_x[:], in0=ab_x[:], scalar=0.0, in1=ab_e[:], op0=ALU.max, op1=ALU.add))
            chV.link(dve, V.tensor_scalar(ab_x[:], ab_x[:], ab_v[:, 3:4], None, ALU.mult))
            chV.link(dve, V.tensor_tensor_scan(row_t[0:8, :], reset[:], ab_x[:], 0.0, ALU.mult, ALU.add))
            for lo, n, w in ((0, NCH, P), (TP, NSEQ, TSEQ)):
                x = row_t[0:8, lo:lo + n * w].rearrange("p (c i) -> p c i", i=w)
                y = row_t[64:72, lo:lo + n * w].rearrange("p (c i) -> p c i", i=w)
                ins = V.tensor_tensor(y, x[:, :, w - 1:w].to_broadcast([8, n, w]), x, ALU.subtract)
                chV.link(dve, ins)
            V.memset(col[:, NCH], 0.0).then_inc(sem("rows_ready"), 1)
            for i, (lo, hi) in enumerate(((0, 5), (5, 8))):
                dve.wait_ge(sem("cols_turned"), i + 1)
                chV.link(dve, V.tensor_copy(col[:, lo:hi], work[i][:, 0:72 * (hi - lo)].rearrange("p (t r) -> p t r", r=72)))
            V.tensor_copy(col[0:TS, NCH], work[1][0:TS, 216:288]).then_inc(sem("cols_read"), 1)
            dve.wait_ge(sem("rows_out"), 32)

        def ab_tensor(pe):
            for t in range(NG):
                pe.wait_ge(sem("h_lo"), 6 * (t + 1))
                job(pe, N_AB, N_AB, t)
            pe.wait_ge(sem("rows_ready"), 1)
            pe.wait_ge(sem("h_lo"), 18)
            for t, (c, n) in enumerate(tokens):
                ins = PE.transpose(work[t // 5][0:n, 72 * (t % 5):72 * (t % 5) + 72], row_t[0:72, c:c + n], ident[0:72, 0:72])
                if t in (4, 8):
                    ins.then_inc(sem("cols_turned"), 1)

        def head_sync(sp, h):
            def load(j):
                col = j * WA + h * HD if j < 4 else pair_cols(h, j - 4)
                load_cols(sp, N_HEAD + j, N_HEAD + j + 8 * h, w_in, col)
            for j in range(2):
                load(j)
            sp.wait_ge(sem("back"), NT9 * h + 1)
            for j in range(3):
                sp.dma_start(sc_in[0:24, j, :], a["state_conv"][0].rearrange("b t c -> (b t) c")[:, bass.ds(j * WA + h * HD, HD)]).then_inc(sem("sc_loaded"), 16)
                sp.dma_start(sc_in[24:28, j, :], a["conv_w"][0][:, bass.ds(j * WA + h * HD, HD)]).then_inc(sem("sc_loaded"), 16)
            for j in range(2, 6):
                load(j)
            sp.wait_ge(sem("oa_stored"), 16 * h + 1)
            sp.wait_ge(sem("rows_out"), 32)
            sp.dma_start(cum_b[:], rows_d[bass.ds(h, 1), :].to_broadcast([P, T])).then_inc(sem("cum_loaded"), 16)
            sp.wait_ge(sem("at_made"), h + 1)
            sp.dma_start(beta_b[:], rows_d[bass.ds(h + 12, 1), :].to_broadcast([P, T])).then_inc(sem("beta_loaded"), 16)
            sp.wait_ge(sem("s0_stored"), 16 * h + 1)
            sp.dma_start(s0[:], a["state_delta"][0][:, bass.ds(h, 1)].rearrange("b o k v -> k (b o) v")).then_inc(sem("s0_loaded"), 16)
            for j in range(6, 8):
                load(j)
            for g in range(3):
                drop = WIN[0] - TSEQ if g == 0 else PAST
                src, dst = (x[0][bass.ds(2 * h, 2)].rearrange("b t s h d -> b t (s h d)") for x in (a[f"cache_win{g}"], a[f"win{g}_s"]))
                sp.dma_start(dst[:, 0:drop], src[:, min(WIN[g], PAST) - drop:]).then_inc(sem("cache_out"), 16)
            sp.wait_ge(sem("tails_out"), h + 1)
            for j in range(3):
                c0 = bass.ds(j * WA + h * HD, HD)
                sp.dma_start(a["conv_p"][0, 0][:, c0], tails_t[0:3, j]).then_inc(sem("tails_stored"), 16)
                sp.dma_start(a["conv_s"][0].rearrange("b t c -> (b t) c")[:, c0], tails_t[3:27, j]).then_inc(sem("tails_stored"), 16)
            sp.wait_ge(sem("at_made"), h + 2)
            for b in range(NBLK):
                r = slice(BLK * b, BLK * b + BLK)
                sp.dma_start(diag_d[:, b].rearrange("c j i -> j c i"), at[r, 0:NCH, r]).then_inc(sem("diag_out"), 16)
            sp.wait_ge(sem("diag_out"), 16 * NBLK * (h + 1))
            sp.dma_start(a_sys, diag_d.rearrange("c b j i -> (c b) (j i)")).then_inc(sem("diag_in"), 16)
            sp.wait_ge(sem("t_solved"), h + 1)
            sp.dma_start(tinv_d.rearrange("c b j i -> (c b) (j i)"), t_sys[:]).then_inc(sem("tinv_out"), 16)
            sp.wait_ge(sem("tinv_out"), 16 * (h + 1) + 1)
            for b in range(NBLK):
                r = slice(BLK * b, BLK * b + BLK)
                sp.dma_start(bd[r, :, r], tinv_d[:, b].rearrange("c i j -> i c j")).then_inc(sem("tinv_in"), 16)

        def head_pool(pool, h):
            def split(j):
                split_lo(pool, N_HEAD + j, N_HEAD + j + 8 * h)
            for j in range(2, 7):
                split(j)
            pool.wait_ge(sem("e_ready"), h + 1)
            pool.wait_ge(sem("o_turned"), 3 * h + 1)
            G.tensor_tensor(em[:, 0:NCH], e_all[:, 0:NCH], masks[:, 0:1].to_broadcast([P, NCH, P]), ALU.mult).then_inc(sem("em_made"), 1)
            G.tensor_tensor(em[0:TS, NCH, 0:TS], e_all[0:TS, NCH, 0:TS], masks_s[:, 0], ALU.mult).then_inc(sem("em_made"), 1)
            pool.wait_ge(sem("beta_loaded"), 16 * h + 16)
            chG.link(pool, G.tensor_tensor(emb[:, 0:NCH], e_all[:, 0:NCH], beta_b[:, 0:TP].rearrange("p (t i) -> p t i", i=P), ALU.mult))
            chG.link(pool, G.tensor_tensor(emb[0:TS, NCH, 0:TS], e_all[0:TS, NCH, 0:TS], beta_b[0:TS, TP:T], ALU.mult))
            G.tensor_tensor(emb[:, 0:NCH], emb[:, 0:NCH], masks[:, 1:2].to_broadcast([P, NCH, P]), ALU.mult).then_inc(sem("emb_made"), 1)
            G.tensor_tensor(emb[0:TS, NCH, 0:TS], emb[0:TS, NCH, 0:TS], masks_s[:, 1], ALU.mult).then_inc(sem("emb_made"), 1)
            pool.wait_ge(sem("at_made"), h + 2)
            for s in range(3):
                G.tensor_tensor(at_lvl[s], at[:, 0:NCH], masks[:, 2 + s:3 + s].to_broadcast([P, NCH, P]), ALU.mult).then_inc(sem("lvl_made"), 1)
            split(7)
            split(8)
            pool.wait_ge(sem("nw_made"), 3 * h + 3)
            G.tensor_tensor(wm, nw[:, TP:T].rearrange("p (o i) -> p o i", o=1).to_broadcast([P, NSEQ, TS]), own_row[:], ALU.mult).then_inc(sem("smp_made"), 1)
            G.tensor_tensor(qm, turned[:, NCH, 2:3, 0:TS].to_broadcast([P, NSEQ, TS]), own_row[:], ALU.mult).then_inc(sem("smp_made"), 1)
            G.tensor_tensor(kdm, kd[0:TS, NCH:NCH + 1].to_broadcast([TS, NSEQ, P]),
                            own_col[:].rearrange("p (b o) -> p b o", o=1).to_broadcast([TS, NSEQ, P]), ALU.mult).then_inc(sem("smp_made"), 1)
            split(9)

        def head_scalar(act, h):
            def split(j):
                split_hi(act, N_HEAD + j, N_HEAD + j + 8 * h, (N_HEAD + j) // 2 + 4 * h + 1)

            def filled(*groups):
                for c in groups:
                    fill_pair(act, N_HEAD + 4, N_HEAD + 4 + 8 * h, h, c, 6 * h)
            for j in range(4):
                n = N_HEAD + j + 8 * h
                if j == 3:
                    act.wait_ge(sem("oa_part"), 3 * h + 1)
                    for t in range(NG):
                        done(act, n, t)
                        A.activation(silz[:, TN * t:TN * t + TN], dense[t][:, 0:TN], ACT.Silu).then_inc(sem(f"d_free{t}"), 1)
                    split(5)
                    break
                s = j % 2
                if j == 0:
                    act.wait_ge(sem("s0_done"), 2 * h + 1)
                for t in range(NG):
                    done(act, n, t)
                    if j == 2 and t == 0:
                        act.wait_ge(sem("conv_done"), 3 * h + 1)
                    c = TN * t
                    w = min(TN, TP - c)
                    ins = A.activation(pre[:, s, 3 + c:3 + c + w], dense[t][:, 0:w], ACT.Copy)
                    if w < TN:
                        ins = A.activation(pre[:, s, 3 + TP:].rearrange("p (b t) -> p b t", t=W7)[:, :, 3:W7], SEQ(dense[t][:, w:TN]), ACT.Copy)
                    ins.then_inc(sem(f"d_free{t}"), 1)
                split(j + 2)
                if j >= 1:
                    silu(act, h, j - 1)
            silu(act, h, 2)
            filled(0, 1, 2)
            split(6)
            act.wait_ge(sem("mean"), NT9 + 2 * h + 1)
            A.activation(ssn[:], ssn[:], ACT.Sqrt).then_inc(sem("root"), 1)
            act.wait_ge(sem("e_arg"), h + 1)
            A.activation(e_all[:, 0:NCH], e_all[:, 0:NCH], ACT.Exp)
            A.activation(e_all[0:TS, NCH, 0:TS], e_all[0:TS, NCH, 0:TS], ACT.Exp).then_inc(sem("e_ready"), 1)
            A.activation(glast[:, 0:NCH], cum_b[:, P - 1:TP:P], ACT.Exp)
            A.activation(glast[:, NCH:2 * NCH], cum_b[:, TP + TSEQ - 1:T:TSEQ], ACT.Exp).then_inc(sem("glast"), 1)
            act.wait_ge(sem("cols_made"), h + 1)
            for t, (c, n) in enumerate(tokens):
                act.wait_ge(sem("fwd"), 2 * (NT9 * h + t) + 2)
                b = work[2 + t % 2]
                if t >= 2:
                    act.wait_ge(sem("back"), NT9 * h + t)
                A.activation(tok3[0:n, t % 2, 1], b[0:n, 0:P], ACT.Copy, scale=cq[0:n, t:t + 1])
                A.activation(tok3[0:n, t % 2, 2], b[0:n, 0:P], ACT.Copy, scale=cqg[0:n, t:t + 1])
                A.activation(vb[0:n, t], b[0:n, P:2 * P], ACT.Copy, scale=cb[0:n, t:t + 1]).then_inc(sem("ev_a"), 1)
                if t >= 1:
                    turned_back(act, h, t - 1)
            turned_back(act, h, NCH)
            filled(3, 4, 5)
            split(7)
            filled(6, 7, 8)
            act.wait_ge(sem("tinv_in"), 16 * NBLK * (h + 1))
            act.wait_ge(sem("at_made"), h + 2)
            A.activation(t_all, bd[:], ACT.Copy).then_inc(sem("t_set"), 1)
            split(8)
            for s in range(3):
                for half in range(2):
                    act.wait_ge(sem("y_done"), 6 * h + 2 * s + half + 2)
                    A.activation(y_all[:, 4 * half:4 * half + 4], work[half][:].rearrange("p (t i) -> p t i", i=P), ACT.Copy).then_inc(sem("y_read"), 1)
            for i in range(3):
                act.wait_ge(sem("nw_done"), 3 * h + i + 1)
                w = 4 * P if i < 2 else TS
                A.activation(nw[:, 4 * P * i:4 * P * i + w], work[(0, 1, 2)[i]][:, 0:w], ACT.Copy, scale=-1.0).then_inc(sem("nw_made"), 1)
            for t, (c, n) in enumerate(tokens):
                act.wait_ge(sem("v_done"), NT9 * h + t + 2)
                A.activation(vnew[0:n, t % 2], work[t % 2][0:n, 0:P], ACT.Copy).then_inc(sem("v_read"), 1)
                if t >= 1:
                    out_sum(act, h, t - 1)
                if t in (1, 5, 8):
                    filled(9 + t // 4)
            split(9)
            out_sum(act, h, NCH)
            act.wait_ge(sem("mean"), NT9 + 2 * h + 2)
            A.activation(osum[:], osum[:], ACT.Sqrt).then_inc(sem("root"), 1)
            act.wait_ge(sem("s_final"), h + 1)
            act.dma_start(a["delta_p"][0, 0][bass.ds(h, 1)].rearrange("o k v -> (o k) v"), state[:, (NCH - 1) % 2]).then_inc(sem("state_stored"), 16)
            act.wait_ge(sem("s0_new"), h + 2)
            act.dma_start(a["delta_s"][0][:, bass.ds(h, 1)].rearrange("b o k v -> k (b o) v"), s0[:]).then_inc(sem("s0_stored"), 16)
            act.wait_ge(sem("oa_ready"), h + 1)
            act.dma_start(oa_d[bass.ds(h, 1)].rearrange("o p t -> (o p) t"), oa_out[:]).then_inc(sem("oa_stored"), 16)

        def silu(act, h, j):
            act.wait_ge(sem("conv_done"), 3 * h + j + 1)
            if j == 0:
                act.wait_ge(sem("y_done"), 6 * h + 1)
            A.activation(qkv[:, j, 0:TP], conv[:, 0:TP], ACT.Silu)
            ins = A.activation(SEQ(qkv[:, j, TP:T]), conv_out(), ACT.Silu)
            ins.then_inc(sem("silu"), 1)
            if j < 2:
                if j == 0:
                    act.wait_ge(sem("v_done"), NT9 * h + 1)
                act.wait_ge(sem("silu"), 3 * h + j + 1)
                A.activation(sq[:, j, 0:T], qkv[:, j, :], ACT.Square).then_inc(sem("squared"), 1)

        def conv_out():
            return bass.AP(conv, TP + 3, [[TP + NSEQ * W7, P], [W7, NSEQ], [1, TSEQ]])

        def turned_back(act, h, t):
            n = tokens[t][1]
            act.wait_ge(sem("back"), NT9 * h + t + 2)
            A.activation(turned[:, t, :, 0:n], work[4][:, 0:3 * P].rearrange("p (x i) -> p x i", x=3)[:, :, 0:n], ACT.Copy).then_inc(sem("back_read"), 1)

        def out_sum(act, h, t):
            n = tokens[t][1]
            act.wait_ge(sem("o_done"), NT9 * h + t + 1)
            if t == 0:
                act.wait_ge(sem("at_made"), h + 2)
            A.activation(o_raw[0:n, t], work[2][0:n, 0:P], ACT.Copy)
            A.activation(work[2][0:n, 0:P], work[2][0:n, 0:P], ACT.Square, accum_out=osum[0:n, t:t + 1]).then_inc(sem("o_read"), 1)

        def head_vector(dve, h):
            dve.wait_ge(sem("sc_turned"), h + 1)
            chV.link(dve, V.tensor_copy(sc_t[:], work[4][:, 0:84].rearrange("p (j r) -> p j r", j=3)))
            dve.wait_ge(sem("s0_done"), 2 * h + 1)
            for s in range(2):
                V.memset(pre[:, s, 0:3], 0.0)
            for j in range(3):
                s = j % 2
                x = pre[:, s]
                tail = x[:, 3 + TP:].rearrange("p (b t) -> p b t", t=W7)
                chV.link(dve, V.tensor_copy(tail[:, :, 0:3], sc_t[:, j, 0:24].rearrange("p (b t) -> p b t", t=3)))
                n = N_HEAD + j + 8 * h
                for t in range(NG):
                    dve.wait_ge(sem(f"d_free{t}"), n + 1)
                if j == 0:
                    dve.wait_ge(sem("tails_turned"), h + 1)
                chV.link(dve, V.tensor_copy(tails[:, j, 0:3], x[:, TP:TP + 3]))
                chV.link(dve, V.tensor_copy(tails[:, j, 3:27].rearrange("p (b t) -> p b t", t=3), tail[:, :, TSEQ:W7]))
                if j == 0:
                    dve.wait_ge(sem("v_done"), NT9 * h + 1)
                else:
                    dve.wait_ge(sem("silu"), 3 * h + j)
                L = TP + NSEQ * W7
                chV.link(dve, V.tensor_scalar(conv[:], x[:, 0:L], sc_t[:, j, 24:25], None, ALU.mult))
                for i in (1, 2, 3):
                    ins = V.scalar_tensor_tensor(out=conv[:], in0=x[:, i:i + L], scalar=sc_t[:, j, 24 + i:25 + i], in1=conv[:], op0=ALU.mult, op1=ALU.add)
                    if i < 3:
                        chV.link(dve, ins)
                ins.then_inc(sem("conv_done"), 1)
            dve.wait_ge(sem("tails_turned"), h + 2)
            dve.wait_ge(sem("tails_stored"), 96 * h + 1)
            V.tensor_copy(tails_t[:], work[2][0:27, 0:3 * P].rearrange("p (j i) -> p j i", j=3)).then_inc(sem("tails_out"), 1)
            dve.wait_ge(sem("ss_done"), h + 1)
            V.tensor_scalar(ssn[:], work[4][:, 0:2 * NT9], EPS, None, ALU.add).then_inc(sem("mean"), 1)
            dve.wait_ge(sem("cum_loaded"), 16 * h + 16)
            chV.link(dve, V.tensor_copy(ccum[:], col[:, :, bass.ds(h, 1)].rearrange("p t o -> p (t o)")))
            chV.link(dve, V.tensor_copy(cb[:], col[:, :, bass.ds(h + 36, 1)].rearrange("p t o -> p (t o)")))
            for t, (c, n) in enumerate(tokens):
                ins = V.tensor_scalar(e_all[0:n, t, 0:n], cum_b[0:n, c:c + n], ccum[0:n, t:t + 1], 0.0, ALU.subtract, ALU.min)
            ins.then_inc(sem("e_arg"), 1)
            dve.wait_ge(sem("root"), NT9 + 2 * h + 1)
            chV.link(dve, V.reciprocal(ssn[:], ssn[:]))
            rq, rk = ssn[:, 0:NT9], ssn[:, NT9:2 * NT9]
            ec, el = (x[:, :, bass.ds(h, 1)].rearrange("p t o -> p (t o)") for x in (ecum, elast))
            V.tensor_copy(ck[:], rk)
            V.tensor_scalar(cq[:], rq, HD ** -0.5, None, ALU.mult)
            V.scalar_tensor_tensor(out=cqg[:], in0=rq, scalar=HD ** -0.5, in1=ec, op0=ALU.mult, op1=ALU.mult)
            chV.link(dve, V.tensor_tensor(ckd[:], rk, el, ALU.mult))
            chV.link(dve, V.tensor_tensor(cbg[:], rk, ec, ALU.mult))
            V.tensor_tensor(cbg[:], cbg[:], cb[:], ALU.mult).then_inc(sem("cols_made"), 1)
            dve.wait_ge(sem("cols_made"), h + 1)
            for t, (c, n) in enumerate(tokens):
                dve.wait_ge(sem("fwd"), 2 * (NT9 * h + t) + 1)
                if t >= 2:
                    dve.wait_ge(sem("back"), NT9 * h + t)
                b = work[t % 2][0:n, 0:P]
                V.tensor_scalar(tok3[0:n, t % 2, 0], b, ck[0:n, t:t + 1], None, ALU.mult)
                V.tensor_scalar(kbg[0:n, t], b, cbg[0:n, t:t + 1], None, ALU.mult)
                V.tensor_scalar(kd[0:n, t], b, ckd[0:n, t:t + 1], None, ALU.mult).then_inc(sem("ev_v"), 1)
            dve.wait_ge(sem("em_made"), 2 * h + 2)
            dve.wait_ge(sem("emb_made"), 2 * h + 2)
            for i in range(5):
                dve.wait_ge(sem("kk_done"), 5 * h + i + 1)
                b = work[i % 2][:].rearrange("p (t x i) -> p t x i", t=2, x=2)
                if i < 4:
                    V.tensor_tensor(at[:, 2 * i:2 * i + 2], b[:, :, 0], emb[:, 2 * i:2 * i + 2], ALU.mult)
                    ins = V.tensor_tensor(qk_t[:, 2 * i:2 * i + 2], b[:, :, 1], em[:, 2 * i:2 * i + 2], ALU.mult)
                else:
                    V.tensor_tensor(at[0:TS, NCH, 0:TS], work[0][0:TS, 0:TS], emb[0:TS, NCH, 0:TS], ALU.mult)
                    ins = V.tensor_tensor(qk_t[0:TS, NCH, 0:TS], work[0][0:TS, TS:2 * TS], em[0:TS, NCH, 0:TS], ALU.mult)
                ins.then_inc(sem("kk_read"), 1)
                dve.wait_ge(sem("kk_read"), 5 * h + i + 1)
            dve.sem_inc(sem("at_made"), 1)
            dve.wait_ge(sem("s8"), 3 * h + 1)
            V.tensor_copy(small8[:, 0], work[2][0:TS, 0:TS]).then_inc(sem("s8_read"), 1)
            chV.link(dve, V.tensor_tensor(small8[:, 2], ident[0:TS, 0:TS], at[0:TS, NCH, 0:TS], ALU.subtract))
            dve.wait_ge(sem("s8"), 3 * h + 2)
            V.tensor_tensor(small8[:, 1], at[0:TS, NCH, 0:TS], work[3][0:TS, 0:TS], ALU.subtract).then_inc(sem("s8_read"), 1)
            dve.wait_ge(sem("s8"), 3 * h + 3)
            chV.link(dve, V.tensor_tensor(tt_all[0:TS, NCH, 0:TS], work[2][0:TS, 0:TS], small8[:, 2], ALU.add))
            dve.wait_ge(sem("diag_in"), 16 * (h + 1))
            dve.wait_ge(sem("tinv_out"), 16 * h + 1)
            av = a_sys.rearrange("s (j i) -> s i j", i=BLK)
            tv = t_sys[:].rearrange("s (i c) -> s i c", c=BLK)
            for i in range(1, BLK):
                prod = p_sys[:, 0:i * i].rearrange("s (c j) -> s c j", j=i)
                chV.link(dve, V.tensor_tensor(prod, tv[:, 0:i, 0:i].rearrange("s j c -> s c j"), av[:, i:i + 1, 0:i].to_broadcast([NCH * NBLK, i, i]), ALU.mult))
                chV.link(dve, V.tensor_reduce(p_sys[:, 240:240 + i], prod, AX.X, ALU.add))
                chV.link(dve, V.tensor_scalar(tv[:, i, 0:i], p_sys[:, 240:240 + i], -1.0, None, ALU.mult))
            dve.sem_inc(sem("t_solved"), 1)
            for half in range(2):
                dve.wait_ge(sem("tt_done"), 2 * h + half + 1)
                V.tensor_copy(tt_all[:, 4 * half:4 * half + 4], work[half][:].rearrange("p (t i) -> p t i", i=P)).then_inc(sem("tt_set"), 1)
            for s in range(3):
                for half in range(2):
                    r = slice(4 * half, 4 * half + 4)
                    dve.wait_ge(sem("z_done"), 6 * h + 2 * s + half + 1)
                    dve.wait_ge(sem("tt_set"), 8 * h + 2 * s + half + 2)
                    if s < 2:
                        V.tensor_tensor(t_all[:, r], t_all[:, r], work[2][:].rearrange("p (t i) -> p t i", i=P), ALU.subtract)
                    V.tensor_tensor(tt_all[:, r], tt_all[:, r], work[3][:].rearrange("p (t i) -> p t i", i=P), ALU.subtract).then_inc(sem("tt_set"), 1)
            dve.wait_ge(sem("glast"), h + 1)
            dve.wait_ge(sem("state_stored"), 16 * h + 1)
            for t in range(NCH):
                dve.wait_ge(sem("sn_done"), NCH * h + t + 1)
                if t == 0:
                    ins = V.tensor_copy(state[:, 0], work[4][:, 0:P])
                else:
                    ins = V.scalar_tensor_tensor(out=state[:, t % 2], in0=state[:, (t - 1) % 2], scalar=glast[:, t:t + 1], in1=work[4][:, 0:P],
                                                 op0=ALU.mult, op1=ALU.add)
                ins.then_inc(sem("s_new"), 1)
                dve.wait_ge(sem("s_new"), NCH * h + t + 1)
            dve.sem_inc(sem("s_final"), 1)
            for i in range(2):
                dve.wait_ge(sem("s0_done"), 2 * h + i + 2)
                for b in range(4):
                    q = 4 * i + b
                    ins = V.scalar_tensor_tensor(out=s0[:, q], in0=s0[:, q], scalar=glast[:, NCH + q:NCH + q + 1], in1=work[3 + i][:, P * b:P * b + P],
                                                 op0=ALU.mult, op1=ALU.add)
                chV.link(dve, ins)
            dve.sem_inc(sem("s0_new"), 1)
            dve.wait_ge(sem("o_read"), NT9 * h + NT9)
            V.tensor_scalar(osum[:], osum[:], 1.0 / HD, EPS, ALU.mult, ALU.add).then_inc(sem("mean"), 1)
            dve.wait_ge(sem("root"), NT9 + 2 * h + 2)
            chV.link(dve, V.reciprocal(osum[:], osum[:]))
            for t, (c, n) in enumerate(tokens):
                ins = V.tensor_scalar(o_raw[0:n, t], o_raw[0:n, t], osum[0:n, t:t + 1], None, ALU.mult)
            ins.then_inc(sem("o_normed"), 1)
            for i, (c, n) in enumerate(((0, 512), (512, 512), (TP, TS))):
                dve.wait_ge(sem("o_turned"), 3 * h + i + 2)
                V.scalar_tensor_tensor(out=oa_out[:, c:c + n], in0=work[i][:, 0:n], scalar=vec[:, GNORM:GNORM + 1], in1=silz[:, c:c + n],
                                       op0=ALU.mult, op1=ALU.mult).then_inc(sem("oa_part"), 1)
            dve.wait_ge(sem("oa_part"), 3 * h + 4)
            dve.sem_inc(sem("oa_ready"), 1)

        def head_tensor(pe, h):
            def fill_parts(first, last):
                for p in range(first, last):
                    part(pe, N_HEAD + 4 + p // 24, N_HEAD + 4 + p // 24 + 8 * h, p % 24)
            for j in range(4):
                for t in range(NG):
                    job(pe, N_HEAD + j, N_HEAD + j + 8 * h, t)
                if j == 0:
                    pe.wait_ge(sem("sc_loaded"), 96 * h + 96)
                    pe.wait_ge(sem("s0_new"), h + 1)
                    apart(pe)
                    for x in range(3):
                        ins = PE.transpose(work[4][:, 28 * x:28 * x + 28], sc_in[:, x], ident[0:28, 0:28])
                    ins.then_inc(sem("sc_turned"), 1)
            fill_parts(0, 24)
            pe.wait_ge(sem("conv_done"), 3 * h + 3)
            pe.wait_ge(sem("oa_part"), 3 * h + 1)
            for j in range(3):
                ins = PE.transpose(work[2][0:27, P * j:P * j + P], tails[:, j], ident[:, :])
            ins.then_inc(sem("tails_turned"), 1)
            pe.wait_ge(sem("squared"), 2 * h + 2)
            for x in range(2):
                for t in range(NT9):
                    ins = PE.matmul(work[4][:, NT9 * x + t:NT9 * x + t + 1], sq[:, x, P * t:P * t + P], ones[:, 0:1], start=True, stop=True)
            ins.then_inc(sem("ss_done"), 1)
            pe.wait_ge(sem("silu"), 3 * h + 3)
            pe.wait_ge(sem("tails_out"), h + 1)
            for t, (c, n) in enumerate(tokens):
                if t >= 2:
                    pe.wait_ge(sem("ev_v"), NT9 * h + t - 1)
                PE.transpose(work[t % 2][0:n, 0:P], qkv[:, 1, c:c + n], ident[:, :]).then_inc(sem("fwd"), 1)
                if t >= 2:
                    pe.wait_ge(sem("ev_a"), NT9 * h + t - 1)
                PE.transpose(work[2 + t % 2][0:n, 0:P], qkv[:, 0, c:c + n], ident[:, :])
                PE.transpose(work[2 + t % 2][0:n, P:2 * P], qkv[:, 2, c:c + n], ident[:, :]).then_inc(sem("fwd"), 1)
                fill_parts(24 + 2 * t, 26 + 2 * t)
                if t >= 1:
                    back(pe, h, t - 1)
            back(pe, h, NCH)
            for i in range(5):
                if i == 0:
                    pe.wait_ge(sem("ev_v"), NT9 * h + NT9)
                    pe.wait_ge(sem("ev_a"), NT9 * h + NT9)
                if i >= 2:
                    pe.wait_ge(sem("kk_read"), 5 * h + i - 1)
                for t in ((2 * i, 2 * i + 1) if i < 4 else (NCH,)):
                    n = tokens[t][1]
                    pe.wait_ge(sem("back_read"), NT9 * h + t + 1)
                    o = (2 * P * (t % 2)) if i < 4 else 0
                    ins = PE.matmul(work[i % 2][0:n, o:o + 2 * n].rearrange("p (x i) -> p x i", x=2), turned[:, t, 0, 0:n], turned[:, t, 0:2, 0:n], start=True, stop=True)
                ins.then_inc(sem("kk_done"), 1)
            pe.wait_ge(sem("at_made"), h + 2)
            apart(pe)
            PE.transpose(work[2][0:TS, 0:TS], at[0:TS, NCH, 0:TS], ident[0:TS, 0:TS]).then_inc(sem("s8"), 1)
            pe.wait_ge(sem("s8_read"), 2 * h + 1)
            apart(pe)
            PE.matmul(work[3][0:TS, 0:TS], small8[:, 0], at[0:TS, NCH, 0:TS], start=True, stop=True).then_inc(sem("s8"), 1)
            pe.wait_ge(sem("s8_read"), 2 * h + 2)
            apart(pe)
            PE.matmul(work[2][0:TS, 0:TS], small8[:, 0], small8[:, 1], start=True, stop=True).then_inc(sem("s8"), 1)
            fill_parts(42, 76)
            pe.wait_ge(sem("t_set"), h + 1)
            for half in range(2):
                for q in range(4):
                    ins = PE.transpose(work[half][:, P * q:P * q + P], t_all[:, 4 * half + q], ident[:, :])
                ins.then_inc(sem("tt_done"), 1)
            for s in range(3):
                pe.wait_ge(sem("lvl_made"), 3 * h + s + 1)
                for half in range(2):
                    pe.wait_ge(sem("tt_set"), 8 * h + 2 * s + half + 1)
                    if s >= 1:
                        pe.wait_ge(sem("y_read"), 6 * h + 2 * (s - 1) + half + 1)
                    for q in range(4):
                        ins = PE.matmul(work[half][:, P * q:P * q + P], at_lvl[s][:, 4 * half + q], t_all[:, 4 * half + q], start=True, stop=True)
                    ins.then_inc(sem("y_done"), 1)
                fill_parts(76 + 2 * s, 78 + 2 * s)
                for half in range(2):
                    pe.wait_ge(sem("y_read"), 6 * h + 2 * s + half + 1)
                    pe.wait_ge(sem("tt_set"), 8 * h + 2 * s + half + 2)
                    for q in range(4):
                        if s < 2:
                            PE.matmul(work[2][:, P * q:P * q + P], tt_all[:, 4 * half + q], y_all[:, 4 * half + q], start=True, stop=True)
                    for q in range(4):
                        ins = PE.matmul(work[3][:, P * q:P * q + P], y_all[:, 4 * half + q], tt_all[:, 4 * half + q], start=True, stop=True)
                    ins.then_inc(sem("z_done"), 1)
            for i in range(3):
                pe.wait_ge(sem("tt_set"), 8 * h + 8)
                for t in range(4 * i, min(4 * i + 4, NT9)):
                    n = tokens[t][1]
                    ins = PE.matmul(work[i][:, P * (t % 4):P * (t % 4) + n], kbg[0:n, t], tt_all[0:n, t, 0:n], start=True, stop=True)
                ins.then_inc(sem("nw_done"), 1)
            pe.wait_ge(sem("nw_made"), 3 * h + 3)
            for t in range(NCH):
                if t >= 2:
                    pe.wait_ge(sem("v_read"), NT9 * h + t - 1)
                ins = PE.matmul(work[t % 2][:, 0:P], tt_all[:, t], vb[:, t], start=True, stop=(t == 0))
                if t:
                    pe.wait_ge(sem("s_new"), NCH * h + t)
                    ins = PE.matmul(work[t % 2][:, 0:P], nw[:, P * t:P * t + P], state[:, (t - 1) % 2], start=False, stop=True)
                ins.then_inc(sem("v_done"), 1)
                if t >= 1:
                    pe.wait_ge(sem("o_read"), NT9 * h + t)
                    PE.matmul(work[2][:, 0:P], turned[:, t, 2], state[:, (t - 1) % 2], start=True, stop=False)
                pe.wait_ge(sem("v_read"), NT9 * h + t + 1)
                PE.matmul(work[4][:, 0:P], kd[:, t], vnew[:, t % 2], start=True, stop=True).then_inc(sem("sn_done"), 1)
                PE.matmul(work[2][:, 0:P], qk_t[:, t], vnew[:, t % 2], start=(t == 0), stop=True).then_inc(sem("o_done"), 1)
                if t < 7:
                    fill_parts(82 + 2 * t, 84 + 2 * t)
            pe.wait_ge(sem("smp_made"), 3 * h + 3)
            pe.wait_ge(sem("s0_loaded"), 16 * h + 16)
            pe.wait_ge(sem("v_read"), NT9 * h + NCH - 1)
            apart(pe)
            PE.matmul(work[0][0:TS, 0:P], tt_all[0:TS, NCH, 0:TS], vb[0:TS, NCH], start=True, stop=False)
            for b in range(NSEQ):
                ins = PE.matmul(work[0][0:TS, 0:P], wm[:, b], s0[:, b], start=False, stop=(b == NSEQ - 1))
            ins.then_inc(sem("v_done"), 1)
            pe.wait_ge(sem("o_read"), NT9 * h + NCH)
            for b in range(NSEQ):
                PE.matmul(work[2][0:TS, 0:P], qm[:, b], s0[:, b], start=(b == 0), stop=False)
            pe.wait_ge(sem("v_read"), NT9 * h + NT9)
            apart(pe)
            PE.matmul(work[2][0:TS, 0:P], qk_t[0:TS, NCH, 0:TS], vnew[0:TS, 0], start=False, stop=True).then_inc(sem("o_done"), 1)
            pe.wait_ge(sem("s_new"), NCH * h + NCH)
            for i in range(2):
                for b in range(4):
                    ins = PE.matmul(work[3 + i][:, P * b:P * b + P], kdm[:, 4 * i + b], vnew[0:TS, 0], start=True, stop=True)
                ins.then_inc(sem("s0_done"), 1)
            pe.wait_ge(sem("o_normed"), h + 1)
            for i in range(3):
                for t in range(4 * i, min(4 * i + 4, NT9)):
                    n = tokens[t][1]
                    ins = PE.transpose(work[i][:, P * (t % 4):P * (t % 4) + n], o_raw[0:n, t], ident[0:n, 0:n])
                ins.then_inc(sem("o_turned"), 1)

        def back(pe, h, t):
            n = tokens[t][1]
            pe.wait_ge(sem("ev_v"), NT9 * h + t + 1)
            pe.wait_ge(sem("ev_a"), NT9 * h + t + 1)
            if t == 0:
                pe.wait_ge(sem("mean"), NT9 + 2 * h + 1)
            else:
                pe.wait_ge(sem("back_read"), NT9 * h + t)
            if t == NCH:
                apart(pe)
            for x in range(3):
                ins = PE.transpose(work[4][:, P * x:P * x + n], tok3[0:n, t % 2, x], ident[0:n, 0:n])
            ins.then_inc(sem("back"), 1)

        def head_stored(sp):
            sp.wait_ge(sem("oa_stored"), 16 * NH + 1)
            sp.wait_ge(sem("s0_stored"), 16 * NH + 1)
            sp.wait_ge(sem("state_stored"), 16 * NH + 1)
            sp.wait_ge(sem("tails_stored"), 96 * NH + 1)
            sp.wait_ge(sem("cache_out"), 48 * NH)
            for s in range(2):
                sp.wait_ge(sem(f"stored{s}"), 16 * 6 * NH + 1)


        sc_att = ExitStack()
        aq = sb("aq", [P, 4, T], F32, sc_att)
        raw = sb("raw", [P, 3, T], F32, sc_att)
        q_scale = sb("q_scale_sb", [P, 2], F32, sc_att)
        kvt = sb("kvt", [P, NCH, 2, P], F32, sc_att)
        kvs = sb("kvs", [TS, 2, P], F32, sc_att)
        bias_p, bias_s = sb("bias_p_sb", [P, 2, 2 * P], F32, sc_att), sb("bias_s_sb", [2 * TS, PAST + TS], F32, sc_att)
        cache = sb("cache", [P, NSEQ, 2, 2, P], F32, sc_att)
        kct = sb("kct", [P, NSEQ, PAST], F32, sc_att)
        prob = sb("prob", [P, 2, 2, 2 * P], F32, sc_att)
        prob_t = sb("prob_t", [P, 2, 2, 2, P], F32, sc_att)
        att = sb("att", [P, NCH, 2, HB + 2], F32, sc_att)
        q_own, own_q = (sb(n, [P, NSEQ + 1, 2, TS], F32, sc_att) for n in ("q_own", "own_q_sb"))
        prob_s, prob_st = sb("prob_s", [2 * TS, PAST + TS], F32, sc_att), sb("prob_st", [P, 3, 2 * TS], F32, sc_att)
        att_st, att_s = sb("att_st", [P, 2 * TS], F32, sc_att), sb("att_s", [2 * TS, HB + 2], F32, sc_att)
        sc_att.close()
        KV_DMAS, ATT_DMAS = (1, 4, 2), (1, 4, 1)

        def block_of(x, g, n):
            if g == 0:
                return x[:, P * n:P * n + P]
            if g == 1:
                return x[:, n // 2 + 512 * (n % 2):n // 2 + 512 * (n % 2) + 509:4]
            return x[:, n:n + 8 * P - 7:8]

        def keys_of(x, g, n):
            if g == 0:
                return x[:, P * (n - 1):P * (n + 1)]
            return x[:, n // 2:n // 2 + 1021:4]

        def is_wide(g, n):
            return n > 0 if g == 0 else n % 2 == 1 if g == 1 else False

        def ncache(g):
            return min(WIN[g], PAST)

        def before(table, g, i):
            return 16 * (2 * sum(table[:g]) + table[g] * i)

        NFILL, FILL0, SENT0 = (4, 2, 2), (N_ATT, N_ATT + 8, N_ATT + 12), (6 * NH, 6 * NH + 12, 6 * NH + 18)

        def parts_done(g, n):
            return min(24 * NFILL[g], (24, 8)[g > 0] + (5, 3)[g > 0] * n)

        def filled(act, g, i, n):
            for c in range(parts_done(g, n - 1) // KD if n else 0, (parts_done(g, n) if n < 15 else 24 * NFILL[g]) // KD):
                n0, per = FILL0[g], NFILL[g]
                before = SENT0[g] + 3 * per // 2 * i
                if g == 0:
                    fill_pair(act, n0, n0 + per * i, NH + i, c, before)
                else:
                    x, t = c // NG, c % NG
                    dst = gb_d[bass.ds(4 * (g - 1) + 2 * i + x, 1)].rearrange("o p t -> (o p) t")
                    fill_out(act, n0 + x, n0 + x + per * i, t, c % 2, before + c // 2, ACT.Sigmoid, dst)
                if c % NG == NG - 1:
                    j = c // NG + 2
                    split_hi(act, n0 + j, n0 + j + per * i, (n0 + j) // 2 + per // 2 * i + 1)

        def att_sync(sp, g, i, first=False):
            it = 2 * g + i
            for x in range(NFILL[g]):
                if first and x == 2:
                    between_sync(sp)
                load_cols(sp, FILL0[g] + x, FILL0[g] + x + NFILL[g] * i, w_in, pair_cols(NH + i, x) if g == 0 else C_GB + (4 * (g - 1) + 2 * i + x) * P)
            sp.wait_ge(sem("mins"), NCH * it + 1)
            sp.dma_start(bias_p[:], a["bias_p"][g][bass.ds(i, 1)].rearrange("o p e k -> p (o e) k")).then_inc(sem("bias_in"), 16)
            sp.wait_ge(sem("min_s"), it + 1)
            sp.dma_start(bias_s[:], a["bias_s"][g][bass.ds(i, 1)].rearrange("o p k -> (o p) k")).then_inc(sem("bias_in"), 16)
            sp.wait_ge(sem("pv_s"), it + 1)
            apart(sp)
            for n in range(ncache(g) // P):
                for s in range(2):
                    src = a[f"cache_win{g}"][0, :, P * n:P * n + P, s].rearrange("b p h d -> p b (h d)")[:, :, bass.ds(i * P, P)]
                    sp.dma_start(cache[:, :, n, s], src).then_inc(sem("cache_in"), 16)
            sp.wait_ge(sem("aq_set"), 4 * it + 4)
            apart(sp)
            if g == 1:
                for s in range(2):
                    sp.wait_ge(sem(f"stored{s}"), 16 * SENT0[1] + 1)
            nxt = it + 1 if g < 2 else 5 - i
            sp.dma_start(raw[:], qkv_d[bass.ds(nxt, 1)].rearrange("o x p t -> p (o x) t")).then_inc(sem("raw_in"), 16)

        def att_pool(pool, g, i):
            it = 2 * g + i
            pool.wait_ge(sem("aq_set"), 4 * it + 4)
            pool.wait_ge(sem("s_smp"), it + 1)
            pool.wait_ge(sem("own_in"), 32)
            G.tensor_tensor(q_own[:], aq[:, 0:2, TP:T].rearrange("p (o e) t -> p o e t", o=1).to_broadcast([P, NSEQ + 1, 2, TS]), own_q[:], ALU.mult).then_inc(sem("q_own"), 1)
            for j in range(NFILL[g]):
                split_lo(pool, FILL0[g] + j, FILL0[g] + j + 2 + NFILL[g] * i)

        def att_scalar(act, g, i):
            it = 2 * g + i
            act.wait_ge(sem("raw_in"), 16 * it + 16)
            act.wait_ge(sem("s_smp"), it + 1)
            act.wait_ge(sem("q_own"), it + 1)
            for dst, src, scale in ((2, 1, 1.0), (3, 2, 1.0), (0, 0, q_scale[:, 0:1]), (1, 0, q_scale[:, 1:2])):
                A.activation(aq[:, dst], raw[:, src], ACT.Copy, scale=scale).then_inc(sem("aq_set"), 1)
            act.wait_ge(sem("kv_stored"), before(KV_DMAS, g, i) + 1)
            act.wait_ge(sem("kvs_stored"), 256 * it + 1)
            for n in range(NCH):
                act.wait_ge(sem("kv_done"), NCH * it + n + 1)
                A.activation(kvt[:, n], work[4][:, 0:2 * P].rearrange("p (s d) -> p s d", s=2), ACT.Copy).then_inc(sem("kv_read"), 1)
                act.wait_ge(sem("mins"), NCH * it + n + 2)
                w = 2 * P if is_wide(g, n) else P
                for e in range(2):
                    ins = A.activation(prob[:, n % 2, e, 0:w], prob[:, n % 2, e, 0:w], ACT.Exp, scale=-1.0, bias=att[:, n, e, HB + 1:HB + 2],
                                       accum_out=att[:, n, e, HB:HB + 1])
                ins.then_inc(sem("exps"), 1)
                filled(act, g, i, n)
            cols = bass.ds(i * P, P)
            win = a[f"win{g}_p"][0, 0].rearrange("t s h d -> t s (h d)")
            act.wait_ge(sem("kv_read"), NCH * it + NCH)
            if g == 0:
                act.dma_start(win[:, :, cols], kvt[:, NCH - 1]).then_inc(sem("kv_stored"), 16)
            elif g == 1:
                for r in range(4):
                    act.dma_start(win[r:r + 509:4, :, cols], kvt[:, 2 * r + 1]).then_inc(sem("kv_stored"), 16)
            else:
                for s in range(2):
                    act.dma_start(win.rearrange("(p n) s x -> p n s x", n=NCH)[:, :, s, cols], kvt[:, :, s]).then_inc(sem("kv_stored"), 16)
            act.wait_ge(sem("kvs_done"), it + 1)
            A.activation(kvs[:], work[4][0:TS, 0:2 * P].rearrange("p (s d) -> p s d", s=2), ACT.Copy).then_inc(sem("kvs_read"), 1)
            for c in range(2 * (ncache(g) // P)):
                act.wait_ge(sem("kct_done"), (0, 4, 12)[g] + 2 * (ncache(g) // P) * i + c + 1)
                A.activation(kct_part(g, c), work[c % 2][:].rearrange("p (b k) -> p b k", k=ncache(g)), ACT.Copy).then_inc(sem("kct_read"), 1)
            filled(act, g, i, 8)
            act.wait_ge(sem("kvs_read"), it + 1)
            nc_ = ncache(g) if g else WIN[0] - TSEQ
            for s in range(2):
                for b in range(NSEQ):
                    dst = a[f"win{g}_s"][0, b].rearrange("t s h d -> t s (h d)")[nc_:nc_ + TSEQ, s, cols]
                    act.dma_start(dst, kvs[TSEQ * b:TSEQ * b + TSEQ, s]).then_inc(sem("kvs_stored"), 16)
            act.wait_ge(sem("o_read_t"), NCH * it + NCH)
            heads = bass.ds(2 * i, 2)
            out = att_d[g, 0:TP, heads]
            if g == 0:
                act.dma_start(out.rearrange("(n p) h x -> p n h x", p=P), att[:]).then_inc(sem("att_stored"), 16)
            elif g == 1:
                for r in range(4):
                    act.dma_start(out.rearrange("(b p r) h x -> r p b h x", b=2, r=4)[r], att[:, 2 * r:2 * r + 2]).then_inc(sem("att_stored"), 16)
            else:
                act.dma_start(out.rearrange("(p n) h x -> p n h x", n=NCH), att[:]).then_inc(sem("att_stored"), 16)
            act.wait_ge(sem("min_s"), it + 2)
            w = ncache(g) + TS
            A.activation(prob_s[:, 0:w], prob_s[:, 0:w], ACT.Exp, scale=-1.0, bias=att_s[:, HB + 1:HB + 2], accum_out=att_s[:, HB:HB + 1]).then_inc(sem("exp_s"), 1)
            for n in range(9, 16):
                filled(act, g, i, n)
            act.wait_ge(sem("att_s_done"), it + 1)
            for e in range(2):
                act.dma_start(att_d[g, TP:T, bass.ds(2 * i + e, 1)].rearrange("t o x -> t (o x)"), att_s[TS * e:TS * e + TS]).then_inc(sem("att_s_stored"), 16)

        def kct_part(g, c):
            m = 512 // ncache(g)
            return kct[:, m * c:m * c + m, 0:ncache(g)]

        def att_vector(dve, g, i):
            it = 2 * g + i
            dve.wait_ge(sem("bias_in"), 32 * it + 32)
            dve.wait_ge(sem("att_stored"), before(ATT_DMAS, g, i) + 1)
            dve.wait_ge(sem("att_s_stored"), 32 * it + 1)
            for n in range(NCH + 1):
                if n >= 1:
                    w = is_wide(g, n - 1) + 1
                    dve.wait_ge(sem("pt_done"), NCH * it + n)
                    V.tensor_copy(prob_t[:, n % 2, :, 0:w], work[2][:].rearrange("p (e k q) -> p e k q", e=2, k=2)[:, :, 0:w]).then_inc(sem("pt_read"), 1)
                if n < NCH:
                    dve.wait_ge(sem("scores"), NCH * it + n + 1)
                    apart(dve)
                    w = 2 * P if is_wide(g, n) else P
                    for e in range(2):
                        ins = V.tensor_tensor_reduce(prob[:, n % 2, e, 0:w], work[n % 2][:, 2 * P * e:2 * P * e + w], bias_p[:, e, 2 * P - w:2 * P],
                                                     1.0, 3e38, ALU.add, ALU.min, att[:, n, e, HB + 1:HB + 2])
                    ins.then_inc(sem("mins"), 1)
                if n >= 1:
                    dve.wait_ge(sem("pv_done"), NCH * it + n)
                    V.tensor_copy(att[:, n - 1, :, 0:HB], work[3][:, 0:2 * HB].rearrange("p (e d) -> p e d", e=2)).then_inc(sem("o_read_t"), 1)
            dve.wait_ge(sem("s_smp"), it + 2)
            apart(dve)
            w = ncache(g) + TS
            V.tensor_tensor_reduce(prob_s[:, 0:w], work[2][0:2 * TS, 0:w], bias_s[:, 0:w], 1.0, 3e38, ALU.add, ALU.min,
                                   att_s[:, HB + 1:HB + 2]).then_inc(sem("min_s"), 1)
            dve.wait_ge(sem("pt_s"), it + 1)
            for n in range(ncache(g) // P):
                V.tensor_copy(prob_st[:, n], work[3][:, 64 * n:64 * n + 64])
            V.tensor_copy(prob_st[0:TS, 2], work[3][0:TS, 128:192]).then_inc(sem("pt_s_read"), 1)
            dve.wait_ge(sem("pv_s"), it + 2)
            V.tensor_copy(att_st[:], work[4][:, 0:2 * TS]).then_inc(sem("st_read"), 1)
            dve.wait_ge(sem("st_turned"), it + 1)
            for e in range(2):
                ins = V.tensor_copy(att_s[TS * e:TS * e + TS, 0:HB], work[2][TS * e:TS * e + TS, HB * e:HB * e + HB])
            ins.then_inc(sem("att_s_done"), 1)

        def att_tensor(pe, g, i):
            it = 2 * g + i
            def fill_parts(n):
                for p in range(parts_done(g, n - 1) if n else 0, parts_done(g, n) if n < 15 else 24 * NFILL[g]):
                    part(pe, FILL0[g] + p // 24, FILL0[g] + p // 24 + NFILL[g] * i, p % 24)
            fill_parts(0)
            pe.wait_ge(sem("aq_set"), 4 * it + 2)
            for n in range(NCH + 1):
                if n < NCH:
                    if n >= 1:
                        pe.wait_ge(sem("kv_read"), NCH * it + n)
                    for s in range(2):
                        ins = PE.transpose(work[4][:, P * s:P * s + P], block_of(aq[:, 2 + s], g, n), ident[:, :])
                    ins.then_inc(sem("kv_done"), 1)
                if n >= 1:
                    m = n - 1
                    pe.wait_ge(sem("exps"), NCH * it + m + 1)
                    for e in range(2):
                        for kb in range(is_wide(g, m) + 1):
                            ins = PE.transpose(work[2][:, 2 * P * e + P * kb:2 * P * e + P * kb + P], prob[:, m % 2, e, P * kb:P * kb + P], ident[:, :])
                    ins.then_inc(sem("pt_done"), 1)
                if n < NCH:
                    if n == 0:
                        pe.wait_ge(sem("aq_set"), 4 * it + 4)
                    w = 2 * P if is_wide(g, n) else P
                    for e in range(2):
                        k = keys_of(aq[:, 2], g, n) if is_wide(g, n) else block_of(aq[:, 2], g, n)
                        ins = PE.matmul(work[n % 2][:, 2 * P * e:2 * P * e + w], block_of(aq[:, e], g, n), k, start=True, stop=True)
                    ins.then_inc(sem("scores"), 1)
                if n < NCH:
                    fill_parts(n + 1)
                if n >= 1:
                    pe.wait_ge(sem("pt_read"), NCH * it + m + 1)
                    pe.wait_ge(sem("kv_read"), NCH * it + m + 1)
                    if m >= 1:
                        pe.wait_ge(sem("o_read_t"), NCH * it + m)
                    nk = is_wide(g, m) + 1
                    for e in range(2):
                        for kb in range(nk):
                            ins = PE.matmul(work[3][:, HB * e:HB * e + HB], prob_t[:, n % 2, e, kb], kvt[:, m + kb - nk + 1, 1, HB * e:HB * e + HB],
                                            start=(kb == 0), stop=(kb == nk - 1))
                    ins.then_inc(sem("pv_done"), 1)
            for s in range(2):
                ins = PE.transpose(work[4][0:TS, P * s:P * s + P], aq[:, 2 + s, TP:T], ident[:, :])
            ins.then_inc(sem("kvs_done"), 1)
            nt = ncache(g) // P
            pe.wait_ge(sem("cache_in"), (0, 64, 192)[g] + 32 * nt * (i + 1))
            for c in range(2 * nt):
                if c >= 2:
                    pe.wait_ge(sem("kct_read"), (0, 4, 12)[g] + 2 * nt * i + c - 1)
                for q in range(4):
                    b, n = (4 * c + q) // nt, (4 * c + q) % nt
                    ins = PE.transpose(work[c % 2][:, P * q:P * q + P], cache[:, b, n, 0], ident[:, :])
                ins.then_inc(sem("kct_done"), 1)
            fill_parts(9)
            pe.wait_ge(sem("kct_read"), (0, 4, 12)[g] + 2 * nt * (i + 1))
            pe.wait_ge(sem("q_own"), it + 2)
            w = ncache(g)
            for b in range(NSEQ):
                PE.matmul(work[2][0:2 * TS, 0:w], q_own[:, b], kct[:, b, 0:w], start=(b == 0), stop=(b == NSEQ - 1))
            PE.matmul(work[2][0:2 * TS, w:w + TS], q_own[:, NSEQ], aq[:, 2, TP:T], start=True, stop=True).then_inc(sem("s_smp"), 1)
            for n in range(10, 12):
                fill_parts(n)
            pe.wait_ge(sem("exp_s"), it + 1)
            apart(pe)
            for n in range(nt):
                PE.transpose(work[3][:, 64 * n:64 * n + 64], prob_s[:, P * n:P * n + P], ident[0:2 * TS, 0:2 * TS])
            PE.transpose(work[3][0:TS, 128:192], prob_s[:, w:w + TS], ident[0:2 * TS, 0:2 * TS]).then_inc(sem("pt_s"), 1)
            for n in range(12, 14):
                fill_parts(n)
            pe.wait_ge(sem("pt_s_read"), it + 1)
            pe.wait_ge(sem("kvs_read"), it + 1)
            for b in range(NSEQ):
                def of_seq(x):
                    return x.rearrange("p (e b q) -> p e b q", e=2, q=TSEQ)[:, :, b]
                o = of_seq(work[4][:, 0:2 * TS])
                PE.matmul(o, kvs[:, 1], of_seq(prob_st[0:TS, 2]), start=True, stop=False)
                for n in range(nt):
                    ins = PE.matmul(o, cache[:, b, n, 1], of_seq(prob_st[:, n]), start=False, stop=(n == nt - 1))
            ins.then_inc(sem("pv_s"), 1)
            for n in range(14, 16):
                fill_parts(n)
            pe.wait_ge(sem("st_read"), it + 1)
            apart(pe)
            PE.transpose(work[2][0:2 * TS, 0:P], att_st[:], ident[:, :]).then_inc(sem("st_turned"), 1)


        def between_sync(sp):
            head_stored(sp)
            sp.dma_start(q_scale[:], a["q_scale"]).then_inc(sem("own_in"), 16)
            sp.dma_start(own_q[:], a["own_q"]).then_inc(sem("own_in"), 16)
            sp.dma_start(raw[:], qkv_d[0].rearrange("x p t -> p x t")).then_inc(sem("raw_in"), 16)

        def between_pool(pool):
            pass

        def between_scalar(act):
            act.wait_ge(sem("oa_ready"), NH)
            act.wait_ge(sem("own_in"), 32)

        def between_vector(dve):
            pass

        def between_tensor(pe):
            pass

        def att_end(sp):
            sp.wait_ge(sem("kv_stored"), 16 * 2 * sum(KV_DMAS) + 1)
            sp.wait_ge(sem("kvs_stored"), 256 * 6 + 1)
            sp.wait_ge(sem("att_stored"), 16 * 2 * sum(ATT_DMAS) + 1)
            sp.wait_ge(sem("att_s_stored"), 32 * 6 + 1)
            sp.wait_ge(sem("raw_in"), 16 * 7)

        sc_e = ExitStack()
        ones_all = sb("ones_all", [P, P], F32, sc_e)
        x1 = sb("x1", [P, KD, T], F32, sc_e)
        sc_c = ExitStack()
        oaH, oaL = sb("oaH", [P, NH, T], F32R, sc_c), sb("oaL", [P, NH, T], F32R, sc_c)
        obH, obL = sb("obH", [P, 2, T], F32R, sc_c), sb("obL", [P, 2, T], F32R, sc_c)
        gates = sb("gates", [P, 2, 2, T], F32, sc_c)
        summed = sb("summed", [P, NG, 2, TN], F32, sc_c)
        prod, ob_tok = sb("prod", [P, 3, NHB, HB], F32, sc_c), sb("ob_tok", [P, 2, NHB * HB], F32, sc_c)
        low, share = sb("low", [P, NT9, NHB], F32, sc_c), sb("share", [P, NT9, 3, NHB], F32, sc_c)
        part_den = sb("part_den", [P, NT9, 3, NHB], F32, sc_c)
        sc_c.close()
        st = x1[:].rearrange("p k t -> p (k t)")[:, 0:NT9 * 3 * NHB * (HB + 2)].rearrange(
            "p (t g h x) -> p t g h x", t=NT9, g=3, h=NHB)
        oa_in = gates[:].rearrange("p a b t -> p (a b) t")
        ga_last = summed[:].rearrange("p g a t -> p (g a t)").rearrange("p (s t) -> p s t", s=2)
        sc_m = ExitStack()
        xcol = sb("xcol", [P, 2, NT9, P], F32, sc_m)
        sq_in, sq_sum = sb("sq_in", [P, T], F32, sc_m), sb("sq_sum", [P, T], F32, sc_m)
        rms, h2 = sb("rms", [P, NG, TN], F32, sc_m), sb("h2", [P, 2, TN], F32, sc_m)
        sc_m.close()
        sc_u = ExitStack()
        uH, uL = sb("uH", [P, KD, T], F32R, sc_u), sb("uL", [P, KD, T], F32R, sc_u)
        uf, relu = sb("uf", [P, NG, TN], F32, sc_u), sb("relu", [P, NG, TN], F32, sc_u)
        sc_u.close()
        sc_y = ExitStack()
        y, fnorm = sb("y", [P, 2, D], F32, sc_y), sb("fnorm", [P, D], F32, sc_y)
        junk_y = sb("junk_y", [P, D // 2], F32, sc_y)
        ssy, ry = sb("ssy", [P, NT9, 2], F32, sc_y), sb("ry", [P, NT9], F32, sc_y)
        sc_y.close()
        sc_e.close()

        def end_sync(sp):
            for j in range(2):
                load_cols(sp, N_GA + j, N_GA + j, w_in, C_GA + (6 + j) * P)
            att_end(sp)
            sp.wait_ge(sem("zeroed"), 8)
            sp.dma_start(oa_in, oa_d.rearrange("k p t -> p k t")).then_inc(sem("oa_loaded"), 16)
            for g in range(3):
                sp.dma_start(st[:, 0:NCH, g], att_d[g, 0:TP].rearrange("(t p) h x -> p t h x", p=P)).then_inc(sem("st_loaded"), 16)
            sp.dma_start(st[0:TS, NCH], att_d[:, TP:T].rearrange("g t h x -> t g h x")).then_inc(sem("st_loaded"), 16)

            def branch_w(i, j):
                load_w(sp, N_BR + j, N_BR + j + 2 * i, lambda raw: [
                    (raw[:, 0:NH], a["w_br_a"][0].rearrange("(k p) n -> p k n", p=P)[:, :, bass.ds((2 * i + j) * P, P)]),
                    (raw[:, NH:NH + 2], a["w_br_b"][0].rearrange("(k p) n -> p k n", p=P)[:, :, bass.ds((2 * i + j) * P, P)])])

            def branch_gates(i, j):
                b = 2 * i + j
                sp.wait_ge(sem("summed"), 3 * b + 3)
                for x, src in enumerate((ga_d, gb_d)):
                    sp.dma_start(gates[:, j, x], src[bass.ds(b, 1)].rearrange("o p t -> (o p) t")).then_inc(sem(f"gates_in{j}"), 16)
            for j in range(2):
                branch_w(0, j)
            for j in range(2):
                sp.wait_ge(sem("ga_last"), 3 * j + 3)
                sp.dma_start(ga_d[6 + j], ga_last[:, j]).then_inc(sem("gate_stored"), 16)
            sp.wait_ge(sem("gate_stored"), 32 + 1)
            for s in range(2):
                sp.wait_ge(sem(f"stored{s}"), 16 * 48 + 1)
            sp.wait_ge(sem("oa_split"), 1)
            with sp.Fori(0, KD // 2 - 1) as i:
                for j in range(2):
                    branch_gates(i, j)
                    branch_w(i + 1, j)
            for j in range(2):
                branch_gates(KD // 2 - 1, j)
            w_out = a["w_out"][0].rearrange("(k p) n -> p k n", p=P)
            with sp.Fori(0, KD // 2) as i:
                for j in range(2):
                    n0, o = N_OUT + j, 2 * i + j
                    load_cols(sp, n0, n0 + 2 * i, w_out, o * P)
                    sp.wait_ge(sem("summed"), 3 * KD + 6)
                    sp.wait_ge(sem("x1_made"), 3 * o + 3)
                    sp.dma_start(xcol[:, j, 0:NCH], a["x_prompt"][0].rearrange("(t p) d -> p t d", p=P)[:, :, bass.ds(o * P, P)]).then_inc(sem(f"gates_in{j}"), 16)
                    sp.dma_start(xcol[0:TS, j, NCH], a["x_sample"].rearrange("b t d -> (b t) d")[:, bass.ds(o * P, P)]).then_inc(sem(f"gates_in{j}"), 16)
            w_up, w_down = (a[n][0].rearrange("(k p) n -> p k n", p=P) for n in ("w_up", "w_down"))
            with sp.Fori(0, 4) as q:
                for m in range(8):
                    load_cols(sp, N_MLP + m, N_MLP + m + 16 * q, w_up, q * D + m * P)
                for m in range(8):
                    load_w(sp, N_MLP + 8 + m, N_MLP + 8 + m + 16 * q, lambda raw: [
                        (raw, w_down[:, bass.ds(q * KD, KD), m * P:m * P + P])])
            done(sp, N_MLP + 63, 2)
            sp.dma_start(fnorm[:], a["final_norm"].rearrange("(o d) -> o d", o=1).to_broadcast([P, D])).then_inc(sem("st_loaded"), 16)
            for t, (c, n) in enumerate(tokens):
                sp.wait_ge(sem("y_made"), t + 1)
                dst = a["y_prompt"][0, c:c + n] if t < NCH else a["y_sample"].rearrange("b t d -> (b t) d")
                sp.dma_start(dst, y[0:n, t % 2]).then_inc(sem(f"stored{t % 2}"), 16)
            sp.wait_ge(sem("stored0"), 16 * (48 + 5) + 1)
            sp.wait_ge(sem("stored1"), 16 * (48 + 4) + 1)

        def end_pool(pool):
            pool.sem_inc(sem("summed"), 6)
            pool.sem_inc(sem("x1_made"), 6)
            pool.sem_inc(sem("u_lo"), 3)
            att_end(pool)
            G.memset(ones_all[:], 1.0).then_inc(sem("zeroed"), 1)
            G.memset(st[:, NCH], 1.0).then_inc(sem("zeroed"), 1)
            pool.wait_ge(sem("oa_hi"), 1)
            G.tensor_tensor(oaL[:], oa_in, oaH[:].bitcast(F32), ALU.subtract).then_inc(sem("oa_split"), 1)
            for j in range(2):
                split_lo(pool, N_BR + j, N_BR + j, 6)
            with pool.Fori(0, KD // 2) as i:
                for j in range(2):
                    n0, b = N_BR + j, 2 * i + j
                    for t in range(NG):
                        pool.wait_ge(sem("h_hi"), 3 * b + t + 19)
                        cols = slice(TN * t, TN * t + TN)
                        G.tensor_tensor(hL[:, bass.ds(b, 1), cols], summed[:, t:t + 1, 0], hH[:, bass.ds(b, 1), cols].bitcast(F32), ALU.subtract).then_inc(sem("h_lo"), 1)
                    split_lo(pool, n0, n0 + 2 + 2 * i)
            with pool.Fori(0, KD // 2) as i:
                for j in range(2):
                    n0, o = N_OUT + j, 2 * i + j
                    split_lo(pool, n0, n0 + 2 + 2 * i)
                    pool.wait_ge(sem("x1_squared"), o + 2)
                    G.tensor_tensor(sq_sum[:], sq_sum[:], sq_in[:], ALU.add).then_inc(sem("sq_added"), 1)
                    pool.wait_ge(sem("sq_added"), o + 2)
            for t in range(NG):
                for m in range(KD):
                    pool.wait_ge(sem("h_hi"), KD * t + m + 43)
                    G.tensor_tensor(hL[:, m, TN * t:TN * t + TN], h2[:, m % 2], hH[:, m, TN * t:TN * t + TN].bitcast(F32), ALU.subtract).then_inc(sem("h_lo"), 1)

            def group(q, last):
                n0 = N_MLP
                for m in range(8):
                    for t in range(NG):
                        k = 24 * q + 3 * m + t
                        pool.wait_ge(sem("u_hi"), k + 1)
                        pool.wait_ge(sem("u_made"), k + 1)
                        cols = slice(TN * t, TN * t + TN)
                        G.tensor_tensor(uL[:, m, cols], uf[:, t], uH[:, m, cols].bitcast(F32), ALU.subtract).then_inc(sem("u_lo"), 1)
                    split_lo(pool, n0 + m, n0 + m + 2 + 16 * q)
                for m in range(8):
                    if not (last and m >= 6):
                        split_lo(pool, n0 + m, n0 + 10 + m + 16 * q)
            with pool.Fori(0, 3) as q:
                group(q, False)
            group(3, True)

        def end_scalar(act):
            act.wait_ge(sem("oa_loaded"), 16)
            A.activation(oaH[:], oa_in, ACT.Copy).then_inc(sem("oa_hi"), 1)
            for j in range(2):
                for t in range(NG):
                    done(act, N_GA + j, t)
                    A.activation(ga_last[:, j, TN * t:TN * t + TN], dense[t][:, 0:TN], ACT.Sigmoid).then_inc(sem(f"d_free{t}"), 1)
                for t in range(NG):
                    act.wait_ge(sem(f"d_free{t}"), N_GA + j + 1)
                    act.sem_inc(sem("ga_last"), 1)
                split_hi(act, N_BR + j, N_BR + j, 27 + j, 6)
            act.wait_ge(sem("share_arg"), 1)
            A.activation(share[:], share[:], ACT.Exp).then_inc(sem("share_exp"), 1)
            for t, (c, n) in enumerate(tokens):
                act.wait_ge(sem("ob_turned"), t + 1)
                A.activation(obH[:, :, c:c + n], work[t % 2][:, 0:2 * P].rearrange("p (k t) -> p k t", k=2)[:, :, 0:n], ACT.Copy).then_inc(sem("ob_hi"), 1)

            def branch(i, last):
                for j in range(2):
                    b = 2 * i + j
                    for t in range(NG):
                        act.wait_ge(sem("summed"), 3 * b + t + 7)
                        A.activation(hH[:, bass.ds(b, 1), TN * t:TN * t + TN], summed[:, t:t + 1, 0], ACT.Copy).then_inc(sem("h_hi"), 1)
                    if last:
                        split_hi(act, N_OUT + j, N_OUT + j, 34 + j)
                    else:
                        split_hi(act, N_BR + j, N_BR + j + 2 + 2 * i, 29 + j + 2 * i, 6)
            with act.Fori(0, KD // 2 - 1) as i:
                branch(i, False)
            branch(KD // 2 - 1, True)
            with act.Fori(0, KD // 2) as i:
                for j in range(2):
                    n0, o = N_OUT + j, 2 * i + j
                    for t in range(NG):
                        done(act, n0 + 2 * i, t)
                        A.activation(x1[:, bass.ds(o, 1), TN * t:TN * t + TN], dense[t][:, 0:TN].rearrange("p (o t) -> p o t", o=1), ACT.Copy).then_inc(sem(f"d_free{t}"), 1)
                    split_hi(act, n0, n0 + 2 + 2 * i, (n0 + 2) // 2 + 5 + i)
                    act.wait_ge(sem("x1_made"), 3 * o + 9)
                    act.wait_ge(sem("sq_added"), o + 1)
                    apart(act)
                    A.activation(sq_in[:], x1[:, bass.ds(o, 1)].rearrange("p o t -> p (o t)"), ACT.Square).then_inc(sem("x1_squared"), 1)
            for t in range(NG):
                act.wait_ge(sem("mean"), NT9 + 2 * NH + t + 1)
                A.activation(rms[:, t], rms[:, t], ACT.Sqrt).then_inc(sem("root"), 1)
            for t in range(NG):
                for m in range(KD):
                    act.wait_ge(sem("h2_made"), KD * t + m + 1)
                    A.activation(hH[:, m, TN * t:TN * t + TN], h2[:, m % 2], ACT.Copy).then_inc(sem("h_hi"), 1)

            def group(q, last):
                n0 = N_MLP
                for m in range(8):
                    for t in range(NG + 1):
                        if t < NG:
                            done(act, n0 + m + 16 * q, t)
                            act.wait_ge(sem("u_lo"), 24 * q + 3 * m + t + 1)
                            A.activation(relu[:, t], dense[t][:, 0:TN], ACT.Relu).then_inc(sem(f"d_free{t}"), 1)
                        if t >= 1:
                            act.wait_ge(sem(f"d_free{t - 1}"), n0 + m + 1 + 16 * q)
                            done(act, n0 - 1 + 16 * q, t - 1)
                            A.activation(uH[:, m, TN * (t - 1):TN * t], relu[:, t - 1], ACT.Square).then_inc(sem("u_hi"), 1)
                    split_hi(act, n0 + m, n0 + m + 2 + 16 * q, (n0 + m + 2) // 2 + 5 + 8 * q)
                for m in range(8):
                    if not (last and m >= 6):
                        split_hi(act, n0 + m, n0 + 10 + m + 16 * q, (n0 + m + 10) // 2 + 5 + 8 * q)
            with act.Fori(0, 3) as q:
                group(q, False)
            group(3, True)

            def square(t):
                c, n = tokens[t]
                for x in range(2):
                    act.wait_ge(sem("turned"), 2 * (NT9 + t) + x + 1)
                    chA.link(act, A.activation(junk_y[0:n], work[2 * (t % 2) + x][0:n, :], ACT.Square, accum_out=ssy[0:n, t, x:x + 1]))
                act.sem_inc(sem("squares"), 1)
            done(act, N_MLP + 63, 2)
            square(0)
            for t, (c, n) in enumerate(tokens):
                act.wait_ge(sem("mean"), NT9 + 2 * NH + NG + t + 1)
                A.activation(ry[0:n, t:t + 1], ry[0:n, t:t + 1], ACT.Sqrt).then_inc(sem("root"), 1)
                if t < NCH:
                    square(t + 1)

        def end_vector(dve):
            dve.wait_ge(sem("st_loaded"), 64)
            chV.link(dve, V.tensor_tensor(low[:], st[:, :, 0, :, HB + 1], st[:, :, 1, :, HB + 1], ALU.min))
            chV.link(dve, V.tensor_tensor(low[:], low[:], st[:, :, 2, :, HB + 1], ALU.min))
            for g in range(3):
                ins = V.tensor_tensor(share[:, :, g], low[:], st[:, :, g, :, HB + 1], ALU.subtract)
            ins.then_inc(sem("share_arg"), 1)
            dve.wait_ge(sem("share_exp"), 1)
            for g in range(3):
                ins = V.tensor_tensor(part_den[:, :, g], share[:, :, g], st[:, :, g, :, HB], ALU.mult)
            chV.link(dve, ins)
            chV.link(dve, V.tensor_tensor(low[:], part_den[:, :, 0], part_den[:, :, 1], ALU.add))
            chV.link(dve, V.tensor_tensor(low[:], low[:], part_den[:, :, 2], ALU.add))
            chV.link(dve, V.reciprocal(low[:], low[:]))
            for g in range(3):
                ins = V.tensor_tensor(share[:, :, g], share[:, :, g], low[:], ALU.mult)
            chV.link(dve, ins)
            for t in range(NT9 + 1):
                if t < NT9:
                    c, n = tokens[t]
                    for g in range(3):
                        w = share[0:n, t, g].rearrange("p (h o) -> p h o", o=1).to_broadcast([n, NHB, HB])
                        ins = V.tensor_tensor(prod[0:n, g], st[0:n, t, g, :, 0:HB], w, ALU.mult)
                    chV.link(dve, ins)
                    chV.link(dve, V.tensor_tensor(prod[0:n, 0], prod[0:n, 0], prod[0:n, 1], ALU.add))
                    if t >= 2:
                        dve.wait_ge(sem("ob_turned"), t - 1)
                    V.tensor_tensor(ob_tok[0:n, t % 2].rearrange("p (h d) -> p h d", h=NHB), prod[0:n, 0], prod[0:n, 2], ALU.add).then_inc(sem("ob_made"), 1)
                    dve.wait_ge(sem("ob_made"), t + 1)
                if t >= 1:
                    c, n = tokens[t - 1]
                    dve.wait_ge(sem("ob_hi"), t)
                    V.tensor_tensor(obL[:, :, c:c + n], work[(t - 1) % 2][:, 0:2 * P].rearrange("p (k t) -> p k t", k=2)[:, :, 0:n],
                                    obH[:, :, c:c + n].bitcast(F32), ALU.subtract).then_inc(sem("ob_split"), 1)
            dve.wait_ge(sem("gate_stored"), 32 + 1)
            with dve.Fori(0, KD // 2) as i:
                for j in range(2):
                    n0, b = N_BR + j, 2 * i + j
                    dve.wait_ge(sem(f"gates_in{j}"), 32 * i + 32)
                    for t in range(NG):
                        cols = slice(TN * t, TN * t + TN)
                        done(dve, n0 + 2 * i, t)
                        if j:
                            dve.wait_ge(sem("h_lo"), 3 * b + t + 16)
                        V.tensor_tensor(summed[:, t, 0], dense[t][:, 0:TN], gates[:, j, 0, cols], ALU.mult)
                        V.tensor_tensor(summed[:, t, 1], work[t][:, 0:TN], gates[:, j, 1, cols], ALU.mult).then_inc(sem(f"d_free{t}"), 1)
                        dve.wait_ge(sem(f"d_free{t}"), n0 + 1 + 2 * i)
                        V.tensor_tensor(summed[:, t, 0], summed[:, t, 0], summed[:, t, 1], ALU.add).then_inc(sem("summed"), 1)
                        dve.wait_ge(sem("summed"), 3 * b + t + 7)
                dve.wait_ge(sem("h_lo"), 6 * i + 24)
            V.memset(sq_sum[:], 0.0).then_inc(sem("x1_squared"), 1)
            cuts = ((0, 384), (384, 384), (768, 288))
            with dve.Fori(0, KD // 2) as i:
                for j in range(2):
                    n0, o = N_OUT + j, 2 * i + j
                    for t in range(NG):
                        dve.wait_ge(sem(f"d_free{t}"), n0 + 1 + 2 * i)
                    for t, (c, n) in enumerate(cuts):
                        dve.wait_ge(sem("x_cols"), 3 * o + t + 1)
                        x = x1[:, bass.ds(o, 1), c:c + n]
                        V.tensor_tensor(x, x, work[t][:, 0:n].rearrange("p (o t) -> p o t", o=1), ALU.add).then_inc(sem("x1_made"), 1)
            for t in range(NG):
                dve.wait_ge(sem("sq_total"), t + 1)
                V.tensor_scalar(rms[:, t], work[t][:, 0:TN], 1.0 / D, EPS, ALU.mult, ALU.add).then_inc(sem("mean"), 1)
            for t in range(NG):
                dve.wait_ge(sem("root"), NT9 + 2 * NH + t + 1)
                chV.link(dve, V.reciprocal(rms[:, t], rms[:, t]))
                for m in range(KD):
                    k = KD * t + m
                    if k >= 2:
                        dve.wait_ge(sem("h_lo"), k + 41)
                    V.scalar_tensor_tensor(out=h2[:, m % 2], in0=x1[:, m, TN * t:TN * t + TN], scalar=vec[:, NORM2 + m:NORM2 + m + 1], in1=rms[:, t],
                                           op0=ALU.mult, op1=ALU.mult).then_inc(sem("h2_made"), 1)
            with dve.Fori(0, 4) as q:
                for m in range(8):
                    for t in range(NG):
                        dve.wait_ge(sem(f"d_free{t}"), N_MLP + m + 1 + 16 * q)
                        V.tensor_tensor(uf[:, t], relu[:, t], relu[:, t], ALU.mult).then_inc(sem("u_made"), 1)
                for m in range(8):
                    for t in range(NG):
                        x = x1[:, m, TN * t:TN * t + TN]
                        done(dve, N_MLP + 8 + m + 16 * q, t)
                        V.tensor_tensor(x, x, dense[t][:, 0:TN], ALU.add).then_inc(sem(f"d_free{t}"), 1)
            dve.wait_ge(sem("st_loaded"), 80)
            for t, (c, n) in enumerate(tokens):
                dve.wait_ge(sem("squares"), NT9 + t + 1)
                chV.link(dve, V.tensor_tensor(ry[0:n, t:t + 1], ssy[0:n, t, 0:1], ssy[0:n, t, 1:2], ALU.add))
                V.tensor_scalar(ry[0:n, t:t + 1], ry[0:n, t:t + 1], 1.0 / D, EPS, ALU.mult, ALU.add).then_inc(sem("mean"), 1)
                dve.wait_ge(sem("root"), NT9 + 2 * NH + NG + t + 1)
                chV.link(dve, V.reciprocal(ry[0:n, t:t + 1], ry[0:n, t:t + 1]))
                if t >= 2:
                    dve.wait_ge(sem(f"stored{t % 2}"), 16 * (48 + t // 2) + 1)
                for x in range(2):
                    half = slice(512 * x, 512 * x + 512)
                    ins = V.scalar_tensor_tensor(out=y[0:n, t % 2, half], in0=work[2 * (t % 2) + x][0:n, :], scalar=ry[0:n, t:t + 1], in1=fnorm[0:n, half],
                                                 op0=ALU.mult, op1=ALU.mult)
                ins.then_inc(sem("y_made"), 1)

        def end_tensor(pe):
            for j in range(2):
                for t in range(NG):
                    job(pe, N_GA + j, N_GA + j, t)
            for t, (c, n) in enumerate(tokens):
                pe.wait_ge(sem("ob_made"), t + 1)
                if t >= 2:
                    pe.wait_ge(sem("ob_split"), t - 1)
                for k in range(2):
                    ins = PE.transpose(work[t % 2][:, P * k:P * k + n], ob_tok[0:n, t % 2, P * k:P * k + P], ident[0:n, 0:n])
                ins.then_inc(sem("ob_turned"), 1)
            pe.wait_ge(sem("ob_split"), NT9)
            pe.wait_ge(sem("oa_split"), 1)
            with pe.Fori(0, KD // 2) as i:
                for j in range(2):
                    n0 = N_BR + j
                    pe.wait_ge(sem("w_split"), n0 + 3 + 2 * i)
                    for t in range(NG):
                        pe.wait_ge(sem(f"d_free{t}"), n0 + 2 * i)
                        product(n0, t, dense[t], oaH, oaL, 0, NH)
                        product(n0, t, work[t], obH, obL, NH, 2).then_inc(sem("d_done"), 1)
            pe.wait_ge(sem("h_lo"), 42)
            with pe.Fori(0, KD // 2) as i:
                for j in range(2):
                    n0, o = N_OUT + j, 2 * i + j
                    for t in range(NG):
                        job(pe, n0, n0 + 2 * i, t)
                    pe.wait_ge(sem(f"gates_in{j}"), 32 * i + 160)
                    pe.wait_ge(sem("x1_made"), 3 * o + 6)
                    for t, (c, n) in enumerate(tokens):
                        ins = PE.transpose(work[t // 3][:, P * (t % 3):P * (t % 3) + n], xcol[0:n, j, t], ident[0:n, 0:n])
                        if t % 3 == 2:
                            ins.then_inc(sem("x_cols"), 1)
            pe.wait_ge(sem("sq_added"), KD + 1)
            pe.wait_ge(sem("x1_made"), 3 * KD + 6)
            for t in range(NG):
                PE.matmul(work[t][:, 0:TN], ones_all[:, :], sq_sum[:, TN * t:TN * t + TN], start=True, stop=True).then_inc(sem("sq_total"), 1)
            for t in range(NG):
                pe.wait_ge(sem("h_lo"), KD * t + KD + 42)
                job(pe, N_MLP, N_MLP, t)
            def group(q, first):
                for m in range(first, 8):
                    for t in range(NG):
                        job(pe, N_MLP + m, N_MLP + m + 16 * q, t)
                for m in range(8):
                    for t in range(NG):
                        if m == 0:
                            pe.wait_ge(sem("u_lo"), 24 * q + 25 + t)
                        job(pe, N_MLP + 8 + m, N_MLP + 8 + m + 16 * q, t, uH, uL)
            group(0, 1)
            with pe.Fori(0, 3) as q:
                group(q + 1, 0)
            for t in range(NG):
                pe.wait_ge(sem(f"d_free{t}"), N_MLP + 64)
            for t, (c, n) in enumerate(tokens):
                if t >= 2:
                    pe.wait_ge(sem("y_made"), t - 1)
                for x in range(2):
                    for k in range(4):
                        ins = PE.transpose(work[2 * (t % 2) + x][0:n, P * k:P * k + P], x1[:, 4 * x + k, c:c + n], ident[:, :])
                    ins.then_inc(sem("turned"), 1)

        block = ctx.enter_context(nc.Block())

        @block.sync
        def _(sp):
            start_sync(sp)
            ab_sync(sp)
            with sp.Fori(0, NH) as h:
                head_sync(sp, h)
            att_sync(sp, 0, 0, first=True)
            att_sync(sp, 0, 1)
            for g in range(1, 3):
                with sp.Fori(0, 2) as i:
                    att_sync(sp, g, i)
            end_sync(sp)

        @block.gpsimd
        def _(pool):
            start_pool(pool)
            ab_pool(pool)
            chG.rounds(pool, "heads", NH, lambda h: head_pool(pool, h))
            for g in range(3):
                chG.rounds(pool, f"attention {g}", 2, lambda i: att_pool(pool, g, i))
            end_pool(pool)

        @block.scalar
        def _(act):
            start_scalar(act)
            ab_scalar(act)
            chA.rounds(act, "heads", NH, lambda h: head_scalar(act, h))
            between_scalar(act)
            for g in range(3):
                chA.rounds(act, f"attention {g}", 2, lambda i: att_scalar(act, g, i))
            end_scalar(act)

        @block.vector
        def _(dve):
            start_vector(dve)
            ab_vector(dve)
            chV.rounds(dve, "heads", NH, lambda h: head_vector(dve, h))
            for g in range(3):
                chV.rounds(dve, f"attention {g}", 2, lambda i: att_vector(dve, g, i))
            end_vector(dve)

        @block.tensor
        def _(pe):
            start_tensor(pe)
            ab_tensor(pe)
            with pe.Fori(0, NH) as h:
                head_tensor(pe, h)
            for g in range(3):
                with pe.Fori(0, 2) as i:
                    att_tensor(pe, g, i)
            end_tensor(pe)


def kernel(**inputs):
    import concourse.bacc as bacc
    from concourse.bass_utils import run_bass_kernel_spmd

    tables = constants()
    arrays = {f"in_{n}": np.ascontiguousarray(inputs[n]) for n in INPUTS}
    arrays |= {f"table_{n}": x for n, x in tables.items()}
    lengths = {}
    for _ in range(2):
        nc = bacc.Bacc("TRN2", target_bir_lowering=False, num_devices=1)
        a = {}
        for n in INPUTS:
            a[n] = nc.dram_tensor(f"in_{n}", arrays[f"in_{n}"].shape, F32, kind="ExternalInput").ap()
        for n, x in tables.items():
            a[n] = nc.dram_tensor(f"table_{n}", x.shape, F32, kind="ExternalInput").ap()
        for n, shape in OUTS:
            a[n] = nc.dram_tensor(f"out_{n}", shape, F32, kind="ExternalOutput").ap()
        build(nc, a, lengths)
    r = run_bass_kernel_spmd(nc, [arrays], core_ids=[0])
    return tuple(r.results[0][f"out_{n}"] for n, _ in OUTS)
```

```python
from contextlib import ExitStack

import numpy as np

import concourse.bass as bass
from concourse import mybir

F32, F32R = mybir.dt.float32, mybir.dt.float32r
ALU, ACT, AX = mybir.AluOpType, mybir.ActivationFunctionType, mybir.AxisListType

P = 128
D, DFF = 1024, 4096
TP, NSEQ, TSEQ = 1024, 8, 4
TS = NSEQ * TSEQ
T = TP + TS
NG, TN = 3, (TP + NSEQ * TSEQ) // 3
KD = D // P
NH, HD = 4, 128
WA = NH * HD
NCH = TP // P
NT9 = NCH + 1
PAST = 256
WIN, DIL = (128, 512, 2048), (1, 4, 16)
NHB, HB = 4, 64
WB = 3 * NHB * HB
C_AB = 4 * WA
C_QKV = C_AB + 2 * NH
C_GA = C_QKV + 3 * WB
C_GB = C_GA + D
EPS = 1e-6
BLK = 16
NBLK = P // BLK
BIG = 1e30


def slopes():
    return np.exp2(-8.0 * np.arange(1, 3 * NHB + 1, dtype=np.float32) / (3 * NHB)).reshape(3, NHB)


def constants():
    c = {"ident": np.eye(P, dtype=np.float32)}
    j, i = np.arange(P)[:, None], np.arange(P)[None, :]
    levels = [((i // (2 * s) == j // (2 * s)) & (i // s > j // s)) for s in (16, 32, 64)]
    c["masks"] = np.stack([i >= j, i > j] + levels, 1).astype(np.float32)
    js, is_ = np.arange(TS)[:, None], np.arange(TS)[None, :]
    same = js // TSEQ == is_ // TSEQ
    c["masks_s"] = np.stack([same & (is_ >= js), same & (is_ > js)], 1).astype(np.float32)
    own = (np.arange(NSEQ)[:, None] == np.arange(TS)[None, :] // TSEQ).astype(np.float32)
    c["own_row"] = np.broadcast_to(own, (P, NSEQ, TS)).copy()
    c["own_col"] = own.T.copy()
    c["q_scale"] = -HB ** -0.5 * (np.arange(P)[:, None] // HB == np.arange(2)[None, :]).astype(np.float32)
    own9 = np.concatenate([own, np.ones((1, TS), np.float32)])
    c["own_q"] = np.broadcast_to(own9[None, :, None, :], (P, NSEQ + 1, 2, TS)).copy()
    reset = np.ones(T, np.float32)
    reset[0:TP:P] = 0
    reset[TP::TSEQ] = 0
    c["reset"] = np.broadcast_to(reset, (8, T)).copy()
    c["unit"] = np.broadcast_to(np.eye(BLK, dtype=np.float32).reshape(1, BLK * BLK), (NCH * NBLK, BLK * BLK)).copy()
    q, k = np.arange(P)[:, None], np.arange(2 * P)[None, :] - P
    sl = slopes()
    bias = np.zeros((3, 2, P, 2, 2 * P), np.float32)
    for g in range(3):
        off = q - k
        ok = (off >= 0) & (off <= WIN[g] // DIL[g])
        dist = off * DIL[g]
        if g == 2:
            ok = (off >= 0) & (off % 2 == 0) & (k >= 0)
            dist = off * 8
        for h in range(NHB):
            bias[g, h // 2, :, h % 2] = np.where(ok, sl[g, h] * dist, BIG)
    c["bias_p"] = bias
    bs = np.zeros((3, 2, 2, TS, PAST + TS), np.float32)
    tok = np.arange(TS)[:, None]
    for g in range(3):
        ncache = min(WIN[g], PAST)
        pos = PAST - ncache + np.arange(ncache)[None, :]
        dist = PAST + tok % TSEQ - pos
        ok = (dist % DIL[g] == 0) & (dist <= WIN[g])
        dn = tok % TSEQ - np.arange(TS)[None, :] % TSEQ
        okn = (tok // TSEQ == np.arange(TS)[None, :] // TSEQ) & (dn >= 0) & (dn % DIL[g] == 0)
        for h in range(NHB):
            bs[g, h // 2, h % 2, :, 0:ncache] = np.where(ok, sl[g, h] * dist, BIG)
            bs[g, h // 2, h % 2, :, ncache:ncache + TS] = np.where(okn, sl[g, h] * dn, BIG)
    c["bias_s"] = bs.reshape(3, 2, 2 * TS, PAST + TS)
    return c


class Chain:

    def __init__(self, sem, lengths, name):
        self.sem, self.lengths, self.name, self.base, self.n = sem, lengths, name, 0, 0

    def link(self, eng, ins):
        self.n += 1
        ins.then_inc(self.sem, 1)
        eng.wait_ge(self.sem, self.base + self.n)

    def rounds(self, eng, name, times, body):
        key = f"{self.name} {name}"
        base, n = self.base, self.n
        with eng.Fori(0, times) as i:
            self.base, self.n = base + n + i * self.lengths.get(key, 0), 0
            body(i)
            per = self.n
        self.lengths[key] = per
        self.base, self.n = base, n + times * per


INPUTS = ["x_prompt", "x_sample", "cache_win0", "cache_win1", "cache_win2", "state_delta", "state_conv",
          "norm1", "w_in", "conv_w", "a_log", "dt_bias", "gnorm_a", "w_br_a", "w_br_b", "w_out", "norm2",
          "w_up", "w_down", "final_norm"]
OUTS = [("y_prompt", (1, TP, D)), ("y_sample", (NSEQ, TSEQ, D)),
        ("win0_p", (1, 1, 128, 2, NHB, HB)), ("win1_p", (1, 1, 512, 2, NHB, HB)), ("win2_p", (1, 1, TP, 2, NHB, HB)),
        ("delta_p", (1, 1, NH, HD, HD)), ("conv_p", (1, 1, 3, 3 * WA)),
        ("win0_s", (1, NSEQ, 128, 2, NHB, HB)), ("win1_s", (1, NSEQ, PAST + TSEQ, 2, NHB, HB)),
        ("win2_s", (1, NSEQ, PAST + TSEQ, 2, NHB, HB)),
        ("delta_s", (1, NSEQ, NH, HD, HD)), ("conv_s", (1, NSEQ, 3, 3 * WA))]

N_AB, N_HEAD, N_ATT, N_GA, N_BR, N_OUT, N_MLP = 0, 1, 33, 49, 51, 59, 67


def build(nc, a, lengths):
    ctx = ExitStack()
    with ctx:
        def sb(name, shape, dt=F32, scope=None):
            return (scope or ctx).enter_context(nc.sbuf_tensor(name, shape, dt))

        S = {}

        def sem(name):
            if name not in S:
                S[name] = ctx.enter_context(nc.semaphore(name))
            return S[name]

        def dram(name, shape):
            return nc.dram_tensor(name, shape, F32).ap()

        rows_d = dram("rows_scratch", [16, T])
        at_d, t_d = dram("at_scratch", [NCH, P + 1, P]), dram("t_scratch", [NCH, P + 1, P])
        oa_d = dram("oa_scratch", [NH, P, T])
        ga_d, gb_d = dram("ga_scratch", [KD, P, T]), dram("gb_scratch", [KD, P, T])
        qkv_d = dram("qkv_scratch", [6, 3, P, T])
        att_d = dram("att_scratch", [3, T, NHB, HB + 2])

        hH, hL = sb("hH", [P, KD, T], F32R), sb("hL", [P, KD, T], F32R)
        Wraw = sb("Wraw", [P, 2, KD, P])
        WH, WL = sb("WH", [P, 2, KD, P], F32R), sb("WL", [P, 2, KD, P], F32R)
        ident, ones = sb("ident_sb", [P, P]), sb("ones", [P, 1])
        vec, vec_rows = sb("vec", [P, 25]), sb("vec_rows", [25, P])
        fill = sb("fill", [P, 2, TN])
        ssx, rx = sb("ssx", [P, 16]), sb("rx", [P, 16])
        NORM1, NORM2, FNORM, GNORM = 0, 8, 16, 24

        dense = [ctx.enter_context(nc.psum_tensor(f"dense{t}", [P, 512], F32)) for t in range(NG)]
        work = [ctx.enter_context(nc.psum_tensor(f"work{t}", [P, 512], F32)) for t in range(5)]

        w_in = a["w_in"][0].rearrange("(k p) n -> p k n", p=P)
        tiles9 = [(TN * g + P * k, P if k < 2 else TN - 2 * P) for g in range(NG) for k in range(3)]
        chV, chA, chG = (Chain(sem(n), lengths, n) for n in ("own_vector", "own_scalar", "own_pool"))
        V, A, G, PE = nc.vector, nc.scalar, nc.gpsimd, nc.tensor

        def load_w(sp, n0, n, parts):
            s = n0 % 2
            sp.wait_ge(sem("w_split"), n + 1)
            for dst, src in parts(Wraw[:, s]):
                sp.dma_start(dst, src).then_inc(sem(f"w_loaded{s}"), 16)

        def load_cols(sp, n0, n, w, col):
            load_w(sp, n0, n, lambda raw: [(raw, w[:, :, bass.ds(col, P)])])

        def split_hi(act, n0, n, loads, k=KD):
            s = n0 % 2
            act.wait_ge(sem(f"w_loaded{s}"), 16 * loads)
            act.wait_ge(sem("d_done"), 3 * n)
            A.activation(WH[:, s, 0:k], Wraw[:, s, 0:k], ACT.Copy).then_inc(sem("w_hi"), 1)

        def split_lo(pool, n0, n, k=KD):
            s = n0 % 2
            pool.wait_ge(sem("w_hi"), n + 1)
            G.tensor_tensor(WL[:, s, 0:k], Wraw[:, s, 0:k], WH[:, s, 0:k].bitcast(F32),
                            ALU.subtract).then_inc(sem("w_split"), 1)

        def product(n0, t, out, xH, xL, k0=0, nk=KD, before_last=None):
            s = n0 % 2
            cols = slice(TN * t, TN * t + TN)
            for k in range(nk):
                if k == nk - 1 and before_last:
                    before_last()
                for i, (w, x) in enumerate(((WH, xH), (WH, xL), (WL, xH))):
                    ins = PE.matmul(out[:, 0:TN], w[:, s, k0 + k, :], x[:, k, cols],
                                    start=(k == 0 and i == 0), stop=(k == nk - 1 and i == 2))
            return ins

        def job(pe, n0, n, t, xH=None, xL=None, before_last=None):
            if t == 0:
                pe.wait_ge(sem("w_split"), n + 3)
            pe.wait_ge(sem(f"d_free{t}"), n)
            product(n0, t, dense[t], hH if xH is None else xH, hL if xL is None else xL, before_last=before_last).then_inc(sem("d_done"), 1)

        def apart(eng):
            eng.sem_inc(sem("apart"), 1)

        def part(pe, n0, n, p):
            t, k, s = p // KD, p % KD, n0 % 2
            if p == 0:
                pe.wait_ge(sem("w_split"), n + 3)
            if k == 0:
                pe.wait_ge(sem(f"d_free{t}"), n)
            for i, (w, x) in enumerate(((WH, hH), (WH, hL), (WL, hH))):
                ins = PE.matmul(dense[t][:, 0:TN], w[:, s, k, :], x[:, k, TN * t:TN * t + TN],
                                start=(k == 0 and i == 0), stop=(k == KD - 1 and i == 2))
            if k == KD - 1:
                ins.then_inc(sem("d_done"), 1)

        def fill_out(act, n0, n, t, half, before, dst):
            done(act, n, t)
            act.wait_ge(sem(f"stored{half}"), 16 * before + 1)
            A.activation(fill[:, half], dense[t][:, 0:TN], ACT.Copy).then_inc(sem(f"d_free{t}"), 1)
            act.wait_ge(sem(f"d_free{t}"), n + 1)
            act.dma_start(dst[:, TN * t:TN * t + TN], fill[:, half]).then_inc(sem(f"stored{half}"), 16)

        def fill_pair(act, n0, n, it, c, before):
            x, t = c // NG, c % NG
            dst = (qkv_d[bass.ds(it, 1), x] if x < 3 else ga_d[bass.ds(it, 1)]).rearrange("o p t -> (o p) t")
            fill_out(act, n0 + x, n + x, t, c % 2, before + c // 2, dst)

        def pair_cols(it, x):
            return C_QKV + x * WB + it * P if x < 3 else C_GA + it * P

        def done(eng, n, t):
            eng.wait_ge(sem("d_done"), 3 * n + t + 4)

        sc_h = ExitStack()
        xt, xs = sb("xt", [P, 3, D], F32, sc_h), sb("xs", [P, 2, D], F32, sc_h)
        junk = sb("junk", [P, D], F32, sc_h)
        sc_h.close()

        def x_rows(sp, m, dst, s):
            c, n = tiles9[m]
            if c + n <= TP:
                sp.dma_start(dst[0:n], a["x_prompt"][0, c:c + n, :]).then_inc(s, 16)
                return 1
            sp.dma_start(dst[0:TP - c], a["x_prompt"][0, c:TP, :]).then_inc(s, 16)
            sp.dma_start(dst[TP - c:n], a["x_sample"].rearrange("b t d -> (b t) d")).then_inc(s, 16)
            return 2

        def start_sync(sp):
            x_rows(sp, 0, xt[:, 0], sem("x_in0"))
            for r, name in ((NORM1, "norm1"), (NORM2, "norm2")):
                sp.dma_start(vec_rows[r:r + KD, :], a[name][0].rearrange("(k p) -> k p", p=P)).then_inc(sem("consts"), 16)
            sp.dma_start(vec_rows[FNORM:FNORM + KD, :], a["final_norm"].rearrange("(k p) -> k p", p=P)).then_inc(sem("consts"), 16)
            sp.dma_start(vec_rows[GNORM:GNORM + 1, :], a["gnorm_a"]).then_inc(sem("consts"), 16)
            sp.dma_start(ident[:], a["ident"]).then_inc(sem("consts"), 16)
            for m in range(1, 9):
                if m >= 3:
                    sp.wait_ge(sem("x_scaled"), m - 2)
                x_rows(sp, m, xt[:, m % 3], sem(f"x_in{m % 3}"))
                if m == 2:
                    load_cols(sp, N_AB, N_AB, w_in, C_AB)
            for j in range(2):
                load_cols(sp, N_HEAD + j, N_HEAD + j, w_in, j * WA)

        FROM_ONE = ("at_made", "att_s_stored", "att_stored", "back", "gate_stored", "kv_stored", "kvs_stored", "min_s", "mins",
                    "o_turned", "oa_part", "oa_stored", "pv_s", "q_own", "s0_done", "s0_new", "s0_stored", "s_smp", "sq_added",
                    "state_stored", "stored0", "stored1", "tails_stored", "tails_turned", "tinv_out", "v_done", "y_done")

        def start_pool(pool):
            for name in FROM_ONE:
                pool.sem_inc(sem(name), 1)
            pool.sem_inc(sem("w_split"), 2)
            G.memset(ones[:], 1.0).then_inc(sem("zeroed"), 1)
            split_lo(pool, N_AB, N_AB)

        def start_scalar(act):
            def square(m):
                n = tiles9[m][1]
                act.wait_ge(sem(f"x_in{m % 3}"), 16 * (m // 3 + 1 + (m == 8)))
                A.activation(junk[0:n, :], xt[0:n, m % 3], ACT.Square, accum_out=ssx[0:n, m:m + 1]).then_inc(sem("squares"), 1)
                act.wait_ge(sem("squares"), m + 1)
            act.wait_ge(sem("vec_T"), 1)
            A.activation(vec[:], work[4][:, 0:25], ACT.Copy).then_inc(sem("vec_set"), 1)
            act.wait_ge(sem("vec_set"), 1)
            def root(m):
                n = tiles9[m][1]
                act.wait_ge(sem("mean"), m + 1)
                A.activation(rx[0:n, m:m + 1], rx[0:n, m:m + 1], ACT.Sqrt).then_inc(sem("root"), 1)
            square(0)
            root(0)
            square(1)
            for m in range(9):
                c, n = tiles9[m]
                if m < 8:
                    root(m + 1)
                if m < 7:
                    square(m + 2)
                for half in range(2):
                    act.wait_ge(sem("turned"), 2 * m + half + 1)
                    for k in range(4):
                        kk = 4 * half + k
                        ins = A.activation(hH[:, kk, c:c + n], work[2 * (m % 2) + half][:, k * P:k * P + n], ACT.Copy,
                                           scale=vec[:, NORM1 + kk:NORM1 + kk + 1])
                    ins.then_inc(sem("h_hi"), 1)
                if m == 0:
                    split_hi(act, N_AB, N_AB, 1)

        def start_vector(dve):
            def mean(m):
                n = tiles9[m][1]
                dve.wait_ge(sem("squares"), m + 1)
                V.tensor_scalar(rx[0:n, m:m + 1], ssx[0:n, m:m + 1], 1.0 / D, EPS, ALU.mult, ALU.add).then_inc(sem("mean"), 1)

            def scaled(m):
                n = tiles9[m][1]
                dve.wait_ge(sem("root"), m + 1)
                chV.link(dve, V.reciprocal(rx[0:n, m:m + 1], rx[0:n, m:m + 1]))
                if m >= 2:
                    dve.wait_ge(sem("turned"), 2 * (m - 1))
                V.tensor_scalar(xs[0:n, m % 2], xt[0:n, m % 3], rx[0:n, m:m + 1], None, ALU.mult).then_inc(sem("x_scaled"), 1)
            mean(0)
            scaled(0)
            mean(1)
            for m in range(9):
                c, n = tiles9[m]
                if m < 8:
                    scaled(m + 1)
                if m < 7:
                    mean(m + 2)
                for half in range(2):
                    dve.wait_ge(sem("h_hi"), 2 * m + half + 1)
                    for k in range(4):
                        kk = 4 * half + k
                        ins = V.scalar_tensor_tensor(out=hL[:, kk, c:c + n], in0=work[2 * (m % 2) + half][:, k * P:k * P + n],
                                                     scalar=vec[:, NORM1 + kk:NORM1 + kk + 1],
                                                     in1=hH[:, kk, c:c + n].bitcast(F32), op0=ALU.mult, op1=ALU.subtract)
                    ins.then_inc(sem("h_lo"), 1)

        def start_tensor(pe):
            pe.wait_ge(sem("consts"), 16 * 5)
            PE.transpose(work[4][:, 0:25], vec_rows[:, :], ident[0:25, 0:25]).then_inc(sem("vec_T"), 1)
            pe.sem_inc(sem("d_done"), 3)
            for m in range(9):
                c, n = tiles9[m]
                pe.wait_ge(sem("x_scaled"), m + 1)
                for half in range(2):
                    if m >= 2:
                        pe.wait_ge(sem("h_lo"), 2 * (m - 2) + half + 1)
                    for k in range(4):
                        kk = 4 * half + k
                        ins = PE.transpose(work[2 * (m % 2) + half][:, k * P:k * P + n], xs[0:n, m % 2, kk * P:kk * P + P],
                                           ident[0:n, 0:n])
                    ins.then_inc(sem("turned"), 1)
                if m in (4, 7):
                    pe.wait_ge(sem("h_lo"), 6 * (m // 3))
                    job(pe, N_AB, N_AB, m // 3 - 1)

        sc_ab = ExitStack()
        row_t = sb("row_t", [72, T], F32, sc_ab)
        ab_x, ab_e = sb("ab_x", [8, T], F32, sc_ab), sb("ab_e", [8, T], F32, sc_ab)
        reset = sb("reset_sb", [8, T], F32, sc_ab)
        ab_v = sb("ab_v", [8, 4], F32, sc_ab)
        sc_ab.close()
        sc_d = ExitStack()
        pre = sb("pre", [P, 2, 3 + TP + NSEQ * 7], F32, sc_d)
        conv = sb("conv", [P, TP + NSEQ * 7], F32, sc_d)
        qkv = sb("qkv", [P, 3, T], F32, sc_d)
        sq = sb("sq", [P, 2, NT9 * P], F32, sc_d)
        em = sb("em", [P, NT9, P], F32, sc_d)
        cum_b, beta_b = sb("cum_b", [P, T], F32, sc_d), sb("beta_b", [P, T], F32, sc_d)
        turned = sb("turned", [P, NT9, 3, P], F32, sc_d)
        kbg, kd, vb = (sb(n, [P, NT9, P], F32, sc_d) for n in ("kbg", "kd", "vb"))
        tok3 = sb("tok3", [P, 2, 3, P], F32, sc_d)
        at = sb("at", [P, NT9, P], F32, sc_d)
        qk_t = sb("qk_t", [P, NT9, P], F32, sc_d)
        silz = sb("silz", [P, T], F32, sc_d)
        t_sys, systems = sb("t_sys", [NCH * NBLK, BLK * BLK], F32, sc_d), sb("systems", [P, 2, BLK * BLK], F32, sc_d)
        state = sb("state", [P, 2, P], F32, sc_d)
        s0 = sb("s0", [P, NSEQ, P], F32, sc_d)
        vnew = sb("vnew", [P, 2, P], F32, sc_d)
        tails, sc_in, sc_t = sb("tails", [P, 3, 27], F32, sc_d), tok3[0:28, 0], sb("sc_t", [P, 3, 28], F32, sc_d)
        tails_t = sb("tails_t", [27, 3, P], F32, sc_d)
        col = sb("col", [P, NT9, 72], F32, sc_d)
        ecum, elast = sb("ecum", [P, NT9, 8], F32, sc_d), sb("elast", [P, NT9, 8], F32, sc_d)
        ck, cq, cbg, ckd, cqg, cb, ccum = (sb(n, [P, NT9], F32, sc_d) for n in ("ck", "cq", "cbg", "ckd", "cqg", "cb", "ccum"))
        ssn = sb("ssn", [P, 2 * NT9], F32, sc_d)
        glast = sb("glast", [P, 2 * NCH], F32, sc_d)
        osum = sb("osum", [P, NT9], F32, sc_d)
        masks = sb("masks_sb", [P, 5, P], F32, sc_d)
        masks_s = sb("masks_s_sb", [TS, 2, TS], F32, sc_d)
        own_row, own_col = sb("own_row_sb", [P, NSEQ, TS], F32, sc_d), sb("own_col_sb", [TS, NSEQ], F32, sc_d)
        small8 = sb("small8", [TS, 4, TS], F32, sc_d)
        sc_d.close()
        e_all = sq[:, 0].rearrange("p (t i) -> p t i", i=P)
        emb = sq[:, 1].rearrange("p (t i) -> p t i", i=P)
        t_all = sq[:, 0, 0:TP].rearrange("p (t i) -> p t i", i=P)
        tt_all = emb
        at_lvl = [qkv[:, s, 0:TP].rearrange("p (t i) -> p t i", i=P) for s in range(3)]
        y_all = pre[:, 1, 0:TP].rearrange("p (t i) -> p t i", i=P)
        kdm = pre[0:TS, 0, 0:TP].rearrange("p (b i) -> p b i", i=P)
        nw = conv[:, 0:T]
        a_sys, p_sys = systems[0:NCH * NBLK, 0], systems[0:NCH * NBLK, 1]
        wm, qm = (systems[:, x].rearrange("p (b t) -> p b t", t=TS) for x in range(2))
        o_raw = em
        oa_out = cum_b
        SEQ = lambda ap: ap.rearrange("p (b t) -> p b t", t=TSEQ)
        W7 = TSEQ + 3
        tokens = [(P * t, P) for t in range(NCH)] + [(TP, TS)]

        def ab_sync(sp):
            sp.wait_ge(sem("zeroed"), 2)
            sp.dma_start(ab_v[0:4, 0:1], a["a_log"].rearrange("o h -> h o")).then_inc(sem("consts"), 16)
            sp.dma_start(ab_v[0:4, 1:2], a["dt_bias"].rearrange("o h -> h o")).then_inc(sem("consts"), 16)
            sp.dma_start(reset[:], a["reset"]).then_inc(sem("consts"), 16)
            for dst, name in ((masks, "masks"), (masks_s, "masks_s"), (own_row, "own_row"), (own_col, "own_col"), (t_sys, "unit")):
                sp.dma_start(dst[:], a[name]).then_inc(sem("consts"), 16)

        def ab_pool(pool):
            pool.wait_ge(sem("h_lo"), 18)
            G.memset(ab_v[:], 0.0).then_inc(sem("zeroed"), 1)
            G.memset(row_t[:], 0.0).then_inc(sem("zeroed"), 1)
            split_lo(pool, N_HEAD, N_HEAD)
            G.memset(at[:], 0.0).then_inc(sem("zeroed"), 1)
            split_lo(pool, N_HEAD + 1, N_HEAD + 1)
            pool.wait_ge(sem("cols_read"), 1)
            G.memset(sq[:, :, T:NT9 * P], 0.0).then_inc(sem("zeroed"), 1)
            G.memset(osum[:], 0.0).then_inc(sem("zeroed"), 1)
            pool.wait_ge(sem("consts"), 208)

        def ab_scalar(act):
            split_hi(act, N_HEAD, N_HEAD, N_HEAD // 2 + 1)
            act.wait_ge(sem("zeroed"), 3)
            for t in range(NG):
                done(act, N_AB, t)
                A.activation(row_t[32:40, TN * t:TN * t + TN], dense[t][0:8, 0:TN], ACT.Sigmoid).then_inc(sem("ab_act"), 1)
            act.wait_ge(sem("consts"), 208)
            A.activation(ab_v[:, 2:3], ab_v[:, 0:1], ACT.Exp).then_inc(sem("ab_act"), 1)
            act.wait_ge(sem("ab_x"), 1)
            chA.link(act, A.activation(ab_e[:], ab_x[:], ACT.Abs))
            chA.link(act, A.activation(ab_e[:], ab_e[:], ACT.Exp, scale=-1.0))
            A.activation(ab_e[:], ab_e[:], ACT.Ln, bias=1.0).then_inc(sem("ab_act"), 1)
            split_hi(act, N_HEAD + 1, N_HEAD + 1, (N_HEAD + 1) // 2 + 1)
            act.wait_ge(sem("zeroed"), 4)
            act.dma_start(t_d[:, 0:P].rearrange("c i j -> i c j"), at[:, 0:NCH]).then_inc(sem("tinv_in"), 16)
            act.wait_ge(sem("rows_ready"), 1)
            act.dma_start(rows_d[0:8, :], row_t[0:8, :]).then_inc(sem("rows_out"), 16)
            act.dma_start(rows_d[8:16, :], row_t[32:40, :]).then_inc(sem("rows_out"), 16)
            act.wait_ge(sem("cols_read"), 1)
            A.activation(ecum[:], col[:, :, 0:8], ACT.Exp)
            A.activation(elast[:], col[:, :, 64:72], ACT.Exp)
            act.wait_ge(sem("rows_out"), 32)
            act.wait_ge(sem("zeroed"), 6)

        def ab_vector(dve):
            dve.wait_ge(sem("consts"), 208)
            for t in range(NG):
                dve.wait_ge(sem("ab_act"), t + 1)
                ins = V.tensor_scalar(ab_x[:, TN * t:TN * t + TN], dense[t][0:8, 0:TN], ab_v[:, 1:2], None, ALU.add)
                ins.then_inc(sem(f"d_free{t}"), 1)
            for t in range(NG):
                dve.wait_ge(sem(f"d_free{t}"), 1)
            dve.wait_ge(sem("ab_act"), 4)
            V.tensor_scalar(ab_v[:, 3:4], ab_v[:, 2:3], -1.0, None, ALU.mult).then_inc(sem("ab_x"), 1)
            dve.wait_ge(sem("ab_act"), 5)
            chV.link(dve, V.scalar_tensor_tensor(out=ab_x[:], in0=ab_x[:], scalar=0.0, in1=ab_e[:], op0=ALU.max, op1=ALU.add))
            chV.link(dve, V.tensor_scalar(ab_x[:], ab_x[:], ab_v[:, 3:4], None, ALU.mult))
            chV.link(dve, V.tensor_tensor_scan(row_t[0:8, :], reset[:], ab_x[:], 0.0, ALU.mult, ALU.add))
            for lo, n, w in ((0, NCH, P), (TP, NSEQ, TSEQ)):
                x = row_t[0:8, lo:lo + n * w].rearrange("p (c i) -> p c i", i=w)
                y = row_t[64:72, lo:lo + n * w].rearrange("p (c i) -> p c i", i=w)
                ins = V.tensor_tensor(y, x[:, :, w - 1:w].to_broadcast([8, n, w]), x, ALU.subtract)
                chV.link(dve, ins)
            V.memset(col[:, NCH], 0.0).then_inc(sem("rows_ready"), 1)
            for i, (lo, hi) in enumerate(((0, 5), (5, 8))):
                dve.wait_ge(sem("cols_turned"), i + 1)
                chV.link(dve, V.tensor_copy(col[:, lo:hi], work[i][:, 0:72 * (hi - lo)].rearrange("p (t r) -> p t r", r=72)))
            V.tensor_copy(col[0:TS, NCH], work[1][0:TS, 216:288]).then_inc(sem("cols_read"), 1)
            dve.wait_ge(sem("rows_out"), 32)
            dve.wait_ge(sem("tinv_in"), 16)

        def ab_tensor(pe):
            pe.wait_ge(sem("h_lo"), 18)
            job(pe, N_AB, N_AB, 2)
            job(pe, N_HEAD, N_HEAD, 0)
            pe.wait_ge(sem("rows_ready"), 1)
            pe.wait_ge(sem("h_lo"), 18)
            for t, (c, n) in enumerate(tokens):
                ins = PE.transpose(work[t // 5][0:n, 72 * (t % 5):72 * (t % 5) + 72], row_t[0:72, c:c + n], ident[0:72, 0:72])
                if t in (4, 8):
                    ins.then_inc(sem("cols_turned"), 1)

        def diagonal(x):
            return bass.AP(x.tensor, 0, [[BLK * (P + 1), NCH * NBLK], [P, BLK], [1, BLK]])

        def head_sync(sp, h, first=False):
            def load(j):
                col = j * WA + h * HD if j < 4 else pair_cols(h, j - 4)
                load_cols(sp, N_HEAD + j, N_HEAD + j + 8 * h, w_in, col)
            if not first:
                for j in range(2):
                    load(j)
            sp.wait_ge(sem("back"), NT9 * h + 1)
            for j in range(3):
                sp.dma_start(sc_in[0:24, j, :], a["state_conv"][0].rearrange("b t c -> (b t) c")[:, bass.ds(j * WA + h * HD, HD)]).then_inc(sem("sc_loaded"), 16)
                sp.dma_start(sc_in[24:28, j, :], a["conv_w"][0][:, bass.ds(j * WA + h * HD, HD)]).then_inc(sem("sc_loaded"), 16)
            for j in range(2, 6):
                load(j)
            sp.wait_ge(sem("oa_stored"), 16 * h + 1)
            sp.wait_ge(sem("rows_out"), 32)
            sp.dma_start(cum_b[:], rows_d[bass.ds(h, 1), :].to_broadcast([P, T])).then_inc(sem("cum_loaded"), 16)
            sp.wait_ge(sem("at_made"), h + 1)
            sp.dma_start(beta_b[:], rows_d[bass.ds(h + 12, 1), :].to_broadcast([P, T])).then_inc(sem("beta_loaded"), 16)
            sp.wait_ge(sem("s0_stored"), 16 * h + 1)
            sp.dma_start(s0[:], a["state_delta"][0][:, bass.ds(h, 1)].rearrange("b o k v -> k (b o) v")).then_inc(sem("s0_loaded"), 16)
            for j in range(6, 8):
                load(j)
            for g in range(3):
                drop = WIN[0] - TSEQ if g == 0 else PAST
                src, dst = (x[0][bass.ds(2 * h, 2)].rearrange("b t s h d -> b t (s h d)") for x in (a[f"cache_win{g}"], a[f"win{g}_s"]))
                sp.dma_start(dst[:, 0:drop], src[:, min(WIN[g], PAST) - drop:]).then_inc(sem("cache_out"), 16)
            sp.wait_ge(sem("tails_out"), h + 1)
            for j in range(3):
                c0 = bass.ds(j * WA + h * HD, HD)
                sp.dma_start(a["conv_p"][0, 0][:, c0], tails_t[0:3, j]).then_inc(sem("tails_stored"), 16)
                sp.dma_start(a["conv_s"][0].rearrange("b t c -> (b t) c")[:, c0], tails_t[3:27, j]).then_inc(sem("tails_stored"), 16)
            sp.wait_ge(sem("at_made"), h + 2)
            sp.dma_start(at_d[:, 0:P].rearrange("c j i -> j c i"), at[:, 0:NCH]).then_inc(sem("diag_out"), 16)
            sp.wait_ge(sem("diag_out"), 16 * h + 16)
            sp.dma_start(a_sys.rearrange("s (j i) -> s j i", i=BLK), diagonal(at_d)).then_inc(sem("diag_in"), 16)
            sp.wait_ge(sem("t_solved"), h + 1)
            sp.wait_ge(sem("tinv_in"), 16 * h + 16)
            sp.dma_start(diagonal(t_d), t_sys[:].rearrange("s (j i) -> s j i", i=BLK)).then_inc(sem("tinv_out"), 16)
            sp.wait_ge(sem("tinv_out"), 16 * (h + 1) + 1)
            sp.dma_start(t_all, t_d[:, 0:P].rearrange("c i j -> i c j")).then_inc(sem("tinv_in"), 16)

        def head_pool(pool, h):
            def split(j):
                split_lo(pool, N_HEAD + j, N_HEAD + j + 8 * h)
            for j in range(2, 6):
                split(j)
            pool.wait_ge(sem("e_ready"), h + 1)
            pool.wait_ge(sem("o_turned"), 3 * h + 1)
            G.tensor_tensor(em[:, 0:NCH], e_all[:, 0:NCH], masks[:, 0:1].to_broadcast([P, NCH, P]), ALU.mult).then_inc(sem("em_made"), 1)
            G.tensor_tensor(em[0:TS, NCH, 0:TS], e_all[0:TS, NCH, 0:TS], masks_s[:, 0], ALU.mult).then_inc(sem("em_made"), 1)
            pool.wait_ge(sem("beta_loaded"), 16 * h + 16)
            chG.link(pool, G.tensor_tensor(emb[:, 0:NCH], e_all[:, 0:NCH], beta_b[:, 0:TP].rearrange("p (t i) -> p t i", i=P), ALU.mult))
            chG.link(pool, G.tensor_tensor(emb[0:TS, NCH, 0:TS], e_all[0:TS, NCH, 0:TS], beta_b[0:TS, TP:T], ALU.mult))
            G.tensor_tensor(emb[:, 0:NCH], emb[:, 0:NCH], masks[:, 1:2].to_broadcast([P, NCH, P]), ALU.mult).then_inc(sem("emb_made"), 1)
            G.tensor_tensor(emb[0:TS, NCH, 0:TS], emb[0:TS, NCH, 0:TS], masks_s[:, 1], ALU.mult).then_inc(sem("emb_made"), 1)
            split(6)
            pool.wait_ge(sem("at_made"), h + 2)
            for s in range(3):
                G.tensor_tensor(at_lvl[s], at[:, 0:NCH], masks[:, 2 + s:3 + s].to_broadcast([P, NCH, P]), ALU.mult).then_inc(sem("lvl_made"), 1)
            split(7)
            split(8)
            pool.wait_ge(sem("nw_made"), 3 * h + 3)
            G.tensor_tensor(wm, nw[:, TP:T].rearrange("p (o i) -> p o i", o=1).to_broadcast([P, NSEQ, TS]), own_row[:], ALU.mult).then_inc(sem("smp_made"), 1)
            G.tensor_tensor(qm, turned[:, NCH, 2:3, 0:TS].to_broadcast([P, NSEQ, TS]), own_row[:], ALU.mult).then_inc(sem("smp_made"), 1)
            G.tensor_tensor(kdm, kd[0:TS, NCH:NCH + 1].to_broadcast([TS, NSEQ, P]),
                            own_col[:].rearrange("p (b o) -> p b o", o=1).to_broadcast([TS, NSEQ, P]), ALU.mult).then_inc(sem("smp_made"), 1)
            split(9)

        def head_scalar(act, h):
            def split(j):
                split_hi(act, N_HEAD + j, N_HEAD + j + 8 * h, (N_HEAD + j) // 2 + 4 * h + 1)

            def filled(*groups):
                for c in groups:
                    fill_pair(act, N_HEAD + 4, N_HEAD + 4 + 8 * h, h, c, 6 * h)
            for j in range(4):
                n = N_HEAD + j + 8 * h
                if j == 3:
                    silu(act, h, 2)
                    act.wait_ge(sem("oa_part"), 3 * h + 1)
                    for t in range(NG):
                        done(act, n, t)
                        A.activation(silz[:, TN * t:TN * t + TN], dense[t][:, 0:TN], ACT.Silu).then_inc(sem(f"d_free{t}"), 1)
                    split(5)
                    break
                s = j % 2
                if j == 0:
                    act.wait_ge(sem("s0_done"), 2 * h + 1)
                for t in range(NG):
                    done(act, n, t)
                    if j == 2 and t == 0:
                        act.wait_ge(sem("conv_done"), 3 * h + 1)
                    c = TN * t
                    w = min(TN, TP - c)
                    ins = A.activation(pre[:, s, 3 + c:3 + c + w], dense[t][:, 0:w], ACT.Copy)
                    if w < TN:
                        ins = A.activation(pre[:, s, 3 + TP:].rearrange("p (b t) -> p b t", t=W7)[:, :, 3:W7], SEQ(dense[t][:, w:TN]), ACT.Copy)
                    ins.then_inc(sem(f"d_free{t}"), 1)
                split(j + 2)
                if j >= 1:
                    silu(act, h, j - 1)
            act.wait_ge(sem("mean"), NT9 + 2 * h + 1)
            A.activation(ssn[:], ssn[:], ACT.Sqrt).then_inc(sem("root"), 1)
            act.wait_ge(sem("e_arg"), h + 1)
            A.activation(e_all[:, 0:NCH], e_all[:, 0:NCH], ACT.Exp)
            A.activation(e_all[0:TS, NCH, 0:TS], e_all[0:TS, NCH, 0:TS], ACT.Exp).then_inc(sem("e_ready"), 1)
            A.activation(glast[:, 0:NCH], cum_b[:, P - 1:TP:P], ACT.Exp)
            A.activation(glast[:, NCH:2 * NCH], cum_b[:, TP + TSEQ - 1:T:TSEQ], ACT.Exp).then_inc(sem("glast"), 1)
            filled(0)
            act.wait_ge(sem("cols_made"), h + 1)
            for t, (c, n) in enumerate(tokens):
                act.wait_ge(sem("fwd"), 2 * (NT9 * h + t) + 2)
                b = work[2 + t % 2]
                if t >= 2:
                    act.wait_ge(sem("back"), NT9 * h + t)
                A.activation(tok3[0:n, t % 2, 1], b[0:n, 0:P], ACT.Copy, scale=cq[0:n, t:t + 1])
                A.activation(tok3[0:n, t % 2, 2], b[0:n, 0:P], ACT.Copy, scale=cqg[0:n, t:t + 1])
                A.activation(vb[0:n, t], b[0:n, P:2 * P], ACT.Copy, scale=cb[0:n, t:t + 1]).then_inc(sem("ev_a"), 1)
                if t >= 1:
                    turned_back(act, h, t - 1)
            turned_back(act, h, NCH)
            filled(1, 2)
            split(6)
            filled(3, 4, 5)
            split(7)
            filled(6, 7, 8)
            for s in range(3):
                for half in range(2):
                    act.wait_ge(sem("y_done"), 6 * h + 2 * s + half + 2)
                    A.activation(y_all[:, 4 * half:4 * half + 4], work[half][:].rearrange("p (t i) -> p t i", i=P), ACT.Copy).then_inc(sem("y_read"), 1)
            split(8)
            for i in range(3):
                act.wait_ge(sem("nw_done"), 3 * h + i + 1)
                w = 4 * P if i < 2 else TS
                A.activation(nw[:, 4 * P * i:4 * P * i + w], work[(0, 1, 2)[i]][:, 0:w], ACT.Copy, scale=-1.0).then_inc(sem("nw_made"), 1)
            for t, (c, n) in enumerate(tokens):
                act.wait_ge(sem("v_done"), NT9 * h + t + 2)
                A.activation(vnew[0:n, t % 2], work[t % 2][0:n, 0:P], ACT.Copy).then_inc(sem("v_read"), 1)
                if t >= 1:
                    out_sum(act, h, t - 1)
                if t in (1, 5, 8):
                    filled(9 + t // 4)
            split(9)
            out_sum(act, h, NCH)
            act.wait_ge(sem("mean"), NT9 + 2 * h + 2)
            A.activation(osum[:], osum[:], ACT.Sqrt).then_inc(sem("root"), 1)
            act.wait_ge(sem("s_final"), h + 1)
            act.dma_start(a["delta_p"][0, 0][bass.ds(h, 1)].rearrange("o k v -> (o k) v"), state[:, (NCH - 1) % 2]).then_inc(sem("state_stored"), 16)
            act.wait_ge(sem("s0_new"), h + 2)
            act.dma_start(a["delta_s"][0][:, bass.ds(h, 1)].rearrange("b o k v -> k (b o) v"), s0[:]).then_inc(sem("s0_stored"), 16)
            act.wait_ge(sem("oa_ready"), h + 1)
            act.dma_start(oa_d[bass.ds(h, 1)].rearrange("o p t -> (o p) t"), oa_out[:]).then_inc(sem("oa_stored"), 16)

        def silu(act, h, j):
            act.wait_ge(sem("conv_done"), 3 * h + j + 1)
            if j == 0:
                act.wait_ge(sem("y_done"), 6 * h + 1)
            A.activation(qkv[:, j, 0:TP], conv[:, 0:TP], ACT.Silu)
            ins = A.activation(SEQ(qkv[:, j, TP:T]), conv_out(), ACT.Silu)
            ins.then_inc(sem("silu"), 1)
            if j < 2:
                if j == 0:
                    act.wait_ge(sem("v_done"), NT9 * h + 1)
                act.wait_ge(sem("silu"), 3 * h + j + 1)
                A.activation(sq[:, j, 0:T], qkv[:, j, :], ACT.Square).then_inc(sem("squared"), 1)

        def conv_out():
            return bass.AP(conv, TP + 3, [[TP + NSEQ * W7, P], [W7, NSEQ], [1, TSEQ]])

        def turned_back(act, h, t):
            n = tokens[t][1]
            act.wait_ge(sem("back"), NT9 * h + t + 2)
            A.activation(turned[:, t, :, 0:n], work[4][:, 0:3 * P].rearrange("p (x i) -> p x i", x=3)[:, :, 0:n], ACT.Copy).then_inc(sem("back_read"), 1)

        def out_sum(act, h, t):
            n = tokens[t][1]
            act.wait_ge(sem("o_done"), NT9 * h + t + 1)
            if t == 0:
                act.wait_ge(sem("at_made"), h + 2)
            o = work[2 + t % 2][0:n, 0:P]
            A.activation(o_raw[0:n, t], o, ACT.Copy)
            A.activation(o, o, ACT.Square, accum_out=osum[0:n, t:t + 1]).then_inc(sem("o_read"), 1)

        def head_vector(dve, h):
            dve.wait_ge(sem("sc_turned"), h + 1)
            chV.link(dve, V.tensor_copy(sc_t[:], work[4][:, 0:84].rearrange("p (j r) -> p j r", j=3)))
            dve.wait_ge(sem("s0_done"), 2 * h + 1)
            for s in range(2):
                V.memset(pre[:, s, 0:3], 0.0)
            for j in range(3):
                s = j % 2
                x = pre[:, s]
                tail = x[:, 3 + TP:].rearrange("p (b t) -> p b t", t=W7)
                chV.link(dve, V.tensor_copy(tail[:, :, 0:3], sc_t[:, j, 0:24].rearrange("p (b t) -> p b t", t=3)))
                n = N_HEAD + j + 8 * h
                for t in range(NG):
                    dve.wait_ge(sem(f"d_free{t}"), n + 1)
                if j == 0:
                    dve.wait_ge(sem("tails_turned"), h + 1)
                chV.link(dve, V.tensor_copy(tails[:, j, 0:3], x[:, TP:TP + 3]))
                chV.link(dve, V.tensor_copy(tails[:, j, 3:27].rearrange("p (b t) -> p b t", t=3), tail[:, :, TSEQ:W7]))
                if j == 0:
                    dve.wait_ge(sem("v_done"), NT9 * h + 1)
                else:
                    dve.wait_ge(sem("silu"), 3 * h + j)
                L = TP + NSEQ * W7
                chV.link(dve, V.tensor_scalar(conv[:], x[:, 0:L], sc_t[:, j, 24:25], None, ALU.mult))
                for i in (1, 2, 3):
                    ins = V.scalar_tensor_tensor(out=conv[:], in0=x[:, i:i + L], scalar=sc_t[:, j, 24 + i:25 + i], in1=conv[:], op0=ALU.mult, op1=ALU.add)
                    if i < 3:
                        chV.link(dve, ins)
                ins.then_inc(sem("conv_done"), 1)
            dve.wait_ge(sem("tails_turned"), h + 2)
            dve.wait_ge(sem("tails_stored"), 96 * h + 1)
            V.tensor_copy(tails_t[:], work[2][0:27, 0:3 * P].rearrange("p (j i) -> p j i", j=3)).then_inc(sem("tails_out"), 1)
            dve.wait_ge(sem("ss_done"), h + 1)
            V.tensor_scalar(ssn[:], work[4][:, 0:2 * NT9], EPS, None, ALU.add).then_inc(sem("mean"), 1)
            dve.wait_ge(sem("cum_loaded"), 16 * h + 16)
            chV.link(dve, V.tensor_copy(ccum[:], col[:, :, bass.ds(h, 1)].rearrange("p t o -> p (t o)")))
            chV.link(dve, V.tensor_copy(cb[:], col[:, :, bass.ds(h + 36, 1)].rearrange("p t o -> p (t o)")))
            for t, (c, n) in enumerate(tokens):
                ins = V.tensor_scalar(e_all[0:n, t, 0:n], cum_b[0:n, c:c + n], ccum[0:n, t:t + 1], 0.0, ALU.subtract, ALU.min)
            ins.then_inc(sem("e_arg"), 1)
            dve.wait_ge(sem("root"), NT9 + 2 * h + 1)
            chV.link(dve, V.reciprocal(ssn[:], ssn[:]))
            rq, rk = ssn[:, 0:NT9], ssn[:, NT9:2 * NT9]
            ec, el = (x[:, :, bass.ds(h, 1)].rearrange("p t o -> p (t o)") for x in (ecum, elast))
            V.tensor_copy(ck[:], rk)
            V.tensor_scalar(cq[:], rq, HD ** -0.5, None, ALU.mult)
            V.scalar_tensor_tensor(out=cqg[:], in0=rq, scalar=HD ** -0.5, in1=ec, op0=ALU.mult, op1=ALU.mult)
            chV.link(dve, V.tensor_tensor(ckd[:], rk, el, ALU.mult))
            chV.link(dve, V.tensor_tensor(cbg[:], rk, ec, ALU.mult))
            V.tensor_tensor(cbg[:], cbg[:], cb[:], ALU.mult).then_inc(sem("cols_made"), 1)
            dve.wait_ge(sem("cols_made"), h + 1)
            for t, (c, n) in enumerate(tokens):
                dve.wait_ge(sem("fwd"), 2 * (NT9 * h + t) + 1)
                if t >= 2:
                    dve.wait_ge(sem("back"), NT9 * h + t)
                b = work[t % 2][0:n, 0:P]
                V.tensor_scalar(tok3[0:n, t % 2, 0], b, ck[0:n, t:t + 1], None, ALU.mult)
                V.tensor_scalar(kbg[0:n, t], b, cbg[0:n, t:t + 1], None, ALU.mult)
                V.tensor_scalar(kd[0:n, t], b, ckd[0:n, t:t + 1], None, ALU.mult).then_inc(sem("ev_v"), 1)
            dve.wait_ge(sem("em_made"), 2 * h + 2)
            dve.wait_ge(sem("emb_made"), 2 * h + 2)
            for i in range(5):
                dve.wait_ge(sem("kk_done"), 5 * h + i + 1)
                b = work[i % 2][:].rearrange("p (t x i) -> p t x i", t=2, x=2)
                if i < 4:
                    V.tensor_tensor(at[:, 2 * i:2 * i + 2], b[:, :, 0], emb[:, 2 * i:2 * i + 2], ALU.mult)
                    ins = V.tensor_tensor(qk_t[:, 2 * i:2 * i + 2], b[:, :, 1], em[:, 2 * i:2 * i + 2], ALU.mult)
                else:
                    V.tensor_tensor(at[0:TS, NCH, 0:TS], work[0][0:TS, 0:TS], emb[0:TS, NCH, 0:TS], ALU.mult)
                    ins = V.tensor_tensor(qk_t[0:TS, NCH, 0:TS], work[0][0:TS, TS:2 * TS], em[0:TS, NCH, 0:TS], ALU.mult)
                ins.then_inc(sem("kk_read"), 1)
                dve.wait_ge(sem("kk_read"), 5 * h + i + 1)
            dve.sem_inc(sem("at_made"), 1)
            dve.wait_ge(sem("s8"), 3 * h + 1)
            V.tensor_copy(small8[:, 0], work[2][0:TS, 0:TS]).then_inc(sem("s8_read"), 1)
            chV.link(dve, V.tensor_tensor(small8[:, 2], ident[0:TS, 0:TS], at[0:TS, NCH, 0:TS], ALU.subtract))
            dve.wait_ge(sem("s8"), 3 * h + 2)
            V.tensor_tensor(small8[:, 1], at[0:TS, NCH, 0:TS], work[3][0:TS, 0:TS], ALU.subtract).then_inc(sem("s8_read"), 1)
            dve.wait_ge(sem("s8"), 3 * h + 3)
            chV.link(dve, V.tensor_tensor(tt_all[0:TS, NCH, 0:TS], work[2][0:TS, 0:TS], small8[:, 2], ALU.add))
            dve.wait_ge(sem("diag_in"), 16 * (h + 1))
            dve.wait_ge(sem("tinv_out"), 16 * h + 1)
            av = a_sys.rearrange("s (j i) -> s i j", i=BLK)
            tv = t_sys[:].rearrange("s (i c) -> s i c", c=BLK)
            chV.link(dve, V.tensor_scalar(a_sys, a_sys, -1.0, None, ALU.mult))
            for i in range(1, BLK):
                prod = p_sys[:, 0:i * i].rearrange("s (c j) -> s c j", j=i)
                chV.link(dve, V.tensor_tensor(prod, tv[:, 0:i, 0:i].rearrange("s j c -> s c j"), av[:, i:i + 1, 0:i].to_broadcast([NCH * NBLK, i, i]), ALU.mult))
                chV.link(dve, V.tensor_reduce(tv[:, i, 0:i], prod, AX.X, ALU.add))
            dve.sem_inc(sem("t_solved"), 1)
            for half in range(2):
                dve.wait_ge(sem("tt_done"), 2 * h + half + 1)
                V.tensor_copy(tt_all[:, 4 * half:4 * half + 4], work[half][:].rearrange("p (t i) -> p t i", i=P)).then_inc(sem("tt_set"), 1)
            for s in range(3):
                for half in range(2):
                    r = slice(4 * half, 4 * half + 4)
                    dve.wait_ge(sem("z_done"), 6 * h + 2 * s + half + 1)
                    dve.wait_ge(sem("tt_set"), 8 * h + 2 * s + half + 2)
                    if s < 2:
                        V.tensor_tensor(t_all[:, r], t_all[:, r], work[2 + half][:].rearrange("p (t i) -> p t i", i=P), ALU.subtract)
                    V.tensor_tensor(tt_all[:, r], tt_all[:, r], work[half][:].rearrange("p (t i) -> p t i", i=P), ALU.subtract).then_inc(sem("tt_set"), 1)
            dve.wait_ge(sem("glast"), h + 1)
            dve.wait_ge(sem("state_stored"), 16 * h + 1)
            for t in range(NCH):
                dve.wait_ge(sem("sn_done"), NCH * h + t + 1)
                if t == 0:
                    ins = V.tensor_copy(state[:, 0], work[4][:, 0:P])
                else:
                    ins = V.scalar_tensor_tensor(out=state[:, t % 2], in0=state[:, (t - 1) % 2], scalar=glast[:, t:t + 1], in1=work[4][:, 0:P],
                                                 op0=ALU.mult, op1=ALU.add)
                ins.then_inc(sem("s_new"), 1)
                dve.wait_ge(sem("s_new"), NCH * h + t + 1)
            dve.sem_inc(sem("s_final"), 1)
            for i in range(2):
                dve.wait_ge(sem("s0_done"), 2 * h + i + 2)
                for b in range(4):
                    q = 4 * i + b
                    ins = V.scalar_tensor_tensor(out=s0[:, q], in0=s0[:, q], scalar=glast[:, NCH + q:NCH + q + 1], in1=work[3 + i][:, P * b:P * b + P],
                                                 op0=ALU.mult, op1=ALU.add)
                chV.link(dve, ins)
            dve.sem_inc(sem("s0_new"), 1)
            dve.wait_ge(sem("o_read"), NT9 * h + NT9)
            V.tensor_scalar(osum[:], osum[:], 1.0 / HD, EPS, ALU.mult, ALU.add).then_inc(sem("mean"), 1)
            dve.wait_ge(sem("root"), NT9 + 2 * h + 2)
            chV.link(dve, V.reciprocal(osum[:], osum[:]))
            for t, (c, n) in enumerate(tokens):
                ins = V.tensor_scalar(o_raw[0:n, t], o_raw[0:n, t], osum[0:n, t:t + 1], None, ALU.mult)
            ins.then_inc(sem("o_normed"), 1)
            for i, (c, n) in enumerate(((0, 512), (512, 512), (TP, TS))):
                dve.wait_ge(sem("o_turned"), 3 * h + i + 2)
                V.scalar_tensor_tensor(out=oa_out[:, c:c + n], in0=work[i][:, 0:n], scalar=vec[:, GNORM:GNORM + 1], in1=silz[:, c:c + n],
                                       op0=ALU.mult, op1=ALU.mult).then_inc(sem("oa_part"), 1)
            dve.wait_ge(sem("oa_part"), 3 * h + 4)
            dve.sem_inc(sem("oa_ready"), 1)

        def head_tensor(pe, h):
            def fill_parts(first, last):
                for p in range(first, last):
                    part(pe, N_HEAD + 4 + p // 24, N_HEAD + 4 + p // 24 + 8 * h, p % 24)
            for j in range(4):
                for t in range(NG):
                    if j or t:
                        job(pe, N_HEAD + j, N_HEAD + j + 8 * h, t)
                if j == 0:
                    pe.wait_ge(sem("sc_loaded"), 96 * h + 96)
                    pe.wait_ge(sem("s0_new"), h + 1)
                    apart(pe)
                    for x in range(3):
                        ins = PE.transpose(work[4][:, 28 * x:28 * x + 28], sc_in[:, x], ident[0:28, 0:28])
                    ins.then_inc(sem("sc_turned"), 1)
            fill_parts(0, 8)
            pe.wait_ge(sem("conv_done"), 3 * h + 3)
            pe.wait_ge(sem("oa_part"), 3 * h + 1)
            for j in range(3):
                ins = PE.transpose(work[2][0:27, P * j:P * j + P], tails[:, j], ident[:, :])
            ins.then_inc(sem("tails_turned"), 1)
            pe.wait_ge(sem("squared"), 2 * h + 2)
            for x in range(2):
                for t in range(NT9):
                    ins = PE.matmul(work[4][:, NT9 * x + t:NT9 * x + t + 1], sq[:, x, P * t:P * t + P], ones[:, 0:1], start=True, stop=True)
            ins.then_inc(sem("ss_done"), 1)
            fill_parts(8, 15)
            pe.wait_ge(sem("silu"), 3 * h + 3)
            pe.wait_ge(sem("tails_out"), h + 1)
            for t, (c, n) in enumerate(tokens):
                if t >= 2:
                    pe.wait_ge(sem("ev_v"), NT9 * h + t - 1)
                PE.transpose(work[t % 2][0:n, 0:P], qkv[:, 1, c:c + n], ident[:, :]).then_inc(sem("fwd"), 1)
                if t >= 2:
                    pe.wait_ge(sem("ev_a"), NT9 * h + t - 1)
                PE.transpose(work[2 + t % 2][0:n, 0:P], qkv[:, 0, c:c + n], ident[:, :])
                PE.transpose(work[2 + t % 2][0:n, P:2 * P], qkv[:, 2, c:c + n], ident[:, :]).then_inc(sem("fwd"), 1)
                fill_parts(15 + t, 16 + t)
                if t >= 1:
                    back(pe, h, t - 1)
            back(pe, h, NCH)
            for i in range(5):
                if i == 0:
                    pe.wait_ge(sem("ev_v"), NT9 * h + NT9)
                    pe.wait_ge(sem("ev_a"), NT9 * h + NT9)
                if i >= 2:
                    pe.wait_ge(sem("kk_read"), 5 * h + i - 1)
                for t in ((2 * i, 2 * i + 1) if i < 4 else (NCH,)):
                    n = tokens[t][1]
                    pe.wait_ge(sem("back_read"), NT9 * h + t + 1)
                    o = (2 * P * (t % 2)) if i < 4 else 0
                    ins = PE.matmul(work[i % 2][0:n, o:o + 2 * n].rearrange("p (x i) -> p x i", x=2), turned[:, t, 0, 0:n], turned[:, t, 0:2, 0:n], start=True, stop=True)
                ins.then_inc(sem("kk_done"), 1)
                if i in (1, 3):
                    fill_parts(24 + i // 2, 25 + i // 2)
            fill_parts(26, 27)
            pe.wait_ge(sem("at_made"), h + 2)
            apart(pe)
            PE.transpose(work[2][0:TS, 0:TS], at[0:TS, NCH, 0:TS], ident[0:TS, 0:TS]).then_inc(sem("s8"), 1)
            fill_parts(27, 28)
            pe.wait_ge(sem("s8_read"), 2 * h + 1)
            apart(pe)
            PE.matmul(work[3][0:TS, 0:TS], small8[:, 0], at[0:TS, NCH, 0:TS], start=True, stop=True).then_inc(sem("s8"), 1)
            fill_parts(28, 29)
            pe.wait_ge(sem("s8_read"), 2 * h + 2)
            apart(pe)
            PE.matmul(work[2][0:TS, 0:TS], small8[:, 0], small8[:, 1], start=True, stop=True).then_inc(sem("s8"), 1)
            fill_parts(29, 72)
            pe.wait_ge(sem("tinv_in"), 16 * h + 32)
            for half in range(2):
                for q in range(4):
                    ins = PE.transpose(work[half][:, P * q:P * q + P], t_all[:, 4 * half + q], ident[:, :])
                ins.then_inc(sem("tt_done"), 1)
            for s in range(3):
                pe.wait_ge(sem("lvl_made"), 3 * h + s + 1)
                for half in range(2):
                    pe.wait_ge(sem("tt_set"), 8 * h + 2 * s + half + 1)
                    if s >= 1:
                        pe.wait_ge(sem("y_read"), 6 * h + 2 * (s - 1) + half + 1)
                    for q in range(4):
                        ins = PE.matmul(work[half][:, P * q:P * q + P], at_lvl[s][:, 4 * half + q], t_all[:, 4 * half + q], start=True, stop=True)
                    ins.then_inc(sem("y_done"), 1)
                fill_parts(72 + 2 * s, 73 + 2 * s)
                for half in range(2):
                    pe.wait_ge(sem("y_read"), 6 * h + 2 * s + half + 1)
                    for q in range(4):
                        if s < 2:
                            PE.matmul(work[2 + half][:, P * q:P * q + P], tt_all[:, 4 * half + q], y_all[:, 4 * half + q], start=True, stop=True)
                    for q in range(4):
                        ins = PE.matmul(work[half][:, P * q:P * q + P], y_all[:, 4 * half + q], tt_all[:, 4 * half + q], start=True, stop=True)
                    ins.then_inc(sem("z_done"), 1)
                fill_parts(73 + 2 * s, 74 + 2 * s)
            for i in range(3):
                pe.wait_ge(sem("tt_set"), 8 * h + 8)
                for t in range(4 * i, min(4 * i + 4, NT9)):
                    n = tokens[t][1]
                    ins = PE.matmul(work[i][:, P * (t % 4):P * (t % 4) + n], kbg[0:n, t], tt_all[0:n, t, 0:n], start=True, stop=True)
                ins.then_inc(sem("nw_done"), 1)
            scanned = (80, 83, 86, 88, 90, 92, 94, 96)
            pe.wait_ge(sem("nw_made"), 3 * h + 3)
            for t in range(NCH):
                if t >= 2:
                    pe.wait_ge(sem("v_read"), NT9 * h + t - 1)
                ins = PE.matmul(work[t % 2][:, 0:P], tt_all[:, t], vb[:, t], start=True, stop=(t == 0))
                if t:
                    fill_parts(scanned[t - 1], scanned[t - 1] + 1)
                    pe.wait_ge(sem("s_new"), NCH * h + t)
                    ins = PE.matmul(work[t % 2][:, 0:P], nw[:, P * t:P * t + P], state[:, (t - 1) % 2], start=False, stop=True)
                ins.then_inc(sem("v_done"), 1)
                fill_parts(scanned[t - 1] + 1 if t else 78, scanned[t])
                pe.wait_ge(sem("v_read"), NT9 * h + t + 1)
                PE.matmul(work[4][:, 0:P], kd[:, t], vnew[:, t % 2], start=True, stop=True).then_inc(sem("sn_done"), 1)
                if t >= 2:
                    pe.wait_ge(sem("o_read"), NT9 * h + t - 1)
                o = work[2 + t % 2][:, 0:P]
                if t:
                    PE.matmul(o, turned[:, t, 2], state[:, (t - 1) % 2], start=True, stop=False)
                PE.matmul(o, qk_t[:, t], vnew[:, t % 2], start=(t == 0), stop=True).then_inc(sem("o_done"), 1)
            pe.wait_ge(sem("smp_made"), 3 * h + 3)
            pe.wait_ge(sem("s0_loaded"), 16 * h + 16)
            pe.wait_ge(sem("v_read"), NT9 * h + NCH - 1)
            apart(pe)
            PE.matmul(work[0][0:TS, 0:P], tt_all[0:TS, NCH, 0:TS], vb[0:TS, NCH], start=True, stop=False)
            for b in range(NSEQ):
                ins = PE.matmul(work[0][0:TS, 0:P], wm[:, b], s0[:, b], start=False, stop=(b == NSEQ - 1))
            ins.then_inc(sem("v_done"), 1)
            pe.wait_ge(sem("o_read"), NT9 * h + NCH)
            for b in range(NSEQ):
                PE.matmul(work[2][0:TS, 0:P], qm[:, b], s0[:, b], start=(b == 0), stop=False)
            pe.wait_ge(sem("v_read"), NT9 * h + NT9)
            apart(pe)
            PE.matmul(work[2][0:TS, 0:P], qk_t[0:TS, NCH, 0:TS], vnew[0:TS, 0], start=False, stop=True).then_inc(sem("o_done"), 1)
            pe.wait_ge(sem("s_new"), NCH * h + NCH)
            for i in range(2):
                for b in range(4):
                    ins = PE.matmul(work[3 + i][:, P * b:P * b + P], kdm[:, 4 * i + b], vnew[0:TS, 0], start=True, stop=True)
                ins.then_inc(sem("s0_done"), 1)
            job(pe, N_HEAD, N_HEAD + 8 + 8 * h, 0)
            pe.wait_ge(sem("o_normed"), h + 1)
            for i in range(3):
                for t in range(4 * i, min(4 * i + 4, NT9)):
                    n = tokens[t][1]
                    ins = PE.transpose(work[i][:, P * (t % 4):P * (t % 4) + n], o_raw[0:n, t], ident[0:n, 0:n])
                ins.then_inc(sem("o_turned"), 1)

        def back(pe, h, t):
            n = tokens[t][1]
            pe.wait_ge(sem("ev_v"), NT9 * h + t + 1)
            pe.wait_ge(sem("ev_a"), NT9 * h + t + 1)
            if t == 0:
                pe.wait_ge(sem("mean"), NT9 + 2 * h + 1)
            else:
                pe.wait_ge(sem("back_read"), NT9 * h + t)
            if t == NCH:
                apart(pe)
            for x in range(3):
                ins = PE.transpose(work[4][:, P * x:P * x + n], tok3[0:n, t % 2, x], ident[0:n, 0:n])
            ins.then_inc(sem("back"), 1)

        def head_stored(sp):
            sp.wait_ge(sem("oa_stored"), 16 * NH + 1)
            sp.wait_ge(sem("s0_stored"), 16 * NH + 1)
            sp.wait_ge(sem("state_stored"), 16 * NH + 1)
            sp.wait_ge(sem("tails_stored"), 96 * NH + 1)
            sp.wait_ge(sem("cache_out"), 48 * NH)
            for s in range(2):
                sp.wait_ge(sem(f"stored{s}"), 16 * 6 * NH + 1)


        sc_att = ExitStack()
        aq = sb("aq", [P, 4, T], F32, sc_att)
        raw = sb("raw", [P, 3, T], F32, sc_att)
        q_scale = sb("q_scale_sb", [P, 2], F32, sc_att)
        kvt = sb("kvt", [P, NCH, 2, P], F32, sc_att)
        kvs = sb("kvs", [TS, 2, P], F32, sc_att)
        bias_p, bias_s = sb("bias_p_sb", [P, 2, 2 * P], F32, sc_att), sb("bias_s_sb", [2 * TS, PAST + TS], F32, sc_att)
        cache = sb("cache", [P, NSEQ, 2, 2, P], F32, sc_att)
        kct = sb("kct", [P, NSEQ, PAST], F32, sc_att)
        prob = sb("prob", [P, 2, 2, 2 * P], F32, sc_att)
        prob_t = sb("prob_t", [P, 2, 2, 2, P], F32, sc_att)
        att = sb("att", [P, NCH, 2, HB + 2], F32, sc_att)
        q_own, own_q = (sb(n, [P, NSEQ + 1, 2, TS], F32, sc_att) for n in ("q_own", "own_q_sb"))
        prob_s, prob_st = sb("prob_s", [2 * TS, PAST + TS], F32, sc_att), sb("prob_st", [P, 3, 2 * TS], F32, sc_att)
        att_st, att_s = sb("att_st", [P, 2 * TS], F32, sc_att), sb("att_s", [2 * TS, HB + 2], F32, sc_att)
        sc_att.close()
        KV_DMAS, ATT_DMAS = (1, 2, 2), (1, 2, 1)

        def block_of(x, g, n):
            if g == 0:
                return x[:, P * n:P * n + P]
            if g == 1:
                return x[:, n // 2 + 512 * (n % 2):n // 2 + 512 * (n % 2) + 509:4]
            return x[:, n:n + 8 * P - 7:8]

        def keys_of(x, g, n):
            if g == 0:
                return x[:, P * (n - 1):P * (n + 1)]
            return x[:, n // 2:n // 2 + 1021:4]

        def is_wide(g, n):
            return n > 0 if g == 0 else n % 2 == 1 if g == 1 else False

        def ncache(g):
            return min(WIN[g], PAST)

        def before(table, g, i):
            return 16 * (2 * sum(table[:g]) + table[g] * i)

        NFILL, FILL0, SENT0 = (4, 2, 2), (N_ATT, N_ATT + 8, N_ATT + 12), (6 * NH, 6 * NH + 12, 6 * NH + 18)

        def parts_done(g, n):
            return min(24 * NFILL[g], (24, 14)[g > 0] + (5, 3)[g > 0] * n)

        def filled(act, g, i, n):
            for c in range(parts_done(g, n - 1) // KD if n else 0, (parts_done(g, n) if n < 15 else 24 * NFILL[g]) // KD):
                n0, per = FILL0[g], NFILL[g]
                before = SENT0[g] + 3 * per // 2 * i
                if g == 0:
                    fill_pair(act, n0, n0 + per * i, NH + i, c, before)
                else:
                    x, t = c // NG, c % NG
                    dst = gb_d[bass.ds(4 * (g - 1) + 2 * i + x, 1)].rearrange("o p t -> (o p) t")
                    fill_out(act, n0 + x, n0 + x + per * i, t, c % 2, before + c // 2, dst)
                if c % NG == NG - 1:
                    j = c // NG + 2
                    split_hi(act, n0 + j, n0 + j + per * i, (n0 + j) // 2 + per // 2 * i + 1)

        def att_sync(sp, g, i, first=False):
            it = 2 * g + i
            for x in range(NFILL[g]):
                if first and x == 2:
                    between_sync(sp)
                load_cols(sp, FILL0[g] + x, FILL0[g] + x + NFILL[g] * i, w_in, pair_cols(NH + i, x) if g == 0 else C_GB + (4 * (g - 1) + 2 * i + x) * P)
            sp.wait_ge(sem("mins"), NCH * it + 1)
            sp.dma_start(bias_p[:], a["bias_p"][g][bass.ds(i, 1)].rearrange("o p e k -> p (o e) k")).then_inc(sem("bias_in"), 16)
            sp.wait_ge(sem("min_s"), it + 1)
            sp.dma_start(bias_s[:], a["bias_s"][g][bass.ds(i, 1)].rearrange("o p k -> (o p) k")).then_inc(sem("bias_in"), 16)
            sp.wait_ge(sem("pv_s"), it + 1)
            apart(sp)
            for n in range(ncache(g) // P):
                for s in range(2):
                    src = a[f"cache_win{g}"][0, :, P * n:P * n + P, s].rearrange("b p h d -> p b (h d)")[:, :, bass.ds(i * P, P)]
                    sp.dma_start(cache[:, :, n, s], src).then_inc(sem("cache_in"), 16)
            sp.wait_ge(sem("aq_set"), 2 * it + 2)
            sp.wait_ge(sem("akv_set"), 2 * it + 2)
            apart(sp)
            if g == 1:
                for s in range(2):
                    sp.wait_ge(sem(f"stored{s}"), 16 * SENT0[1] + 1)
            nxt = it + 1 if g < 2 else 5 - i
            sp.dma_start(raw[:], qkv_d[bass.ds(nxt, 1)].rearrange("o x p t -> p (o x) t")).then_inc(sem("raw_in"), 16)

        def att_pool(pool, g, i):
            it = 2 * g + i
            pool.wait_ge(sem("aq_set"), 2 * it + 2)
            pool.wait_ge(sem("s_smp"), it + 1)
            pool.wait_ge(sem("own_in"), 32)
            G.tensor_tensor(q_own[:], aq[:, 0:2, TP:T].rearrange("p (o e) t -> p o e t", o=1).to_broadcast([P, NSEQ + 1, 2, TS]), own_q[:], ALU.mult).then_inc(sem("q_own"), 1)
            for j in range(NFILL[g]):
                split_lo(pool, FILL0[g] + j, FILL0[g] + j + 2 + NFILL[g] * i)

        def att_scalar(act, g, i):
            it = 2 * g + i
            act.wait_ge(sem("raw_in"), 16 * it + 16)
            act.wait_ge(sem("s_smp"), it + 1)
            act.wait_ge(sem("q_own"), it + 1)
            for e in range(2):
                A.activation(aq[:, e], raw[:, 0], ACT.Copy, scale=q_scale[:, e:e + 1]).then_inc(sem("aq_set"), 1)
            act.wait_ge(sem("kv_stored"), before(KV_DMAS, g, i) + 1)
            act.wait_ge(sem("kvs_stored"), 32 * it + 1)
            for n in range(NCH):
                act.wait_ge(sem("kv_done"), NCH * it + n + 1)
                A.activation(kvt[:, n], work[4][:, 0:2 * P].rearrange("p (s d) -> p s d", s=2), ACT.Copy).then_inc(sem("kv_read"), 1)
                act.wait_ge(sem("mins"), NCH * it + n + 2)
                w = 2 * P if is_wide(g, n) else P
                for e in range(2):
                    ins = A.activation(prob[:, n % 2, e, 0:w], prob[:, n % 2, e, 0:w], ACT.Exp, scale=-1.0, bias=att[:, n, e, HB + 1:HB + 2],
                                       accum_out=att[:, n, e, HB:HB + 1])
                ins.then_inc(sem("exps"), 1)
                filled(act, g, i, n)
            cols = bass.ds(i * P, P)
            win = a[f"win{g}_p"][0, 0].rearrange("t s h d -> t s (h d)")
            act.wait_ge(sem("kv_read"), NCH * it + NCH)
            if g == 0:
                act.dma_start(win[:, :, cols], kvt[:, NCH - 1]).then_inc(sem("kv_stored"), 16)
            elif g == 1:
                for s in range(2):
                    act.dma_start(win.rearrange("(p r) s x -> p r s x", r=4)[:, :, s, cols], kvt[:, 1:NCH:2, s]).then_inc(sem("kv_stored"), 16)
            else:
                for s in range(2):
                    act.dma_start(win.rearrange("(p n) s x -> p n s x", n=NCH)[:, :, s, cols], kvt[:, :, s]).then_inc(sem("kv_stored"), 16)
            act.wait_ge(sem("kvs_done"), it + 1)
            A.activation(kvs[:], work[4][0:TS, 0:2 * P].rearrange("p (s d) -> p s d", s=2), ACT.Copy).then_inc(sem("kvs_read"), 1)
            for c in range(2 * (ncache(g) // P)):
                act.wait_ge(sem("kct_done"), (0, 4, 12)[g] + 2 * (ncache(g) // P) * i + c + 1)
                A.activation(kct_part(g, c), work[c % 2][:].rearrange("p (b k) -> p b k", k=ncache(g)), ACT.Copy).then_inc(sem("kct_read"), 1)
            filled(act, g, i, 8)
            act.wait_ge(sem("kvs_read"), it + 1)
            nc_ = ncache(g) if g else WIN[0] - TSEQ
            for s in range(2):
                dst = a[f"win{g}_s"][0].rearrange("b t s h d -> b t s (h d)")[:, nc_:nc_ + TSEQ, s, cols]
                act.dma_start(dst, kvs[:, s]).then_inc(sem("kvs_stored"), 16)
            act.wait_ge(sem("min_s"), it + 2)
            w = ncache(g) + TS
            A.activation(prob_s[:, 0:w], prob_s[:, 0:w], ACT.Exp, scale=-1.0, bias=att_s[:, HB + 1:HB + 2], accum_out=att_s[:, HB:HB + 1]).then_inc(sem("exp_s"), 1)
            act.wait_ge(sem("o_read_t"), NCH * it + NCH)
            heads = bass.ds(2 * i, 2)
            out = att_d[g, 0:TP, heads]
            if g == 0:
                act.dma_start(out.rearrange("(n p) h x -> p n h x", p=P), att[:]).then_inc(sem("att_stored"), 16)
            elif g == 1:
                for b in range(2):
                    act.dma_start(out.rearrange("(b p r) h x -> b p r h x", b=2, r=4)[b], att[:, b:NCH:2]).then_inc(sem("att_stored"), 16)
            else:
                act.dma_start(out.rearrange("(p n) h x -> p n h x", n=NCH), att[:]).then_inc(sem("att_stored"), 16)
            for n in range(9, 16):
                filled(act, g, i, n)
            act.wait_ge(sem("att_s_done"), it + 1)
            for e in range(2):
                act.dma_start(att_d[g, TP:T, bass.ds(2 * i + e, 1)].rearrange("t o x -> t (o x)"), att_s[TS * e:TS * e + TS]).then_inc(sem("att_s_stored"), 16)

        def kct_part(g, c):
            m = 512 // ncache(g)
            return kct[:, m * c:m * c + m, 0:ncache(g)]

        def att_vector(dve, g, i):
            it = 2 * g + i
            dve.wait_ge(sem("raw_in"), 16 * it + 16)
            dve.wait_ge(sem("s_smp"), it + 1)
            dve.wait_ge(sem("oa_ready"), NH)
            for s in range(2):
                V.tensor_copy(aq[:, 2 + s], raw[:, 1 + s]).then_inc(sem("akv_set"), 1)
            dve.wait_ge(sem("bias_in"), 32 * it + 32)
            dve.wait_ge(sem("att_stored"), before(ATT_DMAS, g, i) + 1)
            dve.wait_ge(sem("att_s_stored"), 32 * it + 1)
            for n in range(NCH + 1):
                if n >= 1:
                    w = is_wide(g, n - 1) + 1
                    dve.wait_ge(sem("pt_done"), NCH * it + n)
                    V.tensor_copy(prob_t[:, n % 2, :, 0:w], work[2][:].rearrange("p (e k q) -> p e k q", e=2, k=2)[:, :, 0:w]).then_inc(sem("pt_read"), 1)
                if n < NCH:
                    dve.wait_ge(sem("scores"), NCH * it + n + 1)
                    apart(dve)
                    w = 2 * P if is_wide(g, n) else P
                    for e in range(2):
                        ins = V.tensor_tensor_reduce(prob[:, n % 2, e, 0:w], work[n % 2][:, 2 * P * e:2 * P * e + w], bias_p[:, e, 2 * P - w:2 * P],
                                                     1.0, 3e38, ALU.add, ALU.min, att[:, n, e, HB + 1:HB + 2])
                    ins.then_inc(sem("mins"), 1)
                if n >= 1:
                    dve.wait_ge(sem("pv_done"), NCH * it + n)
                    V.tensor_copy(att[:, n - 1, :, 0:HB], work[3][:, 0:2 * HB].rearrange("p (e d) -> p e d", e=2)).then_inc(sem("o_read_t"), 1)
            dve.wait_ge(sem("s_smp"), it + 2)
            apart(dve)
            w = ncache(g) + TS
            V.tensor_tensor_reduce(prob_s[:, 0:w], work[2][0:2 * TS, 0:w], bias_s[:, 0:w], 1.0, 3e38, ALU.add, ALU.min,
                                   att_s[:, HB + 1:HB + 2]).then_inc(sem("min_s"), 1)
            dve.wait_ge(sem("pt_s"), it + 1)
            for n in range(ncache(g) // P):
                V.tensor_copy(prob_st[:, n], work[3][:, 64 * n:64 * n + 64])
            V.tensor_copy(prob_st[0:TS, 2], work[3][0:TS, 128:192]).then_inc(sem("pt_s_read"), 1)
            dve.wait_ge(sem("pv_s"), it + 2)
            V.tensor_copy(att_st[:], work[4][:, 0:2 * TS]).then_inc(sem("st_part"), 1)
            dve.wait_ge(sem("st_part"), it + 1)
            V.tensor_tensor(att_st[:], att_st[:], work[4][:, 2 * TS:4 * TS], ALU.add).then_inc(sem("st_read"), 1)
            dve.wait_ge(sem("st_turned"), it + 1)
            for e in range(2):
                ins = V.tensor_copy(att_s[TS * e:TS * e + TS, 0:HB], work[2][TS * e:TS * e + TS, HB * e:HB * e + HB])
            ins.then_inc(sem("att_s_done"), 1)

        def att_tensor(pe, g, i):
            it = 2 * g + i
            def fill_parts(n):
                for p in range(parts_done(g, n - 1) if n else KD, parts_done(g, n) if n < 15 else 24 * NFILL[g]):
                    part(pe, FILL0[g] + p // 24, FILL0[g] + p // 24 + NFILL[g] * i, p % 24)
            fill_parts(0)
            pe.wait_ge(sem("akv_set"), 2 * it + 2)
            for n in range(NCH + 1):
                if n < NCH:
                    if n >= 1:
                        pe.wait_ge(sem("kv_read"), NCH * it + n)
                    for s in range(2):
                        ins = PE.transpose(work[4][:, P * s:P * s + P], block_of(aq[:, 2 + s], g, n), ident[:, :])
                    ins.then_inc(sem("kv_done"), 1)
                if n >= 1:
                    m = n - 1
                    pe.wait_ge(sem("exps"), NCH * it + m + 1)
                    for e in range(2):
                        for kb in range(is_wide(g, m) + 1):
                            ins = PE.transpose(work[2][:, 2 * P * e + P * kb:2 * P * e + P * kb + P], prob[:, m % 2, e, P * kb:P * kb + P], ident[:, :])
                    ins.then_inc(sem("pt_done"), 1)
                if n < NCH:
                    if n == 0:
                        pe.wait_ge(sem("aq_set"), 2 * it + 2)
                    w = 2 * P if is_wide(g, n) else P
                    for e in range(2):
                        k = keys_of(aq[:, 2], g, n) if is_wide(g, n) else block_of(aq[:, 2], g, n)
                        ins = PE.matmul(work[n % 2][:, 2 * P * e:2 * P * e + w], block_of(aq[:, e], g, n), k, start=True, stop=True)
                    ins.then_inc(sem("scores"), 1)
                if n < NCH:
                    fill_parts(n + 1)
                if n >= 1:
                    pe.wait_ge(sem("pt_read"), NCH * it + m + 1)
                    pe.wait_ge(sem("kv_read"), NCH * it + m + 1)
                    if m >= 1:
                        pe.wait_ge(sem("o_read_t"), NCH * it + m)
                    nk = is_wide(g, m) + 1
                    for e in range(2):
                        for kb in range(nk):
                            ins = PE.matmul(work[3][:, HB * e:HB * e + HB], prob_t[:, n % 2, e, kb], kvt[:, m + kb - nk + 1, 1, HB * e:HB * e + HB],
                                            start=(kb == 0), stop=(kb == nk - 1))
                    ins.then_inc(sem("pv_done"), 1)
            for s in range(2):
                ins = PE.transpose(work[4][0:TS, P * s:P * s + P], aq[:, 2 + s, TP:T], ident[:, :])
            ins.then_inc(sem("kvs_done"), 1)
            nt = ncache(g) // P
            pe.wait_ge(sem("cache_in"), (0, 64, 192)[g] + 32 * nt * (i + 1))
            for c in range(2 * nt):
                if c >= 2:
                    pe.wait_ge(sem("kct_read"), (0, 4, 12)[g] + 2 * nt * i + c - 1)
                for q in range(4):
                    b, n = (4 * c + q) // nt, (4 * c + q) % nt
                    ins = PE.transpose(work[c % 2][:, P * q:P * q + P], cache[:, b, n, 0], ident[:, :])
                ins.then_inc(sem("kct_done"), 1)
            fill_parts(9)
            pe.wait_ge(sem("kct_read"), (0, 4, 12)[g] + 2 * nt * (i + 1))
            pe.wait_ge(sem("q_own"), it + 2)
            w = ncache(g)
            for b in range(NSEQ):
                PE.matmul(work[2][0:2 * TS, 0:w], q_own[:, b], kct[:, b, 0:w], start=(b == 0), stop=(b == NSEQ - 1))
            PE.matmul(work[2][0:2 * TS, w:w + TS], q_own[:, NSEQ], aq[:, 2, TP:T], start=True, stop=True).then_inc(sem("s_smp"), 1)
            for n in range(10, 12):
                fill_parts(n)
            pe.wait_ge(sem("exp_s"), it + 1)
            apart(pe)
            for n in range(nt):
                PE.transpose(work[3][:, 64 * n:64 * n + 64], prob_s[:, P * n:P * n + P], ident[0:2 * TS, 0:2 * TS])
            PE.transpose(work[3][0:TS, 128:192], prob_s[:, w:w + TS], ident[0:2 * TS, 0:2 * TS]).then_inc(sem("pt_s"), 1)
            for n in range(12, 14):
                fill_parts(n)
            pe.wait_ge(sem("pt_s_read"), it + 1)
            pe.wait_ge(sem("kvs_read"), it + 1)
            for b in range(NSEQ):
                def of_seq(x):
                    return x.rearrange("p (e b q) -> p e b q", e=2, q=TSEQ)[:, :, b]
                for n in range(nt):
                    PE.matmul(of_seq(work[4][:, 0:2 * TS]), cache[:, b, n, 1], of_seq(prob_st[:, n]), start=(n == 0), stop=(n == nt - 1))
            ins = PE.matmul(work[4][:, 2 * TS:4 * TS], kvs[:, 1], prob_st[0:TS, 2], start=True, stop=True)
            ins.then_inc(sem("pv_s"), 1)
            for n in range(14, 16):
                fill_parts(n)
            pe.wait_ge(sem("st_read"), it + 1)
            apart(pe)
            PE.transpose(work[2][0:2 * TS, 0:P], att_st[:], ident[:, :]).then_inc(sem("st_turned"), 1)
            job(pe, FILL0[g], FILL0[g] + NFILL[g] + NFILL[g] * i, 0)


        def between_sync(sp):
            sp.wait_ge(sem("o_normed"), NH)
            sp.dma_start(raw[:], qkv_d[0].rearrange("x p t -> p x t")).then_inc(sem("raw_in"), 16)
            sp.dma_start(q_scale[:], a["q_scale"]).then_inc(sem("own_in"), 16)
            sp.dma_start(own_q[:], a["own_q"]).then_inc(sem("own_in"), 16)
            head_stored(sp)

        def between_scalar(act):
            act.wait_ge(sem("oa_ready"), NH)
            act.wait_ge(sem("own_in"), 32)

        def att_end(sp):
            sp.wait_ge(sem("kv_stored"), 16 * 2 * sum(KV_DMAS) + 1)
            sp.wait_ge(sem("kvs_stored"), 32 * 6 + 1)
            sp.wait_ge(sem("att_stored"), 16 * 2 * sum(ATT_DMAS) + 1)
            sp.wait_ge(sem("att_s_stored"), 32 * 6 + 1)
            sp.wait_ge(sem("raw_in"), 16 * 7)

        sc_e = ExitStack()
        ones_all = sb("ones_all", [P, P], F32, sc_e)
        x1 = sb("x1", [P, KD, T], F32, sc_e)
        sc_c = ExitStack()
        oaH, oaL = sb("oaH", [P, NH, T], F32R, sc_c), sb("oaL", [P, NH, T], F32R, sc_c)
        obH, obL = sb("obH", [P, 2, T], F32R, sc_c), sb("obL", [P, 2, T], F32R, sc_c)
        prod = sb("prod", [P, 2, 3, NHB * HB], F32, sc_c)
        gates = sb("gates", [P, 2, 2, T], F32, sc_c)
        summed = sb("summed", [P, NG, 2, TN], F32, sc_c)
        sc_c.close()
        flat, n_st, n_gh = x1[:].rearrange("p k t -> p (k t)"), NT9 * 3 * NHB * (HB + 2), NT9 * 3 * NHB
        share, part_den = (flat[:, n_st + n_gh * x:n_st + n_gh * (x + 1)].rearrange("p (t g h) -> p t g h", t=NT9, g=3) for x in range(2))
        low = flat[:, n_st + 2 * n_gh:n_st + 2 * n_gh + NT9 * NHB].rearrange("p (t h) -> p t h", t=NT9)
        st = flat[:, 0:n_st].rearrange(
            "p (t g h x) -> p t g h x", t=NT9, g=3, h=NHB)
        oa_in = gates[:].rearrange("p a b t -> p (a b) t")
        ga_last = summed[:].rearrange("p g a t -> p (g a t)").rearrange("p (s t) -> p s t", s=2)
        sc_u = ExitStack()
        gH, gL = sb("gH", [P, KD, T], F32R, sc_u), sb("gL", [P, KD, T], F32R, sc_u)
        room = sb("room", [P, 3 * T + NT9 * P - T], F32, sc_u)
        sc_u.close()
        uH, uL = hH, hL
        xcol = room[:, 0:NT9 * P].rearrange("p (t d) -> p t d", d=P)
        sq_in, sq_sum = room[:, NT9 * P:NT9 * P + T], room[:, NT9 * P + T:NT9 * P + 2 * T]
        uf, relu = (room[:, T * x:T * x + T].rearrange("p (g t) -> p g t", g=NG) for x in range(2))
        rms2 = sq_sum.rearrange("p (g t) -> p g t", g=NG)
        sq2_in = relu.rearrange("p g t -> p (g t)")
        sc_y = ExitStack()
        y, fnorm = sb("y", [P, 4, D], F32, sc_y), sb("fnorm", [P, D], F32, sc_y)
        ry = sb("ry", [P, NT9], F32, sc_y)
        sc_y.close()
        y_sems = (("stored0", 16 * 48 + 1), ("stored1", 16 * 48 + 1), ("gates_in0", 256), ("gates_in1", 256))
        sc_e.close()

        def end_sync(sp):
            for j in range(2):
                load_cols(sp, N_GA + j, N_GA + j, w_in, C_GA + (6 + j) * P)
            sp.dma_start(oa_in, oa_d.rearrange("k p t -> p k t")).then_inc(sem("oa_loaded"), 16)

            def branch_w(i, j):
                load_w(sp, N_BR + j, N_BR + j + 2 * i, lambda raw: [
                    (raw[:, 0:NH], a["w_br_a"][0].rearrange("(k p) n -> p k n", p=P)[:, :, bass.ds((2 * i + j) * P, P)]),
                    (raw[:, NH:NH + 2], a["w_br_b"][0].rearrange("(k p) n -> p k n", p=P)[:, :, bass.ds((2 * i + j) * P, P)])])

            for j in range(2):
                branch_w(0, j)
            att_end(sp)
            sp.wait_ge(sem("zeroed"), 8)
            for g in range(3):
                sp.dma_start(st[:, 0:NCH, g], att_d[g, 0:TP].rearrange("(t p) h x -> p t h x", p=P)).then_inc(sem("st_loaded"), 16)
            sp.dma_start(st[0:TS, NCH], att_d[:, TP:T].rearrange("g t h x -> t g h x")).then_inc(sem("st_loaded"), 16)
            def branch_gates(i, j):
                b = 2 * i + j
                sp.wait_ge(sem("summed"), 3 * b + 3)
                for x, src in enumerate((ga_d, gb_d)):
                    sp.dma_start(gates[:, j, x], src[bass.ds(b, 1)].rearrange("o p t -> (o p) t")).then_inc(sem(f"gates_in{j}"), 16)
            for j in range(2):
                sp.wait_ge(sem("ga_last"), 3 * j + 3)
                sp.dma_start(ga_d[6 + j], ga_last[:, j]).then_inc(sem("gate_stored"), 16)
            sp.wait_ge(sem("gate_stored"), 32 + 1)
            for s in range(2):
                sp.wait_ge(sem(f"stored{s}"), 16 * 48 + 1)
            sp.wait_ge(sem("oa_split"), 2)
            with sp.Fori(0, KD // 2 - 1) as i:
                for j in range(2):
                    branch_gates(i, j)
                    branch_w(i + 1, j)
            for j in range(2):
                branch_gates(KD // 2 - 1, j)
            w_out = a["w_out"][0].rearrange("(k p) n -> p k n", p=P)
            with sp.Fori(0, KD // 2) as i:
                for j in range(2):
                    n0, o = N_OUT + j, 2 * i + j
                    load_cols(sp, n0, n0 + 2 * i, w_out, o * P)
                    sp.wait_ge(sem("h_lo"), 42)
                    sp.wait_ge(sem("x_cols"), 3 * o + 1)
                    sp.dma_start(xcol[:, 0:NCH], a["x_prompt"][0].rearrange("(t p) d -> p t d", p=P)[:, :, bass.ds(o * P, P)]).then_inc(sem(f"gates_in{j}"), 16)
                    sp.dma_start(xcol[0:TS, NCH], a["x_sample"].rearrange("b t d -> (b t) d")[:, bass.ds(o * P, P)]).then_inc(sem(f"gates_in{j}"), 16)
            w_up, w_down = (a[n][0].rearrange("(k p) n -> p k n", p=P) for n in ("w_up", "w_down"))
            with sp.Fori(0, 4) as q:
                for m in range(8):
                    load_cols(sp, N_MLP + m, N_MLP + m + 16 * q, w_up, q * D + m * P)
                for m in range(8):
                    load_w(sp, N_MLP + 8 + m, N_MLP + 8 + m + 16 * q, lambda raw: [
                        (raw, w_down[:, bass.ds(q * KD, KD), m * P:m * P + P])])
            done(sp, N_MLP + 55, 2)
            sp.dma_start(fnorm[:], a["final_norm"].rearrange("(o d) -> o d", o=1).to_broadcast([P, D])).then_inc(sem("st_loaded"), 16)
            for t, (c, n) in enumerate(tokens):
                sp.wait_ge(sem("y_made"), t + 1)
                dst = a["y_prompt"][0, c:c + n] if t < NCH else a["y_sample"].rearrange("b t d -> (b t) d")
                sp.dma_start(dst, y[0:n, t % 4]).then_inc(sem(y_sems[t % 4][0]), 16)
            for x, (name, before) in enumerate(y_sems):
                sp.wait_ge(sem(name), before + 16 * len(range(x, NT9, 4)))

        def end_pool(pool):
            pool.sem_inc(sem("summed"), 6)
            pool.sem_inc(sem("x_cols"), 1)
            pool.sem_inc(sem("x1_made"), 6)
            pool.sem_inc(sem("u_lo"), 3)
            att_end(pool)
            G.memset(ones_all[:], 1.0).then_inc(sem("zeroed"), 1)
            G.memset(st[:, NCH], 1.0).then_inc(sem("zeroed"), 1)
            split_lo(pool, N_BR, N_BR, 6)
            for x in range(2):
                pool.wait_ge(sem("oa_hi"), x + 1)
                G.tensor_tensor(oaL[:, 2 * x:2 * x + 2], oa_in[:, 2 * x:2 * x + 2], oaH[:, 2 * x:2 * x + 2].bitcast(F32), ALU.subtract).then_inc(sem("oa_split"), 1)
            split_lo(pool, N_BR + 1, N_BR + 1, 6)
            with pool.Fori(0, KD // 2) as i:
                for j in range(2):
                    n0, b = N_BR + j, 2 * i + j
                    for t in range(NG):
                        pool.wait_ge(sem("h_hi"), 3 * b + t + 19)
                        cols = slice(TN * t, TN * t + TN)
                        G.tensor_tensor(hL[:, bass.ds(b, 1), cols], summed[:, t:t + 1, 0], hH[:, bass.ds(b, 1), cols].bitcast(F32), ALU.subtract).then_inc(sem("h_lo"), 1)
                    split_lo(pool, n0, n0 + 2 + 2 * i)
            with pool.Fori(0, KD // 2) as i:
                for j in range(2):
                    n0, o = N_OUT + j, 2 * i + j
                    split_lo(pool, n0, n0 + 2 + 2 * i)
                    pool.wait_ge(sem("x1_squared"), o + 2)
                    G.tensor_tensor(sq_sum, sq_sum, sq_in, ALU.add).then_inc(sem("sq_added"), 1)
                    pool.wait_ge(sem("sq_added"), o + 2)

            def group(q, last):
                n0 = N_MLP
                for m in range(8):
                    for t in range(NG):
                        k = 24 * q + 3 * m + t
                        pool.wait_ge(sem("u_hi"), k + 1)
                        cols = slice(TN * t, TN * t + TN)
                        G.tensor_tensor(uL[:, m, cols], uf[:, t], uH[:, m, cols].bitcast(F32), ALU.subtract).then_inc(sem("u_lo"), 1)
                    split_lo(pool, n0 + m, n0 + m + 2 + 16 * q)
                for m in range(8):
                    if not (last and m >= 6):
                        split_lo(pool, n0 + m, n0 + 10 + m + 16 * q)
                    if last and m:
                        pool.wait_ge(sem("x1_squared"), KD + m + 2)
                        G.tensor_tensor(sq_sum, sq_sum, sq2_in, ALU.add).then_inc(sem("sq_added"), 1)
                        pool.wait_ge(sem("sq_added"), KD + m + 1)
            with pool.Fori(0, 3) as q:
                group(q, False)
            group(3, True)

        def end_scalar(act):
            for j in range(2):
                for t in range(NG):
                    done(act, N_GA + j, t)
                    A.activation(ga_last[:, j, TN * t:TN * t + TN], dense[t][:, 0:TN], ACT.Copy).then_inc(sem(f"d_free{t}"), 1)
                for t in range(NG):
                    act.wait_ge(sem(f"d_free{t}"), N_GA + j + 1)
                    act.sem_inc(sem("ga_last"), 1)
                split_hi(act, N_BR + j, N_BR + j, 27 + j, 6)
                if j == 0:
                    act.wait_ge(sem("oa_loaded"), 16)
                    act.wait_ge(sem("zeroed"), 8)
                    for x in range(2):
                        A.activation(oaH[:, 2 * x:2 * x + 2], oa_in[:, 2 * x:2 * x + 2], ACT.Copy).then_inc(sem("oa_hi"), 1)
                    act.wait_ge(sem("share_arg"), 1)
                    A.activation(share, share, ACT.Exp).then_inc(sem("share_exp"), 1)
            for t, (c, n) in enumerate(tokens):
                act.wait_ge(sem("ob_turned"), t + 1)
                A.activation(obH[:, :, c:c + n], work[t % 2][:, 0:2 * P].rearrange("p (k t) -> p k t", k=2)[:, :, 0:n], ACT.Copy).then_inc(sem("ob_hi"), 1)

            def branch(i, last):
                for j in range(2):
                    b = 2 * i + j
                    act.wait_ge(sem(f"gates_in{j}"), 32 * i + 32)
                    A.activation(gates[:, j], gates[:, j], ACT.Sigmoid).then_inc(sem("gates_set"), 1)
                    for t in range(NG):
                        act.wait_ge(sem("summed"), 3 * b + t + 7)
                        A.activation(hH[:, bass.ds(b, 1), TN * t:TN * t + TN], summed[:, t:t + 1, 0], ACT.Copy).then_inc(sem("h_hi"), 1)
                    if last:
                        split_hi(act, N_OUT + j, N_OUT + j, 34 + j)
                    else:
                        split_hi(act, N_BR + j, N_BR + j + 2 + 2 * i, 29 + j + 2 * i, 6)
            with act.Fori(0, KD // 2 - 1) as i:
                branch(i, False)
            branch(KD // 2 - 1, True)
            with act.Fori(0, KD // 2) as i:
                for j in range(2):
                    n0, o = N_OUT + j, 2 * i + j
                    for t in range(NG):
                        done(act, n0 + 2 * i, t)
                        A.activation(x1[:, bass.ds(o, 1), TN * t:TN * t + TN], dense[t][:, 0:TN].rearrange("p (o t) -> p o t", o=1), ACT.Copy).then_inc(sem(f"d_free{t}"), 1)
                    split_hi(act, n0, n0 + 2 + 2 * i, (n0 + 2) // 2 + 5 + i)
                    act.wait_ge(sem("x1_made"), 3 * o + 9)
                    act.wait_ge(sem("sq_added"), o + 1)
                    apart(act)
                    x = x1[:, bass.ds(o, 1)]
                    A.activation(gH[:, bass.ds(o, 1)], x, ACT.Copy, scale=vec[:, bass.ds(NORM2 + o, 1)]).then_inc(sem("h_hi"), 1)
                    A.activation(sq_in, x.rearrange("p o t -> p (o t)"), ACT.Square).then_inc(sem("x1_squared"), 1)

            def group(q, last):
                n0 = N_MLP
                for m in range(8):
                    for t in range(NG + 1):
                        if t < NG:
                            done(act, n0 + m + 16 * q, t)
                            act.wait_ge(sem("u_lo"), 24 * q + 3 * m + t + 1)
                            A.activation(relu[:, t], dense[t][:, 0:TN], ACT.Relu).then_inc(sem(f"d_free{t}"), 1)
                        if t >= 1:
                            act.wait_ge(sem("u_made"), 24 * q + 3 * m + t)
                            done(act, n0 - 1 + 16 * q, t - 1)
                            A.activation(uH[:, m, TN * (t - 1):TN * t], uf[:, t - 1], ACT.Copy).then_inc(sem("u_hi"), 1)
                    split_hi(act, n0 + m, n0 + m + 2 + 16 * q, (n0 + m + 2) // 2 + 5 + 8 * q)
                for m in range(8):
                    if not (last and m >= 6):
                        split_hi(act, n0 + m, n0 + 10 + m + 16 * q, (n0 + m + 10) // 2 + 5 + 8 * q)
                    if last:
                        for t in range(NG):
                            act.wait_ge(sem(f"d_free{t}"), N_MLP + 57 + m)
                        act.wait_ge(sem("sq_added"), KD + max(m, 1))
                        A.activation(sq2_in if m else sq_sum, x1[:, m], ACT.Square).then_inc(sem("x1_squared"), 1)
            act.wait_ge(sem("sq_added"), KD + 1)
            with act.Fori(0, 3) as q:
                group(q, False)
            group(3, True)

            act.wait_ge(sem("mean"), NT9 + 2 * NH + 1)
            A.activation(ry[:, 0:NCH], ry[:, 0:NCH], ACT.Sqrt)
            A.activation(ry[0:TS, NCH:], ry[0:TS, NCH:], ACT.Sqrt).then_inc(sem("root"), 1)

        def end_vector(dve):
            dve.wait_ge(sem("st_loaded"), 64)
            chV.link(dve, V.tensor_tensor(low, st[:, :, 0, :, HB + 1], st[:, :, 1, :, HB + 1], ALU.min))
            chV.link(dve, V.tensor_tensor(low, low, st[:, :, 2, :, HB + 1], ALU.min))
            for g in range(3):
                ins = V.tensor_tensor(share[:, :, g], low, st[:, :, g, :, HB + 1], ALU.subtract)
            ins.then_inc(sem("share_arg"), 1)
            dve.wait_ge(sem("share_exp"), 1)
            for g in range(3):
                ins = V.tensor_tensor(part_den[:, :, g], share[:, :, g], st[:, :, g, :, HB], ALU.mult)
            chV.link(dve, ins)
            chV.link(dve, V.tensor_tensor(low, part_den[:, :, 0], part_den[:, :, 1], ALU.add))
            chV.link(dve, V.tensor_tensor(low, low, part_den[:, :, 2], ALU.add))
            chV.link(dve, V.reciprocal(low, low))
            for g in range(3):
                ins = V.tensor_tensor(share[:, :, g], share[:, :, g], low, ALU.mult)
            chV.link(dve, ins)
            for t in range(NT9 + 1):
                if t < NT9:
                    c, n = tokens[t]
                    if t >= 2:
                        dve.wait_ge(sem("ob_turned"), t - 1)
                    w = share[0:n, t].rearrange("p g (h o) -> p (g h) o", o=1).to_broadcast([n, 3 * NHB, HB])
                    V.tensor_tensor(prod[0:n, t % 2].rearrange("p g (h d) -> p (g h) d", h=NHB),
                                    st[0:n, t].rearrange("p g h x -> p (g h) x")[:, :, 0:HB], w, ALU.mult).then_inc(sem("ob_made"), 1)
                if t >= 1:
                    c, n = tokens[t - 1]
                    dve.wait_ge(sem("ob_hi"), t)
                    V.tensor_tensor(obL[:, :, c:c + n], work[(t - 1) % 2][:, 0:2 * P].rearrange("p (k t) -> p k t", k=2)[:, :, 0:n],
                                    obH[:, :, c:c + n].bitcast(F32), ALU.subtract).then_inc(sem("ob_split"), 1)
            dve.wait_ge(sem("gate_stored"), 32 + 1)
            with dve.Fori(0, KD // 2) as i:
                for j in range(2):
                    n0, b = N_BR + j, 2 * i + j
                    dve.wait_ge(sem("gates_set"), b + 1)
                    for t in range(NG):
                        cols = slice(TN * t, TN * t + TN)
                        done(dve, n0 + 2 * i, t)
                        if j:
                            dve.wait_ge(sem("h_lo"), 3 * b + t + 16)
                        V.tensor_tensor(summed[:, t, 0], dense[t][:, 0:TN], gates[:, j, 0, cols], ALU.mult)
                        V.tensor_tensor(summed[:, t, 1], work[t][:, 0:TN], gates[:, j, 1, cols], ALU.mult).then_inc(sem(f"d_free{t}"), 1)
                        dve.wait_ge(sem(f"d_free{t}"), n0 + 1 + 2 * i)
                        V.tensor_tensor(summed[:, t, 0], summed[:, t, 0], summed[:, t, 1], ALU.add).then_inc(sem("summed"), 1)
                        dve.wait_ge(sem("summed"), 3 * b + t + 7)
                dve.wait_ge(sem("h_lo"), 6 * i + 24)
            V.memset(sq_sum, 0.0).then_inc(sem("x1_squared"), 1)
            cuts = ((0, 384), (384, 384), (768, 288))
            with dve.Fori(0, KD // 2) as i:
                for j in range(2):
                    n0, o = N_OUT + j, 2 * i + j
                    for t in range(NG):
                        dve.wait_ge(sem(f"d_free{t}"), n0 + 1 + 2 * i)
                    for t, (c, n) in enumerate(cuts):
                        dve.wait_ge(sem("x_cols"), 3 * o + t + 2)
                        x = x1[:, bass.ds(o, 1), c:c + n]
                        V.tensor_tensor(x, x, work[t][:, 0:n].rearrange("p (o t) -> p o t", o=1), ALU.add).then_inc(sem("x1_made"), 1)
                    dve.wait_ge(sem("h_hi"), o + 43)
                    V.scalar_tensor_tensor(out=gL[:, bass.ds(o, 1)], in0=x1[:, bass.ds(o, 1)], scalar=vec[:, bass.ds(NORM2 + o, 1)],
                                           in1=gH[:, bass.ds(o, 1)].bitcast(F32), op0=ALU.mult, op1=ALU.subtract).then_inc(sem("h_lo"), 1)
            for t in range(NG):
                dve.wait_ge(sem("sq_total"), t + 1)
                chV.link(dve, V.tensor_scalar(rms2[:, t], work[t][:, 0:TN], 1.0 / D, EPS, ALU.mult, ALU.add))
                chV.link(dve, V.reciprocal(rms2[:, t], rms2[:, t]))

            def group(q):
                for m in range(8):
                    for t in range(NG):
                        dve.wait_ge(sem(f"d_free{t}"), N_MLP + m + 1 + 16 * q)
                        chV.link(dve, V.tensor_tensor(uf[:, t], relu[:, t], relu[:, t], ALU.mult))
                        V.tensor_tensor(uf[:, t], uf[:, t], rms2[:, t], ALU.mult).then_inc(sem("u_made"), 1)
                for m in range(8):
                    for t in range(NG):
                        x = x1[:, m, TN * t:TN * t + TN]
                        done(dve, N_MLP + 8 + m + 16 * q, t)
                        V.tensor_tensor(x, x, dense[t][:, 0:TN], ALU.add).then_inc(sem(f"d_free{t}"), 1)
            chV.rounds(dve, "mlp", 4, group)
            dve.wait_ge(sem("sq_total"), NG + 1)
            V.tensor_scalar(ry[:, 0:NCH], work[4][:, 0:NCH], 1.0 / D, EPS, ALU.mult, ALU.add)
            V.tensor_scalar(ry[0:TS, NCH:], work[4][0:TS, NCH:NT9], 1.0 / D, EPS, ALU.mult, ALU.add).then_inc(sem("mean"), 1)
            dve.wait_ge(sem("root"), NT9 + 2 * NH + 1)
            V.reciprocal(ry[:, 0:NCH], ry[:, 0:NCH])
            chV.link(dve, V.reciprocal(ry[0:TS, NCH:], ry[0:TS, NCH:]))
            dve.wait_ge(sem("st_loaded"), 80)
            for t, (c, n) in enumerate(tokens):
                if t >= 4:
                    name, before = y_sems[t % 4]
                    dve.wait_ge(sem(name), before + 16 * (t // 4))
                for x in range(2):
                    half = slice(512 * x, 512 * x + 512)
                    dve.wait_ge(sem("turned"), 2 * (NT9 + t) + x + 1)
                    ins = V.scalar_tensor_tensor(out=y[0:n, t % 4, half], in0=work[2 * (t % 2) + x][0:n, :], scalar=ry[0:n, t:t + 1], in1=fnorm[0:n, half],
                                                 op0=ALU.mult, op1=ALU.mult)
                ins.then_inc(sem("y_made"), 1)

        def end_tensor(pe):
            for j in range(2):
                for t in range(NG):
                    if j or t:
                        job(pe, N_GA + j, N_GA + j, t)
            for t, (c, n) in enumerate(tokens):
                pe.wait_ge(sem("ob_made"), t + 1)
                if t >= 2:
                    pe.wait_ge(sem("ob_split"), t - 1)
                for k in range(2):
                    for g in range(3):
                        ins = PE.matmul(work[t % 2][:, P * k:P * k + n], prod[0:n, t % 2, g, P * k:P * k + P], ident[0:n, 0:n], start=(g == 0), stop=(g == 2))
                ins.then_inc(sem("ob_turned"), 1)
            pe.wait_ge(sem("ob_split"), NT9)
            pe.wait_ge(sem("oa_split"), 2)
            with pe.Fori(0, KD // 2) as i:
                for j in range(2):
                    n0 = N_BR + j
                    pe.wait_ge(sem("w_split"), n0 + 3 + 2 * i)
                    for t in range(NG):
                        pe.wait_ge(sem(f"d_free{t}"), n0 + 2 * i)
                        product(n0, t, dense[t], oaH, oaL, 0, NH)
                        product(n0, t, work[t], obH, obL, NH, 2).then_inc(sem("d_done"), 1)
            pe.wait_ge(sem("h_lo"), 39)
            with pe.Fori(0, KD // 2) as i:
                for j in range(2):
                    n0, o = N_OUT + j, 2 * i + j
                    for t in range(NG):
                        job(pe, n0, n0 + 2 * i, t, before_last=lambda: pe.wait_ge(sem("h_lo"), 40 + t))
                    pe.wait_ge(sem(f"gates_in{j}"), 32 * i + 160)
                    pe.wait_ge(sem("x1_made"), 3 * o + 6)
                    for t, (c, n) in enumerate(tokens):
                        ins = PE.transpose(work[t // 3][:, P * (t % 3):P * (t % 3) + n], xcol[0:n, t], ident[0:n, 0:n])
                        if t % 3 == 2:
                            ins.then_inc(sem("x_cols"), 1)
            pe.wait_ge(sem("h_lo"), 42 + KD - 1)
            for t in range(NG):
                job(pe, N_MLP, N_MLP, t, gH, gL, before_last=lambda: pe.wait_ge(sem("h_lo"), 42 + KD))
                if t == 1:
                    pe.wait_ge(sem("sq_added"), KD + 1)
                    pe.wait_ge(sem("x1_made"), 3 * KD + 6)
                    for x in range(NG):
                        PE.matmul(work[x][:, 0:TN], ones_all[:, :], sq_sum[:, TN * x:TN * x + TN], start=True, stop=True).then_inc(sem("sq_total"), 1)

            def group(q, first):
                for m in range(first, 8):
                    for t in range(NG):
                        job(pe, N_MLP + m, N_MLP + m + 16 * q, t, gH, gL)
                for m in range(8):
                    for t in range(NG):
                        if m == 0:
                            pe.wait_ge(sem("u_lo"), 24 * q + 25 + t)
                        job(pe, N_MLP + 8 + m, N_MLP + 8 + m + 16 * q, t)
            group(0, 1)
            with pe.Fori(0, 3) as q:
                group(q + 1, 0)
            for t in range(NG):
                pe.wait_ge(sem(f"d_free{t}"), N_MLP + 64)
            for t, (c, n) in enumerate(tokens):
                if t == 2:
                    pe.wait_ge(sem("sq_added"), 2 * KD)
                    for x, (cx, nx) in enumerate(tokens):
                        ins = PE.matmul(work[4][0:nx, x:x + 1], sq_sum[:, cx:cx + nx], ones[:, 0:1], start=True, stop=True)
                    ins.then_inc(sem("sq_total"), 1)
                if t >= 2:
                    pe.wait_ge(sem("y_made"), t - 1)
                for x in range(2):
                    for k in range(4):
                        ins = PE.transpose(work[2 * (t % 2) + x][0:n, P * k:P * k + P], x1[:, 4 * x + k, c:c + n], ident[:, :])
                    ins.then_inc(sem("turned"), 1)

        block = ctx.enter_context(nc.Block())

        @block.sync
        def _(sp):
            start_sync(sp)
            ab_sync(sp)
            head_sync(sp, 0, first=True)
            with sp.Fori(1, NH) as h:
                head_sync(sp, h)
            att_sync(sp, 0, 0, first=True)
            att_sync(sp, 0, 1)
            for g in range(1, 3):
                with sp.Fori(0, 2) as i:
                    att_sync(sp, g, i)
            end_sync(sp)

        @block.gpsimd
        def _(pool):
            start_pool(pool)
            ab_pool(pool)
            chG.rounds(pool, "heads", NH, lambda h: head_pool(pool, h))
            for g in range(3):
                chG.rounds(pool, f"attention {g}", 2, lambda i: att_pool(pool, g, i))
            end_pool(pool)

        @block.scalar
        def _(act):
            start_scalar(act)
            ab_scalar(act)
            chA.rounds(act, "heads", NH, lambda h: head_scalar(act, h))
            between_scalar(act)
            for g in range(3):
                chA.rounds(act, f"attention {g}", 2, lambda i: att_scalar(act, g, i))
            end_scalar(act)

        @block.vector
        def _(dve):
            start_vector(dve)
            ab_vector(dve)
            chV.rounds(dve, "heads", NH, lambda h: head_vector(dve, h))
            for g in range(3):
                chV.rounds(dve, f"attention {g}", 2, lambda i: att_vector(dve, g, i))
            end_vector(dve)

        @block.tensor
        def _(pe):
            start_tensor(pe)
            ab_tensor(pe)
            with pe.Fori(0, NH) as h:
                head_tensor(pe, h)
            for g in range(3):
                with pe.Fori(0, 2) as i:
                    att_tensor(pe, g, i)
            end_tensor(pe)


def kernel(**inputs):
    import concourse.bacc as bacc
    from concourse.bass_utils import run_bass_kernel_spmd

    tables = constants()
    arrays = {f"in_{n}": np.ascontiguousarray(inputs[n]) for n in INPUTS}
    arrays |= {f"table_{n}": x for n, x in tables.items()}
    lengths = {}
    for _ in range(2):
        nc = bacc.Bacc("TRN2", target_bir_lowering=False, num_devices=1)
        a = {}
        for n in INPUTS:
            a[n] = nc.dram_tensor(f"in_{n}", arrays[f"in_{n}"].shape, F32, kind="ExternalInput").ap()
        for n, x in tables.items():
            a[n] = nc.dram_tensor(f"table_{n}", x.shape, F32, kind="ExternalInput").ap()
        for n, shape in OUTS:
            a[n] = nc.dram_tensor(f"out_{n}", shape, F32, kind="ExternalOutput").ap()
        build(nc, a, lengths)
    r = run_bass_kernel_spmd(nc, [arrays], core_ids=[0])
    return tuple(r.results[0][f"out_{n}"] for n, _ in OUTS)
```
